# Optimizing a Trainium2 kernel written in Bass

```python
import math
import jax, jax.numpy as jnp
from jax import lax
import numpy as np

D_MODEL = 2048
BATCH = 1
SEQ = 256
DEPTH = 1

D_SSM = D_MODEL // 2
D_ATTN = D_MODEL // 2
D_MIX = D_SSM + D_ATTN
SSM_GROUP = 16
N_SSM_GROUPS = D_SSM // SSM_GROUP
SSM_STATE = 64
DT_MIN = 1e-3
DT_MAX = 1e-1

HEAD_DIM = 128
N_HEADS = D_ATTN // HEAD_DIM
N_KV = 2
HPG = N_HEADS // N_KV
CMP_LEN = 32
CMP_STRIDE = 16
CMP_HIDDEN = 256
SLC_LEN = 64
SLC_TOPK = 16
WINDOW = 512
Q_BLOCK = 128
N_BRANCH = 3

N_BUCKETS = 32
MAX_DISTANCE = 1024

PEER_HEADS = 8
PEER_NKEYS = 128
PEER_EXPERTS = PEER_NKEYS * PEER_NKEYS
PEER_DKEY = 256
PEER_TOPK = 16
PEER_CHUNK = 128

KV_COLS = N_BRANCH * 2 * N_KV * HEAD_DIM
GATE_COLS = N_BRANCH * N_HEADS
D_IN = D_SSM + D_ATTN + KV_COLS + GATE_COLS
N_ADA = 6
EPS = 1e-6
NEG = -1e30
FORCED = 1e6


def rmsnorm(x, g):
    xf = x.astype(jnp.float32)
    return xf * lax.rsqrt(jnp.mean(xf * xf, axis=-1, keepdims=True) + EPS) * g

def t5_bucket(dist):
    n = jnp.maximum(dist, 0)
    max_exact = N_BUCKETS // 2
    scaled = jnp.log(jnp.maximum(n, max_exact).astype(jnp.float32) / max_exact) / math.log(MAX_DISTANCE / max_exact)
    large = max_exact + (scaled * (N_BUCKETS - max_exact)).astype(jnp.int32)
    return jnp.where(n < max_exact, n, jnp.minimum(large, N_BUCKETS - 1))

def s5_mixer(u, lam_re, lam_im, log_dt, b_re, b_im, c_re, c_im, d_skip, w_glu, b_glu):
    B, L, _ = u.shape
    f32 = jnp.float32
    uf = u.astype(f32).reshape(B, L, N_SSM_GROUPS, SSM_GROUP)
    dt = jnp.exp(log_dt.astype(f32))[:, None]
    lr = lam_re.astype(f32)
    li = lam_im.astype(f32)
    mag = jnp.exp(lr * dt)
    ab_re = mag * jnp.cos(li * dt)
    ab_im = mag * jnp.sin(li * dt)
    den = lr * lr + li * li
    nr = ab_re - 1.0
    ni = ab_im
    w_re = (nr * lr + ni * li) / den
    w_im = (ni * lr - nr * li) / den
    br = b_re.astype(f32)
    bi = b_im.astype(f32)
    bb_re = w_re[..., None] * br - w_im[..., None] * bi
    bb_im = w_re[..., None] * bi + w_im[..., None] * br
    xr = jnp.einsum('gph,blgh->blgp', bb_re, uf)
    xi = jnp.einsum('gph,blgh->blgp', bb_im, uf)
    ar = jnp.broadcast_to(ab_re, xr.shape)
    ai = jnp.broadcast_to(ab_im, xi.shape)

    def combine(e1, e2):
        a1r, a1i, b1r, b1i = e1
        a2r, a2i, b2r, b2i = e2
        return (a1r * a2r - a1i * a2i, a1r * a2i + a1i * a2r,
                a2r * b1r - a2i * b1i + b2r, a2r * b1i + a2i * b1r + b2i)

    _, _, sr, si = lax.associative_scan(combine, (ar, ai, xr, xi), axis=1)
    y = (jnp.einsum('ghp,blgp->blgh', c_re.astype(f32), sr)
         - jnp.einsum('ghp,blgp->blgh', c_im.astype(f32), si)
         + d_skip.astype(f32) * uf)
    z = jax.nn.gelu(y.reshape(B, L, D_SSM))
    return z * jax.nn.sigmoid(z @ w_glu + b_glu)

def compress(kv, pe, w1, w2):
    B, L, G, dh = kv.shape
    ch = kv.reshape(B, L // CMP_STRIDE, CMP_STRIDE, G, dh)
    blocks = jnp.concatenate([ch[:, :-1], ch[:, 1:]], axis=2)
    blocks = blocks + pe[None, None, :, None, :]
    n_cmp = blocks.shape[1]
    flat = blocks.transpose(0, 1, 3, 2, 4).reshape(B, n_cmp, G, CMP_LEN * dh)
    return jax.nn.gelu(flat @ w1) @ w2

def nsa_attention(q, k_cmp, v_cmp, k_slc, v_slc, k_win, v_win, gates, rel_bias,
                  pe_k, w1_k, w2_k, pe_v, w1_v, w2_v):
    B, L = q.shape[:2]
    f32 = jnp.float32
    scale = HEAD_DIM ** -0.5
    kc = compress(k_cmp, pe_k, w1_k, w2_k)
    vc = compress(v_cmp, pe_v, w1_v, w2_v)
    n_cmp = kc.shape[1]
    n_slc = L // SLC_LEN
    topk = min(SLC_TOPK, n_slc)
    cmp_start = jnp.arange(n_cmp) * CMP_STRIDE
    cmp_end = cmp_start + CMP_LEN - 1
    slc_start = jnp.arange(n_slc) * SLC_LEN
    ov = (jnp.minimum(cmp_start[:, None] + CMP_LEN, slc_start[None, :] + SLC_LEN)
          - jnp.maximum(cmp_start[:, None], slc_start[None, :]))
    overlap = jnp.maximum(ov, 0).astype(f32) / CMP_STRIDE
    ks_blk = k_slc.reshape(B, n_slc, SLC_LEN, N_KV, HEAD_DIM).transpose(0, 3, 1, 2, 4)
    vs_blk = v_slc.reshape(B, n_slc, SLC_LEN, N_KV, HEAD_DIM).transpose(0, 3, 1, 2, 4)
    pad = ((0, 0), (WINDOW, 0), (0, 0), (0, 0))
    kw = jnp.pad(k_win, pad)
    vw = jnp.pad(v_win, pad)
    n_qb = L // Q_BLOCK
    qb = q.reshape(B, n_qb, Q_BLOCK, N_KV, HPG, HEAD_DIM).transpose(1, 0, 2, 3, 4, 5)
    gb = gates.reshape(B, n_qb, Q_BLOCK, N_BRANCH, N_KV, HPG).transpose(1, 0, 2, 3, 4, 5)
    bias_g = rel_bias.reshape(N_BUCKETS, N_KV, HPG)
    bidx = jnp.arange(B)[:, None, None, None]
    gidx = jnp.arange(N_KV)[None, None, :, None]
    gidx5 = jnp.arange(N_KV)[None, None, :, None, None]
    jblk = jnp.arange(n_slc)

    def block_fn(args):
        qi, gi, bi = args
        t = bi * Q_BLOCK + jnp.arange(Q_BLOCK)
        lc = jnp.einsum('bqgpd,bngd->bgpqn', qi, kc).astype(f32) * scale
        dist_c = t[:, None] - cmp_end[None, :]
        valid_c = dist_c >= 0
        lc = lc + bias_g[t5_bucket(dist_c)].transpose(2, 3, 0, 1)[None]
        lc = jnp.where(valid_c, lc, NEG)
        pc = jax.nn.softmax(lc, axis=-1) * valid_c
        oc = jnp.einsum('bgpqn,bngd->bqgpd', pc.astype(vc.dtype), vc)
        imp = jnp.einsum('bgqn,nj->bgqj', pc.sum(axis=2), overlap)
        qblk = t // SLC_LEN
        forced = ((jblk[None, :] == 0) | (jblk[None, :] == qblk[:, None])
                  | (jblk[None, :] == qblk[:, None] - 1))
        causal_s = slc_start[None, :] <= t[:, None]
        score = jnp.where(causal_s, jnp.where(forced, FORCED, imp), NEG)
        sel_val, sel_idx = lax.top_k(score, topk)
        idx = sel_idx.transpose(0, 2, 1, 3)
        ok = (sel_val > NEG * 0.5).transpose(0, 2, 1, 3)
        ks = ks_blk[bidx, gidx, idx]
        vs = vs_blk[bidx, gidx, idx]
        pos = idx[..., None] * SLC_LEN + jnp.arange(SLC_LEN)
        dist_s = t[None, :, None, None, None] - pos
        valid_s = ok[..., None] & (dist_s >= 0)
        ls = jnp.einsum('bqgpd,bqgskd->bqgskp', qi, ks).astype(f32) * scale
        ls = ls + bias_g[t5_bucket(dist_s), gidx5]
        ls = jnp.where(valid_s[..., None], ls, NEG)
        ps = jax.nn.softmax(ls, axis=(3, 4))
        osl = jnp.einsum('bqgskp,bqgskd->bqgpd', ps.astype(vs.dtype), vs)
        q0 = bi * Q_BLOCK
        kwin = lax.dynamic_slice_in_dim(kw, q0, WINDOW + Q_BLOCK, axis=1)
        vwin = lax.dynamic_slice_in_dim(vw, q0, WINDOW + Q_BLOCK, axis=1)
        spos = q0 - WINDOW + jnp.arange(WINDOW + Q_BLOCK)
        dist_w = t[:, None] - spos[None, :]
        valid_w = (dist_w >= 0) & (dist_w < WINDOW) & (spos[None, :] >= 0)
        lw = jnp.einsum('bqgpd,bkgd->bgpqk', qi, kwin).astype(f32) * scale
        lw = lw + bias_g[t5_bucket(dist_w)].transpose(2, 3, 0, 1)[None]
        lw = jnp.where(valid_w, lw, NEG)
        pw = jax.nn.softmax(lw, axis=-1)
        ow = jnp.einsum('bgpqk,bkgd->bqgpd', pw.astype(vwin.dtype), vwin)
        return (gi[:, :, 0, :, :, None] * oc + gi[:, :, 1, :, :, None] * osl
                + gi[:, :, 2, :, :, None] * ow)

    out = lax.map(block_fn, (qb, gb, jnp.arange(n_qb)))
    return out.transpose(1, 0, 2, 3, 4, 5).reshape(B, L, D_ATTN)

def peer(h, w_q, sub_k1, sub_k2, exp_u, exp_v):
    B, L, D = h.shape
    T = B * L
    hf = h.reshape(T, D)
    q = (hf @ w_q).reshape(T, PEER_HEADS, 2, PEER_DKEY // 2)
    s1 = jnp.einsum('thd,nd->thn', q[:, :, 0], sub_k1).astype(jnp.float32)
    s2 = jnp.einsum('thd,nd->thn', q[:, :, 1], sub_k2).astype(jnp.float32)
    v1, i1 = lax.top_k(s1, PEER_TOPK)
    v2, i2 = lax.top_k(s2, PEER_TOPK)
    cand = (v1[..., :, None] + v2[..., None, :]).reshape(T, PEER_HEADS, PEER_TOPK * PEER_TOPK)
    sv, si = lax.top_k(cand, PEER_TOPK)
    e1 = jnp.take_along_axis(i1, si // PEER_TOPK, axis=-1)
    e2 = jnp.take_along_axis(i2, si % PEER_TOPK, axis=-1)
    expert = e1 * PEER_NKEYS + e2
    gate = jax.nn.softmax(sv, axis=-1)
    n_chunks = T // PEER_CHUNK

    def chunk_fn(args):
        xc, ec, gc = args
        u = exp_u[ec]
        a = jax.nn.gelu(jnp.einsum('cd,chkd->chk', xc, u).astype(jnp.float32))
        w = (gc * a).astype(exp_v.dtype)
        return jnp.einsum('chk,chkd->cd', w, exp_v[ec])

    out = lax.map(chunk_fn, (hf.reshape(n_chunks, PEER_CHUNK, D),
                             expert.reshape(n_chunks, PEER_CHUNK, PEER_HEADS, PEER_TOPK),
                             gate.reshape(n_chunks, PEER_CHUNK, PEER_HEADS, PEER_TOPK)))
    return out.reshape(B, L, D)

def first_inputs(seed: int = 0) -> dict:
    key = jax.random.key(seed)
    ks = jax.random.split(key, 33)
    f32 = jnp.float32
    D = D_MODEL
    G, P, H = N_SSM_GROUPS, SSM_STATE, SSM_GROUP

    def nrm(k, shape, s):
        return jax.random.normal(k, shape, f32) * s

    lam_im_base = jnp.pi * jnp.arange(P, dtype=f32)
    return {
        'x': nrm(ks[0], (BATCH, SEQ, D), 1.0),
        'c': nrm(ks[1], (BATCH, D), 1.0),
        'w_ada': nrm(ks[2], (DEPTH, D, N_ADA * D), 0.5 * D ** -0.5),
        'b_ada': nrm(ks[3], (DEPTH, N_ADA * D), 0.02),
        'norm1_g': 1.0 + nrm(ks[4], (DEPTH, D), 0.02),
        'norm2_g': 1.0 + nrm(ks[5], (DEPTH, D), 0.02),
        'w_in': nrm(ks[6], (DEPTH, D, D_IN), D ** -0.5),
        'w_out': nrm(ks[7], (DEPTH, D_MIX, D), D_MIX ** -0.5),
        'beta_ssm': 1.0 + nrm(ks[8], (DEPTH, D_SSM), 0.02),
        'beta_attn': 1.0 + nrm(ks[9], (DEPTH, D_ATTN), 0.02),
        'ssm_lam_re': -0.5 + nrm(ks[10], (DEPTH, G, P), 0.01),
        'ssm_lam_im': lam_im_base + nrm(ks[11], (DEPTH, G, P), 0.01),
        'ssm_log_dt': jax.random.uniform(ks[12], (DEPTH, G), f32, math.log(DT_MIN), math.log(DT_MAX)),
        'ssm_b_re': nrm(ks[13], (DEPTH, G, P, H), (2 * H) ** -0.5),
        'ssm_b_im': nrm(ks[14], (DEPTH, G, P, H), (2 * H) ** -0.5),
        'ssm_c_re': nrm(ks[15], (DEPTH, G, H, P), (2 * P) ** -0.5 * 4.0),
        'ssm_c_im': nrm(ks[16], (DEPTH, G, H, P), (2 * P) ** -0.5 * 4.0),
        'ssm_d': nrm(ks[17], (DEPTH, G, H), 1.0),
        'ssm_w_glu': nrm(ks[18], (DEPTH, D_SSM, D_SSM), D_SSM ** -0.5),
        'ssm_b_glu': nrm(ks[19], (DEPTH, D_SSM), 0.02),
        'cmp_pe_k': nrm(ks[20], (DEPTH, CMP_LEN, HEAD_DIM), 0.02),
        'cmp_w1_k': nrm(ks[21], (DEPTH, CMP_LEN * HEAD_DIM, CMP_HIDDEN), (CMP_LEN * HEAD_DIM) ** -0.5),
        'cmp_w2_k': nrm(ks[22], (DEPTH, CMP_HIDDEN, HEAD_DIM), CMP_HIDDEN ** -0.5 * 2.0),
        'cmp_pe_v': nrm(ks[23], (DEPTH, CMP_LEN, HEAD_DIM), 0.02),
        'cmp_w1_v': nrm(ks[24], (DEPTH, CMP_LEN * HEAD_DIM, CMP_HIDDEN), (CMP_LEN * HEAD_DIM) ** -0.5),
        'cmp_w2_v': nrm(ks[25], (DEPTH, CMP_HIDDEN, HEAD_DIM), CMP_HIDDEN ** -0.5 * 2.0),
        'rel_bias': nrm(ks[26], (N_BUCKETS, N_HEADS), 0.1),
        'peer_w_q': nrm(ks[27], (DEPTH, D, PEER_HEADS * PEER_DKEY), D ** -0.5),
        'peer_k1': nrm(ks[28], (DEPTH, PEER_NKEYS, PEER_DKEY // 2), (PEER_DKEY // 2) ** -0.5),
        'peer_k2': nrm(ks[29], (DEPTH, PEER_NKEYS, PEER_DKEY // 2), (PEER_DKEY // 2) ** -0.5),
        'peer_u': nrm(ks[30], (DEPTH, PEER_EXPERTS, D), D ** -0.5),
        'peer_v': nrm(ks[31], (DEPTH, PEER_EXPERTS, D), PEER_HEADS ** -0.5),
        'final_g': 1.0 + nrm(ks[32], (D,), 0.02),
    }

def first_block(x, c, w_ada, b_ada, norm1_g, norm2_g, w_in, w_out, beta_ssm, beta_attn,
              ssm_lam_re, ssm_lam_im, ssm_log_dt, ssm_b_re, ssm_b_im, ssm_c_re, ssm_c_im,
              ssm_d, ssm_w_glu, ssm_b_glu, cmp_pe_k, cmp_w1_k, cmp_w2_k, cmp_pe_v, cmp_w1_v,
              cmp_w2_v, rel_bias, peer_w_q, peer_k1, peer_k2, peer_u, peer_v, final_g):
    B, L, _ = x.shape
    for l in range(DEPTH):
        cond = jax.nn.silu(c) @ w_ada[l] + b_ada[l]
        sh1, sc1, g1, sh2, sc2, g2 = [m[:, None, :] for m in jnp.split(cond, N_ADA, axis=-1)]
        h = rmsnorm(x, norm1_g[l]) * (1.0 + sc1) + sh1
        proj = h @ w_in[l]
        u_ssm, q, kv, gate_logits = jnp.split(
            proj, [D_SSM, D_SSM + D_ATTN, D_SSM + D_ATTN + KV_COLS], axis=-1)
        q = q.reshape(B, L, N_HEADS, HEAD_DIM)
        kv = kv.reshape(B, L, N_BRANCH, 2, N_KV, HEAD_DIM)
        gates = jax.nn.sigmoid(gate_logits.reshape(B, L, N_BRANCH, N_HEADS))
        y_ssm = s5_mixer(u_ssm, ssm_lam_re[l], ssm_lam_im[l], ssm_log_dt[l], ssm_b_re[l], ssm_b_im[l],
                         ssm_c_re[l], ssm_c_im[l], ssm_d[l], ssm_w_glu[l], ssm_b_glu[l])
        y_att = nsa_attention(q, kv[:, :, 0, 0], kv[:, :, 0, 1], kv[:, :, 1, 0], kv[:, :, 1, 1],
                              kv[:, :, 2, 0], kv[:, :, 2, 1], gates, rel_bias,
                              cmp_pe_k[l], cmp_w1_k[l], cmp_w2_k[l], cmp_pe_v[l], cmp_w1_v[l], cmp_w2_v[l])
        mixed = jnp.concatenate([rmsnorm(y_ssm, beta_ssm[l]), rmsnorm(y_att, beta_attn[l])], axis=-1)
        x = x + g1 * (mixed @ w_out[l])
        h2 = rmsnorm(x, norm2_g[l]) * (1.0 + sc2) + sh2
        x = x + g2 * peer(h2, peer_w_q[l], peer_k1[l], peer_k2[l], peer_u[l], peer_v[l])
    return rmsnorm(x, final_g)


_first_inputs = first_inputs


def first_inputs(seed=0):
    import zlib

    import numpy as np

    out = dict(_first_inputs(seed))
    spreads = {}
    factors = {'norm1_g': 6.82,
     'norm2_g': 34.907,
     'beta_ssm': 87.121,
     'beta_attn': 83.139,
     'ssm_lam_re': 200.0,
     'ssm_b_glu': 8.0,
     'cmp_pe_k': 8.0,
     'cmp_pe_v': 26.35,
     'rel_bias': 5.38,
     'final_g': 20.865}
    for name, (base, spread) in spreads.items():
        noise = np.random.default_rng([zlib.crc32(name.encode()), seed]).standard_normal(out[name].shape)
        drawn = base * np.exp(spread * noise) if base else spread * noise
        out[name] = __import__('jax').numpy.asarray(drawn.astype(out[name].dtype))
    for name, factor in factors.items():
        out[name] = (out[name] * factor).astype(out[name].dtype)
    return out


_narrow_inputs = first_inputs


def first_inputs(seed=0):
    out = dict(_narrow_inputs(seed))
    wider = {'ssm_lam_re': 12.0, 'ssm_lam_im': 3.49, 'ssm_log_dt': 3.42, 'final_g': 3.1}
    for name, times in wider.items():
        mean = out[name].mean()
        out[name] = (mean + times * (out[name] - mean)).astype(out[name].dtype)
    return out


CHUNK = 64

D_A = 768
K_A = 31
POOL_WINDOWS = (2, 4, 8, 16)
N_POOL_GROUPS = 4
POOL_GROUP = 128
D_B = N_POOL_GROUPS * POOL_GROUP
D_C = 768
K_C = 3
D_IN_2 = 2 * D_A + D_B + 3 * D_C
D_FF = 4 * D_MODEL


def rmsnorm_2(x, g):
    xf = x.astype(jnp.float32)
    y = xf * lax.rsqrt(jnp.mean(xf * xf, axis=-1, keepdims=True) + EPS)
    return (y * g.astype(jnp.float32)).astype(x.dtype)

def layernorm(x, g, b):
    xf = x.astype(jnp.float32)
    mu = jnp.mean(xf, axis=-1, keepdims=True)
    xc = xf - mu
    var = jnp.mean(xc * xc, axis=-1, keepdims=True)
    y = xc * lax.rsqrt(var + EPS) * g.astype(jnp.float32) + b.astype(jnp.float32)
    return y.astype(x.dtype)

def causal_dwconv(u, w):
    k, c = w.shape
    return lax.conv_general_dilated(
        u, w[:, None, :].astype(u.dtype), window_strides=(1,), padding=[(k - 1, 0)],
        dimension_numbers=("NWC", "WIO", "NWC"), feature_group_count=c)

def multiscale_pool(u, w_grp, scale):
    b, s, _ = u.shape
    ug = u.reshape(b, s, N_POOL_GROUPS, POOL_GROUP).astype(jnp.float32)
    cs = jnp.cumsum(ug, axis=1)
    pos = jnp.arange(1, s + 1, dtype=jnp.float32)
    means = []
    for gi, w in enumerate(POOL_WINDOWS):
        c = cs[:, :, gi]
        lag = jnp.pad(c, ((0, 0), (w, 0), (0, 0)))[:, :s]
        cnt = jnp.minimum(pos, float(w))[None, :, None]
        means.append((c - lag) / cnt)
    pooled = (jnp.stack(means, axis=2) - ug).astype(u.dtype)
    mixed = jnp.einsum("bsgc,gcd->bsgd", pooled, w_grp)
    return mixed.reshape(b, s, D_B) * scale

def second_inputs(seed: int = 0) -> dict:
    key = jax.random.key(seed)
    ks = jax.random.split(key, 24)
    f32 = jnp.float32
    nrm = lambda k, shape, scale: jax.random.normal(k, shape, f32) * scale
    L, D = DEPTH, D_MODEL
    return {
        "x": jax.random.normal(ks[0], (BATCH, SEQ, D), f32),
        "g_mix": 1.0 + nrm(ks[1], (L, D), 0.02),
        "w_in": nrm(ks[2], (L, D, D_IN_2), D ** -0.5),
        "w_gate": nrm(ks[3], (L, D, N_BRANCH * D), D ** -0.5),
        "b_gate": nrm(ks[4], (L, N_BRANCH * D), 0.01),
        "b_glu": nrm(ks[5], (L, 2 * D_A), 0.01),
        "w_dw_a": nrm(ks[6], (L, K_A, D_A), K_A ** -0.5),
        "b_dw_a": nrm(ks[7], (L, D_A), 0.01),
        "ln_g_a": 1.0 + nrm(ks[8], (L, D_A), 0.02),
        "ln_b_a": nrm(ks[9], (L, D_A), 0.01),
        "w_a_out": nrm(ks[10], (L, D_A, D), D_A ** -0.5),
        "w_pool_grp": nrm(ks[11], (L, N_POOL_GROUPS, POOL_GROUP, POOL_GROUP), POOL_GROUP ** -0.5),
        "pool_scale": 1.0 + nrm(ks[12], (L, D_B), 0.02),
        "w_b_out": nrm(ks[13], (L, D_B, D), D_B ** -0.5),
        "w_dw_c": nrm(ks[14], (L, K_C, D_C), K_C ** -0.5),
        "w_c_out": nrm(ks[15], (L, D_C, D), D_C ** -0.5),
        "w_o": nrm(ks[16], (L, D, D), D ** -0.5),
        "g_mlp": 1.0 + nrm(ks[17], (L, D), 0.02),
        "w_up": nrm(ks[18], (L, D, D_FF), D ** -0.5),
        "w_down": nrm(ks[19], (L, D_FF, D), 0.5 * D_FF ** -0.5),
        "g_final": 1.0 + nrm(ks[20], (D,), 0.02),
    }

def second_block(x, g_mix, w_in, w_gate, b_gate, b_glu, w_dw_a, b_dw_a, ln_g_a, ln_b_a, w_a_out,
              w_pool_grp, pool_scale, w_b_out, w_dw_c, w_c_out, w_o, g_mlp, w_up, w_down, g_final):
    b, s, d = x.shape
    for l in range(DEPTH):
        h = rmsnorm_2(x, g_mix[l])
        z = h @ w_in[l]
        za = z[..., : 2 * D_A] + b_glu[l]
        zb = z[..., 2 * D_A: 2 * D_A + D_B]
        zc = z[..., 2 * D_A + D_B:]

        ua = za[..., :D_A] * jax.nn.sigmoid(za[..., D_A:])
        va = causal_dwconv(ua, w_dw_a[l]) + b_dw_a[l]
        va = jax.nn.silu(layernorm(va, ln_g_a[l], ln_b_a[l]))
        ya = va @ w_a_out[l]

        yb = multiscale_pool(zb, w_pool_grp[l], pool_scale[l]) @ w_b_out[l]

        gb, gc, xv = zc[..., :D_C], zc[..., D_C: 2 * D_C], zc[..., 2 * D_C:]
        yc = (gb * causal_dwconv(gc * xv, w_dw_c[l])) @ w_c_out[l]

        gates = jax.nn.sigmoid(h @ w_gate[l] + b_gate[l]).reshape(b, s, N_BRANCH, d)
        merged = gates[:, :, 0] * ya + gates[:, :, 1] * yb + gates[:, :, 2] * yc
        x = x + merged @ w_o[l]

        h2 = rmsnorm_2(x, g_mlp[l])
        x = x + jnp.square(jax.nn.relu(h2 @ w_up[l])) @ w_down[l]
    return rmsnorm_2(x, g_final)


_first_inputs_2 = second_inputs


def second_inputs(seed=0):
    import zlib

    import numpy as np

    out = dict(_first_inputs_2(seed))
    spreads = {}
    factors = {'g_mix': 2.92,
     'b_gate': 22.136,
     'b_glu': 64.0,
     'b_dw_a': 40.641,
     'ln_g_a': 64.0,
     'ln_b_a': 64.0,
     'pool_scale': 33.347,
     'g_mlp': 19.592,
     'g_final': 8.278}
    for name, (base, spread) in spreads.items():
        noise = np.random.default_rng([zlib.crc32(name.encode()), seed]).standard_normal(out[name].shape)
        drawn = base * np.exp(spread * noise) if base else spread * noise
        out[name] = __import__('jax').numpy.asarray(drawn.astype(out[name].dtype))
    for name, factor in factors.items():
        out[name] = (out[name] * factor).astype(out[name].dtype)
    return out


_narrow_inputs_2 = second_inputs


def second_inputs(seed=0):

    out = dict(_narrow_inputs_2(seed))
    wider = {'ln_g_a': 6.17, 'ln_b_a': 12.0, 'pool_scale': 3.31, 'g_final': 3.24}
    for name, times in wider.items():
        mean = out[name].mean()
        out[name] = (mean + times * (out[name] - mean)).astype(out[name].dtype)
    return out


def setup_inputs(seed=0):
    out = dict(first_inputs(seed))
    for name, value in second_inputs(seed + 1).items():
        if name != "x":
            out[name + "_2"] = value
    return out


def reference(
    x, c, w_ada, b_ada, norm1_g, norm2_g, w_in, w_out, beta_ssm, beta_attn, ssm_lam_re,
    ssm_lam_im, ssm_log_dt, ssm_b_re, ssm_b_im, ssm_c_re, ssm_c_im, ssm_d, ssm_w_glu, ssm_b_glu,
    cmp_pe_k, cmp_w1_k, cmp_w2_k, cmp_pe_v, cmp_w1_v, cmp_w2_v, rel_bias, peer_w_q, peer_k1,
    peer_k2, peer_u, peer_v, final_g, g_mix_2, w_in_2, w_gate_2, b_gate_2, b_glu_2, w_dw_a_2,
    b_dw_a_2, ln_g_a_2, ln_b_a_2, w_a_out_2, w_pool_grp_2, pool_scale_2, w_b_out_2, w_dw_c_2,
    w_c_out_2, w_o_2, g_mlp_2, w_up_2, w_down_2, g_final_2,
):
    x = first_block(
        x, c, w_ada, b_ada, norm1_g, norm2_g, w_in, w_out, beta_ssm, beta_attn, ssm_lam_re,
        ssm_lam_im, ssm_log_dt, ssm_b_re, ssm_b_im, ssm_c_re, ssm_c_im, ssm_d, ssm_w_glu,
        ssm_b_glu, cmp_pe_k, cmp_w1_k, cmp_w2_k, cmp_pe_v, cmp_w1_v, cmp_w2_v, rel_bias,
        peer_w_q, peer_k1, peer_k2, peer_u, peer_v, final_g,
    )
    return second_block(
        x, g_mix_2, w_in_2, w_gate_2, b_gate_2, b_glu_2, w_dw_a_2, b_dw_a_2, ln_g_a_2, ln_b_a_2,
        w_a_out_2, w_pool_grp_2, pool_scale_2, w_b_out_2, w_dw_c_2, w_c_out_2, w_o_2, g_mlp_2,
        w_up_2, w_down_2, g_final_2,
    )


_drawn_inputs = setup_inputs


def setup_inputs(seed=0):
    import zlib

    import numpy as np

    out = dict(_drawn_inputs(seed))
    spreads = {}
    factors = {}
    for name, (base, spread) in spreads.items():
        noise = np.random.default_rng([zlib.crc32(name.encode()), seed]).standard_normal(out[name].shape)
        drawn = base * np.exp(spread * noise) if base else spread * noise
        out[name] = __import__('jax').numpy.asarray(drawn.astype(out[name].dtype))
    for name, factor in factors.items():
        out[name] = (out[name] * factor).astype(out[name].dtype)
    return out
```

```python
from contextlib import ExitStack, contextmanager
import math

import numpy as np

import concourse.bass as bass
from concourse import mybir

F32 = mybir.dt.float32
U32 = mybir.dt.uint32
ALU = mybir.AluOpType
ACT = mybir.ActivationFunctionType
AX_X = mybir.AxisListType.X

P = 128
T = 256
D = 2048
KT = D // P
UNIT = 4096
RING = 4
NSTATE_T = 32
N_CMP = 15
HEADS = 8
NEG = -1e30
EPS = 1e-6
SCALE = 128 ** -0.5
EXP_T = 64
TOPK = 16

STREAM = [("ada", 48), ("w_in", 14), ("cmp", 4), ("glu", 2), ("w_out", 8), ("peer_q", 8),
          ("u0", 32), ("v0", 32), ("u1", 32), ("v1", 32),
          ("z", 17), ("gate", 24), ("abc", 8), ("w_o", 8), ("up", 32), ("down", 32)]
FIRST = {}
N_UNITS = 0
for _name, _n in STREAM:
    FIRST[_name] = N_UNITS
    N_UNITS += _n

CONST = [("c", 16), ("b_ada", 96), ("norm1_g", 16), ("norm2_g", 16), ("final_g", 16), ("g_mix", 16),
         ("g_mlp", 16), ("g_final", 16), ("beta", 16), ("lam_re", 32), ("lam_im", 32), ("log_dt", 32),
         ("d_skip", 8), ("b_glu", 8), ("b_gate", 48), ("b_glu2", 12), ("w_dw_a", 186), ("b_dw_a", 6),
         ("ln_g", 6), ("ln_b", 6), ("pool_scale", 4), ("w_dw_c", 18), ("pool_rcnt", 64)]
COL = {}
N_CONST = 0
for _name, _n in CONST:
    COL[_name] = N_CONST
    N_CONST += _n

SKEW_W = 384
ASC_0 = 255
ASC_W = 480

STATS = [16, 8, 8, 16, 16, 16, 6, 16, 16]
CHUNK = 4


def chunks_of(n):
    return [(a, min(CHUNK, n - a)) for a in range(0, n, CHUNK)]


STAT_CHUNK0 = [sum(len(chunks_of(m)) for m in STATS[:q]) for q in range(len(STATS))]


def early_schedule():
    slots = [("unit", v) for v in range(4, 14)] + [("gates", 0)] + [("cmp", v) for v in range(4)]
    out, x, y = [], 0, 0
    for s in slots:
        out.append(s)
        for _ in range(2):
            out.append(("x", x))
            x += 1
            if x - y > 3:
                out.append(("y", y))
                y += 1
    while y < NSTATE_T:
        if x < NSTATE_T:
            out.append(("x", x))
            x += 1
        out.append(("y", y))
        y += 1
    return out


class Chain:

    def __init__(self, eng, sem):
        self.eng, self.sem, self.n, self.i, self.per = eng, sem, 0, None, 0

    def put(self, ins):
        ins.then_inc(self.sem, 1)
        self.n += 1
        return self.value()

    def value(self):
        return self.n if self.i is None else self.i * self.per + self.n

    def wait(self, back=0):
        self.eng.wait_ge(self.sem, self.value() - back)

    @contextmanager
    def loop(self, times, per):
        with self.eng.Fori(0, times) as i:
            n0, self.i, self.per = self.n, i, per
            yield i
            assert self.n - n0 == per, (self.n - n0, per)
        self.i = None
        self.n = n0 + per * times


def program(nc, xT_d, wst, cst_d, dyn1_d, dyn2_d, dyn3_d, onehot_d, bmat_d, cmat_d, skew_d, out_d):
    ctx = ExitStack()
    with ctx:
        def sb(name, cols, dt=F32):
            return ctx.enter_context(nc.sbuf_tensor(name, [P, cols], dt))

        def sem(name):
            return ctx.enter_context(nc.semaphore(name))

        ring = sb("ring", RING * UNIT)
        A = sb("arena", 64 * T)
        X = sb("x_res", KT * T)
        H = sb("h_act", KT * T)
        J = sb("proj", 28 * T)
        W = sb("work", 8 * T)
        cst = sb("cst", N_CONST)
        dyn = sb("dyn", 960)
        mod = sb("mod", 96)
        csilu = sb("csilu", KT)
        affine = sb("affine", KT)
        rs = sb("rs", T)
        mag = sb("mag", NSTATE_T)
        small = sb("small", 64)
        ident = sb("ident", P)
        ones = sb("ones", P)
        psW = ctx.enter_context(nc.psum_tensor("psW", [P, 4, 512], F32))
        psM = ctx.enter_context(nc.psum_tensor("psM", [P, 4, 512], F32))

        def const(name, a=0, n=1):
            return cst[:, COL[name] + a:COL[name] + a + n]

        def tiles(buf, a, n=1):
            return buf[:, a * T:(a + n) * T]

        tab = A[:, :].rearrange("p (i r t) -> p i r t", i=NSTATE_T, r=2)
        cmat = X[:, 0:2048].rearrange("p (r i c) -> p r i c", r=2, i=NSTATE_T)
        scanb = X[:, 2048:3072].rearrange("p (b r t) -> p b r t", b=2, r=2)
        bmat = X[:, 3072:4096].rearrange("p (s r n) -> p s r n", s=4, r=2)
        onehot = J[0:33, 0:SKEW_W + ASC_W + HEADS]
        skew_sb = J[:, 1024:1024 + HEADS * SKEW_W]
        blk = H[:, 0:1920].rearrange("p (v o n) -> p v o n", v=2, o=32)
        cmp_hid = H[:, 1920:2040].rearrange("p (v m n) -> p v m n", v=2, m=2)
        bias = H[:, 2048:4096].rearrange("p (h s) -> p h s", h=HEADS)
        gate_w = dyn[:, 0:384].rearrange("p (k n) -> p k n", k=KT)
        kc = dyn[:, 0:30]
        vc = dyn[0:N_CMP, 32:32 + 256].rearrange("p (g d) -> p g d", g=2)
        w2 = dyn[:, 384:896].rearrange("p (v m d) -> p v m d", v=2, m=2)
        pe = dyn[:, 896:960].rearrange("p (v o) -> p v o", v=2)
        keys = dyn[:, 0:256].rearrange("p (f n) -> p f n", f=2)
        pool_w = dyn[:, 0:512].rearrange("p (g n) -> p g n", g=4)
        vnat = A[:, 0:1024].rearrange("p (b g s d) -> p b g s d", b=2, g=2, s=2)
        LW = 528
        logit = [A[:, 1024 + LW * i:1024 + LW * (i + 1)] for i in range(3)]
        probT = [A[:, 2816 + 640 * i:2816 + 640 * (i + 1)] for i in range(2)]
        glu_s = A[:, 8192:8192 + 8 * T]
        mxb = small[:, 0:9].rearrange("p (b c) -> p b c", b=3)
        smb = small[:, 9:18].rearrange("p (b c) -> p b c", b=3)
        gates = sb("gates", 48)[:, :].rearrange("p (q h c) -> p q h c", q=2, h=HEADS)
        cvalid = sb("cvalid", 30)[:, :].rearrange("p (q n) -> p q n", q=2)
        cbias = sb("cbias", 240)[:, :].rearrange("p (q n h) -> p q n h", q=2, n=N_CMP)
        cand = J[:, 0:2048].rearrange("p (h a b) -> p h a b", h=HEADS, a=TOPK)
        sel = J[:, 2048:4096]
        val = sel[:, 0:256].rearrange("p (h f k) -> p h f k", h=HEADS, f=2)
        idx = sel[:, 256:512].bitcast(U32).rearrange("p (h f k) -> p h f k", h=HEADS, f=2)
        idxf = sel[:, 512:768].rearrange("p (h f k) -> p h f k", h=HEADS, f=2)
        cval = sel[:, 768:896].rearrange("p (h k) -> p h k", h=HEADS)
        cidx = sel[:, 896:1024].bitcast(U32)
        part = sel[:, 1024:1280].bitcast(U32).rearrange("p (f n) -> p f n", f=2)
        partf = sel[:, 1280:1536].rearrange("p (f h k) -> p f h k", f=2, h=HEADS)
        pick = sel[:, 1536:1920].rearrange("p (f n) -> p f n", f=3)
        gsum = sel[:, 1920:1928]
        pickT = W[:, 1024:1792].rearrange("p (f t) -> p f t", f=3)
        hot2 = [J[:, 4096 + 1024 * b:4096 + 1024 * (b + 1)].rearrange("p (t e) -> p t e", t=8) for b in range(2)]
        hot1 = [J[:, 6144 + 512 * b:6144 + 512 * (b + 1)].rearrange("p (t e) -> p t e", t=8) for b in range(2)]
        iota = sb("iota", P)
        diag = iota

        def key_scores(c):
            buf = J[:, 4096 + 512 * c:4096 + 512 * (c + 1)] if c < 6 else W[:, 512 * (c - 6):512 * (c - 5)]
            return buf.rearrange("p (s n) -> p s n", s=4)

        cst_in, dyn_in, x_in, onehot_in = sem("cst_in"), sem("dyn_in"), sem("x_in"), sem("onehot_in")
        cmat_in, skew_out, skew_in, y_out = sem("cmat_in"), sem("skew_out"), sem("skew_in"), sem("y_out")
        bmat_in = [sem(f"bmat_in{i}") for i in range(4)]
        slot_full = [sem(f"slot_full{i}") for i in range(RING)]
        w_used, bank_free = sem("w_used"), sem("bank_free")
        pool_const = sem("pool_const")
        dve_seq, act_seq, pool_seq = sem("dve_seq"), sem("act_seq"), sem("pool_seq")
        stat_sq, stat_used, stat_ms, stat_rs = sem("stat_sq"), sem("stat_used"), sem("stat_ms"), sem("stat_rs")
        c_ready, act_trig, dve_trig = sem("c_ready"), sem("act_trig"), sem("dve_trig")
        h_ready, h_raw, cmat_ready = sem("h_ready"), sem("h_raw"), sem("cmat_ready")
        bias_ps, bias_sb, cbias_sb = sem("bias_ps"), sem("bias_sb"), sem("cbias_sb")
        x_ps, x_read, scan_out, rotated, scan_free = sem("x_ps"), sem("x_read"), sem("scan_out"), sem("rotated"), sem("scan_free")
        diag_ready, z_ready, gates_ps, gates_sb = sem("diag_ready"), sem("z_ready"), sem("gates_ps"), sem("gates_sb")
        blk_ready, cmp_hid_sb, cmp_ps, cmp_sb = sem("blk_ready"), sem("cmp_hid_sb"), sem("cmp_ps"), sem("cmp_sb")
        glu_sb, mix_ready = sem("glu_sb"), sem("mix_ready")
        v_ps, v_sb = sem("v_ps"), sem("v_sb")
        score_ps, logit_sb, negmax, exp_sb, prob_sb = sem("score_ps"), sem("logit_sb"), sem("negmax"), sem("exp_sb"), sem("prob_sb")
        probT_ps, probT_sb, att_ps, att_sb = sem("probT_ps"), sem("probT_sb"), sem("att_ps"), sem("att_sb")
        key_ps, key_sb, topv, gexp, picked, pickT_ps, pickT_sb = (
            sem("key_ps"), sem("key_sb"), sem("topv"), sem("gexp"), sem("picked"), sem("pickT_ps"), sem("pickT_sb"))
        hot2_ready, hot1_ready, hot_used, route_used = sem("hot2_ready"), sem("hot1_ready"), sem("hot_used"), sem("route_used")
        z_all, pooled, pool_ps, pool_sb = sem("z_all"), sem("pooled"), sem("pool_ps"), sem("pool_sb")
        conv_done, ln_ps, ln_mu, ln_x, va_ready, yc_ready = (
            sem("conv_done"), sem("ln_ps"), sem("ln_mu"), sem("ln_x"), sem("va_ready"), sem("yc_ready"))
        pool_tick = sem("pool_tick")
        iota_ready = sem("iota_ready")
        merged, out_ready, relu_sb = sem("merged"), sem("out_ready"), sem("relu_sb")

        block = ctx.enter_context(nc.Block())

        @block.sync
        def _(sp):
            def load(u, slot):
                sp.dma_start(ring[:, slot * UNIT:(slot + 1) * UNIT], wst[u, :, :]).then_inc(slot_full[slot], 16)

            for u in range(RING):
                load(u, u)
            turns = N_UNITS // RING
            with sp.Fori(1, turns) as i:
                for s in range(RING):
                    sp.wait_ge(w_used, i * RING + (s + 1 - RING))
                    sp.dma_start(ring[:, s * UNIT:(s + 1) * UNIT],
                                 wst[bass.ds(i * RING + s, 1), :, :].rearrange("o p n -> (o p) n"))\
                      .then_inc(slot_full[s], 16)
            for u in range(turns * RING, N_UNITS):
                sp.wait_ge(w_used, u + 1 - RING)
                load(u, u % RING)
            sp.wait_ge(out_ready, 1)
            sp.dma_start(out_d.rearrange("p k t -> p (k t)"), X[:, :]).then_inc(y_out, 16)
            sp.wait_ge(y_out, 16)

        @block.tensor
        def _(pe_):
            def slot_ready(u0, j, i):
                s = (u0 + j) % RING
                pe_.wait_ge(slot_full[s], i * 16 + 16 * ((u0 + j) // RING + 1))
                return s

            def stage(name, emit, n=None, first=0, lead=1, drained=True):
                u0 = FIRST[name] + first
                n = n if n is not None else dict(STREAM)[name] - first
                if drained:
                    pe_.wait_ge(bank_free, u0 + 4)

                def body(i, js):
                    for j in js:
                        s = slot_ready(u0, j, i)
                        if lead != 2 or j % 2 == 0:
                            pe_.wait_ge(bank_free, i * 4 + (u0 + j + lead))
                        emit(s, j).then_inc(w_used, 1)

                turns = n // 4
                if turns > 1:
                    with pe_.Fori(0, turns) as i:
                        body(i, range(4))
                elif turns:
                    body(0, range(4))
                if n % 4:
                    body(turns, range(n % 4))

            def unit_a(s, bank, rhs):
                for m in range(2):
                    for k in range(KT):
                        w = ring[:, s * UNIT + k * 256 + m * P:s * UNIT + k * 256 + (m + 1) * P]
                        mm = nc.tensor.matmul(psW[:, bank, m * T:(m + 1) * T], w, rhs(k),
                                              start=(k == 0), stop=(k == KT - 1))
                return mm

            def unit_b(s, j, rhs):
                for k in range(32):
                    w = ring[:, s * UNIT + k * P:s * UNIT + (k + 1) * P]
                    mm = nc.tensor.matmul(psW[:, j // 2, 0:T], w, rhs(32 * (j % 2) + k),
                                          start=(j % 2 == 0 and k == 0), stop=(j % 2 == 1 and k == 31))
                return mm

            def stat_sum(q):
                n = STATS[q]
                if q:
                    pe_.wait_ge(stat_ms, q)
                for ci, (a, m) in enumerate(chunks_of(n)):
                    g = STAT_CHUNK0[q] + ci
                    pe_.wait_ge(stat_sq, g + 1)
                    for k in range(m):
                        mm = nc.tensor.matmul(psM[:, 3, 0:T], ones[:, :], tiles(W, CHUNK * (ci % 2) + k),
                                              start=(a + k == 0), stop=(a + k == n - 1))
                    mm.then_inc(stat_used, 1)

            pe_.wait_ge(onehot_in, 16)
            pe_.wait_ge(pool_const, 4)
            table = onehot[:, SKEW_W + ASC_W:SKEW_W + ASC_W + HEADS]
            for h in range(HEADS):
                if h >= 4:
                    pe_.wait_ge(bias_sb, h - 3)
                nc.tensor.matmul(psM[:, h % 4, 0:SKEW_W], table[:, h:h + 1].to_broadcast([33, P]),
                                 onehot[:, 0:SKEW_W], start=True, stop=True).then_inc(bias_ps, 1)
            for qb in range(2):
                for n in range(N_CMP):
                    a = SKEW_W + ASC_0 + qb * P - 16 * n - 31
                    mm = nc.tensor.matmul(psW[:, 0, (qb * N_CMP + n) * 8:(qb * N_CMP + n) * 8 + 8],
                                          onehot[:, a:a + P], table, start=True, stop=True)
            mm.then_inc(bias_ps, 1)
            pe_.wait_ge(bias_sb, HEADS)
            pe_.wait_ge(cbias_sb, 1)

            pe_.wait_ge(c_ready, 1)

            def ada(s, j):
                for m in range(2):
                    for k in range(KT):
                        w = ring[:, s * UNIT + k * 256 + m * P:s * UNIT + k * 256 + (m + 1) * P]
                        mm = nc.tensor.matmul(psW[:, j, m:m + 1], w, csilu[:, k:k + 1],
                                              start=(k == 0), stop=(k == KT - 1))
                return mm
            stage("ada", ada, n=16)
            stat_sum(0)
            stage("ada", ada, first=16, drained=False)
            pe_.wait_ge(h_ready, 1)
            h_rhs = lambda k: tiles(H, k)
            stage("w_in", lambda s, j: unit_a(s, j, h_rhs), n=4)

            pe_.wait_ge(bank_free, FIRST["w_in"] + 8)
            pe_.wait_ge(cmat_ready, 1)
            pe_.wait_ge(dyn_in, 16)
            for what, v in early_schedule():
                if what == "unit":
                    u = FIRST["w_in"] + v
                    s = slot_ready(u, 0, 0)
                    pe_.wait_ge(bank_free, u + 1)
                    unit_a(s, v % 4, h_rhs).then_inc(w_used, 1)
                elif what == "x":
                    ct, j = v // 4, v % 4
                    if j == 0:
                        pe_.wait_ge(bmat_in[ct % 4], 16 * (ct // 4 + 1))
                    if v >= 2:
                        pe_.wait_ge(x_read, v - 1)
                    for r in range(2):
                        mm = nc.tensor.matmul(psM[:, v % 2, r * T:(r + 1) * T],
                                              bmat[32 * j:32 * j + 32, ct % 4, r, :],
                                              J[32 * j:32 * j + 32, ct * T:(ct + 1) * T], start=True, stop=True)
                    mm.then_inc(x_ps, 1)
                elif what == "y":
                    ct, j = v // 4, v % 4
                    if j == 0:
                        pe_.wait_ge(diag_ready, ct + 1)
                        pe_.wait_ge(z_ready, ct) if ct else None
                        nc.tensor.matmul(psM[:, 2, 0:T], diag[:, :], tiles(J, ct), start=True, stop=False)
                    pe_.wait_ge(rotated, v + 1)
                    for r in range(2):
                        mm = nc.tensor.matmul(psM[32 * j:32 * j + 32, 2, 0:T], cmat[:, r, v, :], scanb[:, v % 2, r, :],
                                              start=False, stop=(r == 1))
                    mm.then_inc(scan_free, 1)
                elif what == "gates":
                    for qb in range(2):
                        for k in range(KT):
                            mm = nc.tensor.matmul(psM[:, 3, qb * 24:qb * 24 + 24],
                                                  H[:, k * T + qb * P:k * T + (qb + 1) * P], gate_w[:, k, :],
                                                  start=(k == 0), stop=(k == KT - 1))
                    mm.then_inc(gates_ps, 1)
                elif what == "cmp":
                    u = FIRST["cmp"] + v
                    if v == 0:
                        pe_.wait_ge(bank_free, u + 4)
                        pe_.wait_ge(blk_ready, 1)
                    s = slot_ready(u, 0, 0)
                    kv, part_ = v // 2, v % 2
                    for m in range(2):
                        for o in range(16):
                            mm = nc.tensor.matmul(psW[:, 2 * kv + m, 0:30],
                                                  ring[:, s * UNIT + o * 256 + m * P:s * UNIT + o * 256 + (m + 1) * P],
                                                  blk[:, kv, 16 * part_ + o, :],
                                                  start=(part_ == 0 and o == 0), stop=(part_ == 1 and o == 15))
                    mm.then_inc(w_used, 1)
            pe_.wait_ge(cmp_hid_sb, 2)
            pe_.wait_ge(gates_sb, 1)
            for m in range(2):
                nc.tensor.matmul(psM[:, 3, 0:30], w2[:, 0, m, :], cmp_hid[:, 0, m, :], start=(m == 0), stop=(m == 1))
            for g in range(2):
                for m in range(2):
                    mm = nc.tensor.matmul(psM[0:N_CMP, 3, 128 + 128 * g:256 + 128 * g], cmp_hid[:, 1, m, 15 * g:15 * g + 15],
                                          w2[:, 1, m, :], start=(m == 0), stop=(m == 1))
            mm.then_inc(cmp_ps, 1)

            pe_.wait_ge(z_ready, 8)

            def glu(s, j):
                for m in range(4):
                    for k in range(8):
                        mm = nc.tensor.matmul(psW[:, 2 * j + m // 2, (m % 2) * T:(m % 2 + 1) * T],
                                              ring[:, s * UNIT + k * 512 + m * P:s * UNIT + k * 512 + (m + 1) * P],
                                              tiles(J, k), start=(k == 0), stop=(k == 7))
                return mm
            stage("glu", glu)
            pe_.wait_ge(cmp_sb, 2)
            stat_sum(1)
            pe_.wait_ge(bank_free, FIRST["w_out"] + 4)
            for b in range(2):
                for g in range(2):
                    for s2 in range(2):
                        tile = 16 + 4 * (b + 1) + 2 + g
                        mm = nc.tensor.transpose(psW[:, b, (2 * g + s2) * P:(2 * g + s2 + 1) * P],
                                                 J[:, tile * T + s2 * P:tile * T + (s2 + 1) * P], ident[:, :])
                mm.then_inc(v_ps, 1)
            pe_.wait_ge(v_sb, 2)

            def scores(r):
                h, qb = r // 2, r % 2
                g, nk = h // 4, P * (qb + 1)
                q = J[:, (8 + h) * T + qb * P:(8 + h) * T + (qb + 1) * P]
                if r >= 2:
                    pe_.wait_ge(logit_sb, r - 1)
                for b in range(2):
                    kt = 16 + 4 * (b + 1) + g
                    nc.tensor.matmul(psW[:, r % 2, b * 256:b * 256 + nk], q, J[:, kt * T:kt * T + nk],
                                     start=True, stop=True)
                nc.tensor.matmul(psM[:, r % 2, 0:N_CMP], q, kc[:, 15 * g:15 * g + 15],
                                 start=True, stop=True).then_inc(score_ps, 1)

            def prob_turn(r):
                h, qb = r // 2, r % 2
                pe_.wait_ge(prob_sb, r + 1)
                if r >= 1:
                    pe_.wait_ge(probT_sb, 2 * r)
                for b in range(2):
                    for s2 in range(qb + 1):
                        nc.tensor.transpose(psW[:, 2, (2 * b + s2) * P:(2 * b + s2 + 1) * P],
                                            logit[r % 3][:, b * 256 + s2 * P:b * 256 + (s2 + 1) * P], ident[:, :])
                nc.tensor.transpose(psM[0:N_CMP, 2, 0:P], logit[r % 3][:, 512:512 + N_CMP], ident[:, :])\
                    .then_inc(probT_ps, 1)

            def att_out(r):
                h, qb = r // 2, r % 2
                g = h // 4
                pe_.wait_ge(probT_sb, 2 * (r + 1))
                if r >= 1:
                    pe_.wait_ge(att_sb, r)
                first = True
                for b in range(2):
                    for s2 in range(qb + 1):
                        nc.tensor.matmul(psW[:, 3, 0:P], vnat[:, b, g, s2, :],
                                         probT[r % 2][:, (2 * b + s2) * P:(2 * b + s2 + 1) * P], start=first, stop=False)
                        first = False
                nc.tensor.matmul(psW[:, 3, 0:P], vc[:, g, :], probT[r % 2][0:N_CMP, 512:512 + P],
                                 start=False, stop=True).then_inc(att_ps, 1)

            pe_.wait_ge(skew_in, 16)
            for r in range(16 + 2):
                if r < 16:
                    scores(r)
                if 1 <= r <= 16:
                    prob_turn(r - 1)
                if r >= 2:
                    att_out(r - 2)
            stat_sum(2)
            pe_.wait_ge(mix_ready, 2)
            stage("w_out", lambda s, j: unit_a(s, j, lambda k: tiles(J, k)))
            stat_sum(3)
            pe_.wait_ge(h_ready, 2)
            stage("peer_q", lambda s, j: unit_a(s, j, h_rhs))
            pe_.wait_ge(bank_free, FIRST["u0"] + 4)
            pe_.wait_ge(dyn_in, 32)
            for c in range(8):
                qb = c // 4
                if c >= 2:
                    pe_.wait_ge(key_sb, c - 1)
                for s4 in range(4):
                    t = 2 * (2 * (c % 4) + s4 // 2) + s4 % 2
                    mm = nc.tensor.matmul(psM[:, c % 2, s4 * P:(s4 + 1) * P], J[:, t * T + qb * P:t * T + (qb + 1) * P],
                                          keys[:, s4 % 2, :], start=True, stop=True)
                mm.then_inc(key_ps, 1)

            def turn_picks(qb):
                pe_.wait_ge(picked, qb + 1)
                if qb:
                    pe_.wait_ge(pickT_sb, 1)
                for f in range(3):
                    mm = nc.tensor.transpose(psM[:, 2, f * P:(f + 1) * P], pick[:, f, :], ident[:, :])
                mm.then_inc(pickT_ps, 1)

            expert_in = lambda s, j: unit_a(s, j, h_rhs)
            for half in range(2):
                if half == 0:
                    stage("u0", expert_in, n=16)
                    turn_picks(0)
                    stage("u0", expert_in, first=16, n=12, drained=False)
                    turn_picks(1)
                    stage("u0", expert_in, first=28, n=4, drained=False)
                else:
                    stage("u1", expert_in)
                pe_.wait_ge(bank_free, FIRST[f"v{half}"] + 4)
                with pe_.Fori(0, 16) as i:
                    for b in range(2):
                        n = i * 2 + (32 * half + b + 1)
                        pe_.wait_ge(hot2_ready, n)
                        pe_.wait_ge(hot1_ready, n)
                        pe_.wait_ge(route_used, n)
                        for t in range(8):
                            mm = nc.tensor.matmul(psM[:, b, t * 64:(t + 1) * 64], hot2[b][:, t, :], hot1[b][:, t, :],
                                                  start=True, stop=True)
                        mm.then_inc(hot_used, 1)
                pe_.wait_ge(route_used, 32 * (half + 1) + 2)
                stage(f"v{half}", lambda s, j: unit_b(s, j, lambda k: tiles(A, k)), lead=2)
            stat_sum(4)
            stat_sum(5)
            pe_.wait_ge(h_ready, 3)
            stage("z", lambda s, j: unit_a(s, j, h_rhs))
            stage("gate", lambda s, j: unit_a(s, j, h_rhs), n=16)
            pe_.wait_ge(dyn_in, 48)
            pe_.wait_ge(pooled, 1)
            for g in range(4):
                mm = nc.tensor.matmul(psM[:, g // 2, (g % 2) * T:(g % 2 + 1) * T], pool_w[:, g, :], tiles(A, 60 + g),
                                      start=True, stop=True)
            mm.then_inc(pool_ps, 1)
            pe_.wait_ge(conv_done, 6)
            pe_.wait_ge(stat_ms, 6)
            for k in range(6):
                mm = nc.tensor.matmul(psM[:, 3, 0:T], ones[:, :], tiles(A, 54 + k), start=(k == 0), stop=(k == 5))
            mm.then_inc(ln_ps, 1)
            stage("gate", lambda s, j: unit_a(s, j, h_rhs), first=16, n=4, drained=False)
            pe_.wait_ge(ln_mu, 1)
            stat_sum(6)
            stage("gate", lambda s, j: unit_a(s, j, h_rhs), first=20, n=4, drained=False)

            pe_.wait_ge(va_ready, 6)
            pe_.wait_ge(pool_sb, 1)
            pe_.wait_ge(yc_ready, 1)
            mix_rhs = [tiles(A, 54 + k) for k in range(6)] + [tiles(J, 18 + k) for k in range(4)] + \
                      [tiles(J, k) for k in range(6)]

            def abc(s, j):
                ps = psW if j % 2 == 0 else psM
                for b, (k0, k1) in enumerate(((0, 6), (6, 10), (10, 16))):
                    for m in range(2):
                        for k in range(k0, k1):
                            mm = nc.tensor.matmul(ps[:, b, m * T:(m + 1) * T],
                                                  ring[:, s * UNIT + k * 256 + m * P:s * UNIT + k * 256 + (m + 1) * P],
                                                  mix_rhs[k], start=(k == k0), stop=(k == k1 - 1))
                return mm
            stage("abc", abc, lead=3)
            pe_.wait_ge(merged, 1)
            stage("w_o", lambda s, j: unit_a(s, j, h_rhs))
            stat_sum(7)
            pe_.wait_ge(h_ready, 4)
            stage("up", lambda s, j: unit_a(s, j, h_rhs))
            pe_.wait_ge(relu_sb, 32)
            stage("down", lambda s, j: unit_b(s, j, lambda k: tiles(A, k)), lead=2)
            stat_sum(8)


        @block.vector
        def _(v):
            D = Chain(v, dve_seq)
            tt, ts, stt = v.tensor_tensor, v.tensor_scalar, v.scalar_tensor_tensor

            def squares(q, src):
                for ci, (a, m) in enumerate(chunks_of(STATS[q])):
                    g = STAT_CHUNK0[q] + ci
                    if g >= 2:
                        v.wait_ge(stat_used, g - 1)
                    tt(tiles(W, CHUNK * (ci % 2), m), src(a, m), src(a, m), ALU.mult).then_inc(stat_sq, 1)

            def inverse_rms(q):
                v.wait_ge(stat_used, STAT_CHUNK0[q] + len(chunks_of(STATS[q])))
                D.put(ts(rs[:, :], psM[:, 3, 0:T], 1.0 / (STATS[q] * P), EPS, ALU.mult, ALU.add))
                D.wait()
                v.reciprocal(rs[:, :], rs[:, :]).then_inc(stat_ms, 1)
                v.wait_ge(stat_rs, q + 1)

            def par(k):
                return J[:, 4096 + 32 * k:4096 + 32 * (k + 1)]
            dt, lrdt, th, rnd, r, co, cos, sin, w_re, w_im, pr, pi, q1, q2, q3, npr, npi = (par(k) for k in range(17))
            lr, li = const("lam_re", 0, 32), const("lam_im", 0, 32)

            def step(ins):
                D.put(ins)
                D.wait()

            v.wait_ge(act_trig, 1)
            tt(lrdt, lr, dt, ALU.mult).then_inc(dve_trig, 1)
            step(tt(th, li, dt, ALU.mult))
            magic = 12582912.0
            c1 = 6.28125
            c2 = float(np.float32(int((2 * math.pi - c1) * 2 ** 20) / 2 ** 20))
            c3 = 2 * math.pi - c1 - c2
            step(ts(rnd, th, 1 / (2 * math.pi), magic, ALU.mult, ALU.add))
            step(ts(rnd, rnd, magic, None, ALU.subtract))
            step(stt(r, rnd, -c1, th, ALU.mult, ALU.add))
            step(stt(r, rnd, -c2, r, ALU.mult, ALU.add))
            step(stt(r, rnd, -c3, r, ALU.mult, ALU.add))
            step(ts(r, r, 3.1415925, -3.1415925, ALU.min, ALU.max))
            step(stt(co, r, -1.0, r, ALU.mult, ALU.max))
            ts(co, co, -1.0, math.pi / 2, ALU.mult, ALU.add).then_inc(dve_trig, 1)
            v.wait_ge(act_trig, 4)
            D.put(tt(q1, mag[:, :], cos, ALU.mult))
            step(tt(q2, mag[:, :], sin, ALU.mult))
            step(ts(q1, q1, 1.0, None, ALU.subtract))
            D.put(tt(w_re, q1, lr, ALU.mult))
            D.put(tt(q3, q2, li, ALU.mult))
            D.put(tt(w_im, q2, lr, ALU.mult))
            step(tt(npr, q1, li, ALU.mult))
            D.put(tt(w_re, w_re, q3, ALU.add))
            step(tt(w_im, w_im, npr, ALU.subtract))
            D.put(tt(q1, lr, lr, ALU.mult))
            step(tt(q2, li, li, ALU.mult))
            step(tt(q1, q1, q2, ALU.add))
            step(v.reciprocal(q1, q1))
            D.put(tt(w_re, w_re, q1, ALU.mult))
            D.put(tt(w_im, w_im, q1, ALU.mult))
            D.put(v.memset(tab[:, :, 0, 0:1], 1.0))
            D.put(v.memset(tab[:, :, 1, 0:1], 0.0))
            D.put(v.tensor_copy(pr, cos))
            step(v.tensor_copy(pi, sin))
            tmp = H[:, :].rearrange("p (i t) -> p i t", i=NSTATE_T)
            k = 1
            while k < T:
                def wide(x):
                    return x.unsqueeze(2).to_broadcast([P, NSTATE_T, k])
                c0, s0, cd, sd = tab[:, :, 0, 0:k], tab[:, :, 1, 0:k], tab[:, :, 0, k:2 * k], tab[:, :, 1, k:2 * k]
                D.put(tt(cd, c0, wide(pr), ALU.mult))
                step(tt(tmp[:, :, 0:k], s0, wide(pi), ALU.mult))
                D.put(tt(cd, cd, tmp[:, :, 0:k], ALU.subtract))
                D.put(tt(sd, c0, wide(pi), ALU.mult))
                D.wait(1)
                step(tt(tmp[:, :, 0:k], s0, wide(pr), ALU.mult))
                D.put(tt(sd, sd, tmp[:, :, 0:k], ALU.add))
                D.put(tt(npr, pr, pr, ALU.mult))
                D.put(tt(q1, pi, pi, ALU.mult))
                step(stt(npi, pr, 2.0, pi, ALU.mult, ALU.mult))
                D.put(tt(pr, npr, q1, ALU.subtract))
                step(v.tensor_copy(pi, npi))
                k *= 2

            v.wait_ge(x_in, 16)
            squares(0, lambda a, m: tiles(X, a, m))
            inverse_rms(0)
            v.wait_ge(bank_free, 16 + 4)
            step(tt(mod[:, 0:32], mod[:, 0:32], const("b_ada", 0, 32), ALU.add))
            step(stt(affine[:, :], mod[:, 16:32], 1.0, const("norm1_g", 0, 16), ALU.add, ALU.mult))
            for k in range(KT):
                D.put(stt(tiles(H, k), tiles(X, k), affine[:, k:k + 1], rs[:, :], ALU.mult, ALU.mult))
            for k in range(KT):
                D.wait(KT - 1)
                ins = ts(tiles(H, k), tiles(H, k), mod[:, k:k + 1], None, ALU.add)
                if k < KT - 1:
                    D.put(ins)
                else:
                    ins.then_inc(h_ready, 1)
            v.wait_ge(cmat_in, 16)
            cre, cim = cmat[:, 0, :, :], cmat[:, 1, :, :]
            t_a = X[:, 2048:3072].rearrange("p (i c) -> p i c", i=NSTATE_T)
            t_b = X[:, 3072:4096].rearrange("p (i c) -> p i c", i=NSTATE_T)
            wr = w_re.unsqueeze(2).to_broadcast([P, NSTATE_T, 32])
            wi = w_im.unsqueeze(2).to_broadcast([P, NSTATE_T, 32])
            D.put(tt(t_a, cim, wi, ALU.mult))
            D.put(tt(t_b, cre, wi, ALU.mult))
            D.wait()
            D.put(tt(cre, cre, wr, ALU.mult))
            D.put(tt(cim, cim, wr, ALU.mult))
            D.wait()
            D.put(tt(cre, cre, t_a, ALU.subtract))
            stt(cim, cim, -1.0, t_b, ALU.mult, ALU.subtract).then_inc(cmat_ready, 1)
            v.wait_ge(bank_free, 48 + 4)
            step(tt(mod[:, 32:96], mod[:, 32:96], const("b_ada", 32, 64), ALU.add))
            v.wait_ge(cmat_ready, 1)

            t1 = W[:, 0:512].rearrange("p (r t) -> p r t", r=2)
            t2 = W[:, 512:1024].rearrange("p (r t) -> p r t", r=2)
            with D.loop(8, 16) as c:
                for j in range(4):
                    v.wait_ge(x_ps, c * 4 + (j + 1))
                    cosv = A[:, bass.ds(c * 2048 + j * 512, T)].unsqueeze(1).to_broadcast([P, 2, T])
                    sinv = A[:, bass.ds(c * 2048 + (j * 512 + T), T)].unsqueeze(1).to_broadcast([P, 2, T])
                    xp = psM[:, j % 2, :].rearrange("p (r t) -> p r t", r=2)
                    D.put(tt(t1, xp, cosv, ALU.mult))
                    tt(t2, xp, sinv, ALU.mult).then_inc(x_read, 1)
                    D.wait()
                    v.wait_ge(x_read, c * 4 + (j + 1))
                    D.put(tt(t1[:, 0, :], t1[:, 0, :], t2[:, 1, :], ALU.add))
                    D.put(tt(t1[:, 1, :], t1[:, 1, :], t2[:, 0, :], ALU.subtract))
                    v.wait_ge(scan_free, c * 4 + (j + 1))
                    m = mag[:, bass.ds(c * 4 + j, 1)].to_broadcast([P, T])
                    D.wait(1)
                    D.put(v.tensor_tensor_scan(out=scanb[:, j % 2, 0, :], data0=m, data1=t1[:, 0, :], initial=0.0,
                                               op0=ALU.mult, op1=ALU.add))
                    D.wait(1)
                    v.tensor_tensor_scan(out=scanb[:, j % 2, 1, :], data0=m, data1=t1[:, 1, :], initial=0.0,
                                         op0=ALU.mult, op1=ALU.add).then_inc(scan_out, 1)
                    v.wait_ge(scan_out, c * 4 + (j + 1))

            v.wait_ge(glu_sb, 8)
            step(tt(J[:, 0:8 * T], J[:, 0:8 * T], glu_s, ALU.mult))
            squares(1, lambda a, m: tiles(J, a, m))
            inverse_rms(1)

            def scale_rms(buf, k0, n, name, g0, signal=None):
                for k in range(n):
                    ins = stt(tiles(buf, k0 + k), tiles(buf, k0 + k), const(name, g0 + k), rs[:, :], ALU.mult, ALU.mult)
                    if k == n - 1 and signal is not None:
                        ins.then_inc(signal, 1)
                    else:
                        D.put(ins)
            scale_rms(J, 0, 8, "beta", 0, mix_ready)

            v.wait_ge(skew_in, 16)
            v.wait_ge(gates_sb, 1)
            v.wait_ge(pool_const, 4)

            def views(r):
                nk = P * (r % 2 + 1)
                two = logit[r % 3][:, 0:512].rearrange("p (b s) -> p b s", b=2)[:, :, 0:nk]
                return nk, two, logit[r % 3][:, 512:512 + N_CMP]

            def logits(r):
                h, qb = r // 2, r % 2
                nk, two, lc = views(r)
                v.wait_ge(score_ps, r + 1)
                if r >= 3:
                    v.wait_ge(probT_ps, r - 2)
                ps = psW[:, r % 2, :].rearrange("p (b s) -> p b s", b=2)[:, :, 0:nk]
                D.put(stt(two, ps, SCALE, bias[:, h:h + 1, 256 - nk:256].to_broadcast([P, 2, nk]), ALU.mult, ALU.add))
                stt(lc, psM[:, r % 2, 0:N_CMP], SCALE, cbias[:, qb, :, h], ALU.mult, ALU.add).then_inc(logit_sb, 1)
                D.wait()
                D.put(v.tensor_reduce(mxb[:, r % 3, 0:2], two, AX_X, ALU.max))
                v.wait_ge(logit_sb, r + 1)
                D.put(v.tensor_reduce(mxb[:, r % 3, 2:3], lc, AX_X, ALU.max))
                D.wait()
                ts(mxb[:, r % 3, :], mxb[:, r % 3, :], -1.0, None, ALU.mult).then_inc(negmax, 1)

            def probs(r):
                h, qb = r // 2, r % 2
                nk, two, lc = views(r)
                v.wait_ge(exp_sb, 3 * (r + 1))
                step(v.reciprocal(smb[:, r % 3, :], smb[:, r % 3, :]))
                step(tt(smb[:, r % 3, :], smb[:, r % 3, :], gates[:, qb, h, :], ALU.mult))
                for b in range(2):
                    D.put(ts(two[:, b, :], two[:, b, :], smb[:, r % 3, b:b + 1], None, ALU.mult))
                stt(lc, lc, smb[:, r % 3, 2:3], cvalid[:, qb, :], ALU.mult, ALU.mult).then_inc(prob_sb, 1)

            for r in range(16 + 1):
                if r < 16:
                    logits(r)
                if r >= 1:
                    probs(r - 1)
            v.wait_ge(att_sb, 16)
            squares(2, lambda a, m: tiles(J, 8 + a, m))
            inverse_rms(2)
            scale_rms(J, 8, 8, "beta", 8, mix_ready)

            def residual(name, gain, per_unit):
                u0, n = FIRST[name], dict(STREAM)[name]
                with v.Fori(0, n // 4) as i:
                    for j in range(4):
                        if per_unit == 2:
                            v.wait_ge(w_used, i * 4 + (u0 + j + 1))
                            for m in range(2):
                                x = X[:, bass.ds(i * 8 * T + (2 * j + m) * T, T)]
                                g = mod[:, bass.ds(i * 8 + (gain + 2 * j + m), 1)]
                                ins = stt(x, psW[:, j, m * T:(m + 1) * T], g, x, ALU.mult, ALU.add)
                            ins.then_inc(bank_free, 1)
                        elif j % 2:
                            v.wait_ge(w_used, i * 4 + (u0 + j + 1))
                            x = X[:, bass.ds(i * 2 * T + (j // 2) * T, T)]
                            if gain is None:
                                ins = tt(x, psW[:, j // 2, 0:T], x, ALU.add)
                            else:
                                g = mod[:, bass.ds(i * 2 + (gain + j // 2), 1)]
                                ins = stt(x, psW[:, j // 2, 0:T], g, x, ALU.mult, ALU.add)
                            ins.then_inc(bank_free, 2)

            v.wait_ge(x_in, 32)
            residual("w_out", 32, 2)
            v.wait_ge(bank_free, FIRST["peer_q"] + 4)
            squares(3, lambda a, m: tiles(X, a, m))
            inverse_rms(3)
            step(stt(affine[:, :], mod[:, 64:80], 1.0, const("norm2_g", 0, 16), ALU.add, ALU.mult))
            for k in range(KT):
                stt(tiles(H, k), tiles(X, k), affine[:, k:k + 1], rs[:, :], ALU.mult, ALU.mult).then_inc(h_raw, 1)

            io16 = iota[:, 0:16].unsqueeze(1).unsqueeze(1)
            v.wait_ge(iota_ready, 1)
            for qb in range(2):
                v.wait_ge(key_sb, 8)
                if qb:
                    v.wait_ge(pickT_ps, 1)
                for h in range(HEADS):
                    s4 = key_scores(4 * qb + h // 2)
                    for f in range(2):
                        s = s4[:, (h % 2) * 2 + f, :]
                        step(v.max(val[:, h, f, 0:8], s))
                        D.put(v.max_index(idx[:, h, f, 0:8], val[:, h, f, 0:8], s))
                        D.wait()
                        step(v.match_replace(s, val[:, h, f, 0:8], s, -3e38))
                        step(v.max(val[:, h, f, 8:16], s))
                        step(v.max_index(idx[:, h, f, 8:16], val[:, h, f, 8:16], s))
                for h in range(HEADS):
                    D.put(tt(cand[:, h, :, :], val[:, h, 0, :].unsqueeze(2).to_broadcast([P, TOPK, TOPK]),
                             val[:, h, 1, :].unsqueeze(1).to_broadcast([P, TOPK, TOPK]), ALU.add))
                D.put(v.tensor_copy(sel[:, 512:768], sel[:, 256:512].bitcast(U32)))
                D.wait()
                for h in range(HEADS):
                    cf = cand[:, h, :, :].rearrange("p a b -> p (a b)")
                    ci = cidx[:, h * TOPK:(h + 1) * TOPK]
                    step(v.max(cval[:, h, 0:8], cf))
                    step(v.max_index(ci[:, 0:8], cval[:, h, 0:8], cf))
                    step(v.match_replace(cf, cval[:, h, 0:8], cf, -3e38))
                    step(v.max(cval[:, h, 8:16], cf))
                    step(v.max_index(ci[:, 8:16], cval[:, h, 8:16], cf))
                pgate = pick[:, 2, :].rearrange("p (h k) -> p h k", h=HEADS)
                tt(pgate, cval, cval[:, :, 0:1].to_broadcast([P, HEADS, TOPK]), ALU.subtract).then_inc(topv, 1)
                D.put(ts(part[:, 0, :], cidx, 4, None, ALU.logical_shift_right))
                D.put(ts(part[:, 1, :], cidx, 15, None, ALU.bitwise_and))
                D.wait()
                step(v.tensor_copy(sel[:, 1280:1536], sel[:, 1024:1280].bitcast(U32)))
                for f in range(2):
                    step(tt(cand, partf[:, f, :, :].unsqueeze(3).to_broadcast([P, HEADS, TOPK, TOPK]),
                            io16.to_broadcast([P, HEADS, TOPK, TOPK]), ALU.is_equal))
                    step(tt(cand, cand, idxf[:, :, f, :].unsqueeze(2).to_broadcast([P, HEADS, TOPK, TOPK]), ALU.mult))
                    step(v.tensor_reduce(pick[:, f, :].rearrange("p (h k) -> p h k", h=HEADS), cand, AX_X, ALU.add))
                v.wait_ge(gexp, qb + 1)
                step(v.tensor_reduce(gsum, pgate, AX_X, ALU.add))
                step(v.reciprocal(gsum, gsum))
                tt(pgate, pgate,
                   gsum.unsqueeze(2).to_broadcast([P, HEADS, TOPK]), ALU.mult).then_inc(picked, 1)

            v.wait_ge(pickT_sb, 2)
            acts = A[:, :].rearrange("p (e t) -> p t e", e=EXP_T)
            for half in range(2):
                v.wait_ge(bank_free, FIRST[f"v{half}"] + 4)
                with D.loop(16, 2) as i:
                    for b in range(2):
                        cols = lambda f: W[:, bass.ds(i * 16 + (1024 + f * T + 8 * b), 8)].unsqueeze(2).to_broadcast([P, 8, 64])
                        v.wait_ge(hot_used, i * 2 + (32 * half + b + 1))
                        D.put(tt(hot1[b], iota[:, 64 * half:64 * half + 64].unsqueeze(1).to_broadcast([P, 8, 64]),
                                 cols(0), ALU.is_equal))
                        D.wait()
                        tt(hot1[b], hot1[b], cols(2), ALU.mult).then_inc(hot1_ready, 1)
                    for b in range(2):
                        v.wait_ge(hot_used, i * 2 + (32 * half + b + 3))
                        a = acts[:, bass.ds(i * 16 + 8 * b, 8), :]
                        tt(a, a, psM[:, b, :].rearrange("p (t e) -> p t e", t=8), ALU.mult).then_inc(route_used, 1)
                residual(f"v{half}", 80, 1)
            v.wait_ge(bank_free, FIRST["z"] + 4)
            squares(4, lambda a, m: tiles(X, a, m))
            inverse_rms(4)
            scale_rms(X, 0, KT, "final_g", 0)
            D.wait()
            squares(5, lambda a, m: tiles(X, a, m))
            inverse_rms(5)

            def norm_into_h(name):
                for k in range(KT):
                    ins = stt(tiles(H, k), tiles(X, k), const(name, k), rs[:, :], ALU.mult, ALU.mult)
                    D.put(ins) if k < KT - 1 else ins.then_inc(h_ready, 1)
            norm_into_h("g_mix")

            v.wait_ge(bank_free, FIRST["gate"] + 4)
            step(tt(tiles(J, 22, 6), tiles(J, 22, 6), tiles(A, 48, 6), ALU.mult))
            for k in range(6):
                D.put(ts(tiles(A, 54 + k), tiles(J, 22 + k), const("w_dw_a", 31 * k + 30), const("b_dw_a", k),
                         ALU.mult, ALU.add))
            for tap in range(29, -1, -1):
                d = 30 - tap
                for k in range(6):
                    o = A[:, (54 + k) * T + d:(55 + k) * T]
                    D.wait(5 if tap else 5 - k)
                    ins = stt(o, J[:, (22 + k) * T:(23 + k) * T - d], const("w_dw_a", 31 * k + tap), o,
                              ALU.mult, ALU.add)
                    if tap:
                        D.put(ins)
                    else:
                        ins.then_inc(conv_done, 1)
            v.wait_ge(ln_ps, 1)
            step(ts(rs[:, :], psM[:, 3, 0:T], 1.0 / 768, None, ALU.mult))
            v.wait_ge(conv_done, 6)
            va = tiles(A, 54, 6).rearrange("p (k t) -> p k t", k=6)
            rs6 = rs[:, :].unsqueeze(1).to_broadcast([P, 6, T])
            tt(va, va, rs6, ALU.subtract).then_inc(ln_mu, 1)
            v.wait_ge(ln_mu, 1)
            v.wait_ge(pooled, 1)
            squares(6, lambda a, m: tiles(A, 54 + a, m))
            step(tt(tiles(J, 6, 6), tiles(J, 6, 6), tiles(J, 12, 6), ALU.mult))
            for k in range(6):
                D.put(ts(tiles(J, 12 + k), tiles(J, 6 + k), const("w_dw_c", 3 * k + 2), None, ALU.mult))
            for tap in (1, 0):
                d = 2 - tap
                for k in range(6):
                    o = J[:, (12 + k) * T + d:(13 + k) * T]
                    D.wait(5)
                    D.put(stt(o, J[:, (6 + k) * T:(7 + k) * T - d], const("w_dw_c", 3 * k + tap), o, ALU.mult, ALU.add))
            D.wait()
            tt(tiles(J, 0, 6), tiles(J, 0, 6), tiles(J, 12, 6), ALU.mult).then_inc(yc_ready, 1)
            inverse_rms(6)
            tt(va, va, rs6, ALU.mult).then_inc(ln_x, 1)

            u0 = FIRST["abc"]
            v.wait_ge(bank_free, u0 + 4)
            with D.loop(2, 16) as i:
                for j in range(4):
                    ps = psW if j % 2 == 0 else psM
                    D.wait()
                    v.wait_ge(w_used, i * 4 + (u0 + j + 1))
                    for b in range(3):
                        g = A[:, bass.ds(i * 8 * T + (16 * b + 2 * j) * T, 2 * T)]
                        ins = tt(tiles(W, 2 * b, 2), ps[:, b, :], g, ALU.mult)
                        if b < 2:
                            D.put(ins)
                        else:
                            ins.then_inc(bank_free, 1)
                    D.wait()
                    D.put(tt(tiles(W, 0, 2), tiles(W, 0, 2), tiles(W, 2, 2), ALU.add))
                    D.wait()
                    v.wait_ge(bank_free, i * 4 + (u0 + j + 5))
                    D.put(tt(H[:, bass.ds(i * 8 * T + 2 * j * T, 2 * T)], tiles(W, 0, 2), tiles(W, 4, 2), ALU.add))
            D.wait()
            v.sem_inc(merged, 1)
            u0 = FIRST["w_o"]
            with v.Fori(0, 2) as i:
                for j in range(4):
                    v.wait_ge(w_used, i * 4 + (u0 + j + 1))
                    x = X[:, bass.ds(i * 8 * T + 2 * j * T, 2 * T)]
                    tt(x, psW[:, j, :], x, ALU.add).then_inc(bank_free, 1)
            v.wait_ge(bank_free, FIRST["up"] + 4)
            squares(7, lambda a, m: tiles(X, a, m))
            inverse_rms(7)
            norm_into_h("g_mlp")
            u0 = FIRST["up"]
            with v.Fori(0, 8) as i:
                for j in range(4):
                    hid = A[:, bass.ds(i * 2048 + j * 512, 512)]
                    v.wait_ge(bank_free, i * 4 + (u0 + j + 5))
                    tt(hid, hid, hid, ALU.mult).then_inc(relu_sb, 1)
            residual("down", None, 1)
            v.wait_ge(bank_free, N_UNITS + 4)
            squares(8, lambda a, m: tiles(X, a, m))
            inverse_rms(8)
            scale_rms(X, 0, KT, "g_final", 0, out_ready)

        @block.scalar
        def _(a):
            act = a.activation
            S = Chain(a, act_seq)

            def root(q):
                a.wait_ge(stat_ms, q + 1)
                act(rs[:, :], rs[:, :], ACT.Sqrt).then_inc(stat_rs, 1)

            def take(name, put, n=None, first=0, loop=True):
                u0 = FIRST[name] + first
                n = n if n is not None else dict(STREAM)[name] - first

                def body(i, js):
                    for j in js:
                        a.wait_ge(w_used, i * 4 + (u0 + j + 1))
                        put(i, j).then_inc(bank_free, 1)
                if n >= 8:
                    with a.Fori(0, n // 4) as i:
                        body(i, range(4))
                elif n >= 4:
                    body(0, range(4))
                if n % 4:
                    body(n // 4, range(n % 4))

            def into(buf, func, j0=0):
                return lambda i, j: act(buf[:, bass.ds(i * 4 * 512 + (j0 + j) * 512, 512)]
                                        if not isinstance(i, int) else buf[:, (4 * i + j0 + j) * 512:(4 * i + j0 + j + 1) * 512],
                                        psW[:, j, :], func)

            def par(k):
                return J[:, 4096 + 32 * k:4096 + 32 * (k + 1)]
            dt, lrdt, th, rnd, r_, co, cos, sin = (par(k) for k in range(8))
            a.wait_ge(cst_in, 16)
            act(csilu[:, :], const("c", 0, KT), ACT.Silu).then_inc(c_ready, 1)
            act(dt, const("log_dt", 0, 32), ACT.Exp).then_inc(act_trig, 1)
            for h in range(HEADS):
                a.wait_ge(bias_ps, h + 1)
                act(skew_sb[:, h * SKEW_W:(h + 1) * SKEW_W], psM[:, h % 4, 0:SKEW_W], ACT.Copy).then_inc(bias_sb, 1)
            a.wait_ge(bias_ps, HEADS + 1)
            act(cbias.rearrange("p q n h -> p (q n h)"), psW[:, 0, 0:240], ACT.Copy).then_inc(cbias_sb, 1)
            a.wait_ge(dve_trig, 1)
            act(mag[:, :], lrdt, ACT.Exp).then_inc(act_trig, 1)
            a.wait_ge(dve_trig, 2)
            act(sin, r_, ACT.Sin).then_inc(act_trig, 1)
            act(cos, co, ACT.Sin).then_inc(act_trig, 1)
            def ada(j0):
                return lambda i, j: act(mod[:, bass.ds(i * 8 + 2 * (j0 + j), 2)], psW[:, j, 0:2], ACT.Copy)
            take("ada", ada(0), n=16)
            root(0)
            take("ada", ada(16), first=16)
            a.wait_ge(cmat_ready, 1)
            for ct in range(4):
                a.dma_start(bmat[:, ct, :, :], bmat_d[:, ct, :, :]).then_inc(bmat_in[ct], 16)
            a.wait_ge(pool_const, 4)
            a.wait_ge(dyn_in, 16)
            a.wait_ge(skew_out, 16)
            take("w_in", into(J, ACT.Copy), n=4)
            act(diag[:, :], ident[:, :], ACT.Copy, scale=const("d_skip", 0)).then_inc(diag_ready, 1)
            for what, n in early_schedule():
                if what == "unit":
                    a.wait_ge(w_used, FIRST["w_in"] + n + 1)
                    act(J[:, n * 512:(n + 1) * 512], psW[:, n % 4, :], ACT.Copy).then_inc(bank_free, 1)
                elif what == "y" and n % 4 == 3:
                    ct = n // 4
                    a.wait_ge(scan_free, 2 + n + 1)
                    act(tiles(J, ct), psM[:, 2, 0:T], ACT.Gelu_apprx_tanh).then_inc(z_ready, 1)
                    if ct < 4:
                        a.dma_start(bmat[:, ct, :, :], bmat_d[:, ct + 4, :, :]).then_inc(bmat_in[ct], 16)
                    if ct < 7:
                        act(diag[:, :], ident[:, :], ACT.Copy, scale=const("d_skip", ct + 1)).then_inc(diag_ready, 1)
                elif what == "gates":
                    a.wait_ge(gates_ps, 1)
                    act(gates.rearrange("p q h c -> p (q h c)"), psM[:, 3, 0:48], ACT.Sigmoid).then_inc(gates_sb, 1)
                    a.wait_ge(bank_free, FIRST["cmp"] + 4)
                    for kv in range(2):
                        for o in range(32):
                            src = J[:, (16 + 2 * kv) * T:(18 + 2 * kv) * T].rearrange("p (g n s) -> p g n s", g=2, s=16)
                            src = src[:, :, o // 16:o // 16 + N_CMP, o % 16]
                            ins = act(blk[:, kv, o, :].rearrange("p (g n) -> p g n", g=2), src, ACT.Identity,
                                      bias=pe[:, kv, o:o + 1])
                    ins.then_inc(blk_ready, 1)
                    a.dma_start(bias, bass_skew(skew_d)).then_inc(skew_in, 16)
                elif what == "cmp" and n % 2:
                    kv = n // 2
                    a.wait_ge(w_used, FIRST["cmp"] + n + 1)
                    act(cmp_hid[:, kv, :, :], psW[:, 2 * kv:2 * kv + 2, 0:30], ACT.Gelu_apprx_tanh).then_inc(cmp_hid_sb, 1)
                    a.wait_ge(cmp_hid_sb, kv + 1)
                    a.sem_inc(bank_free, 2)
            a.wait_ge(cmp_ps, 1)
            act(kc, psM[:, 3, 0:30], ACT.Copy).then_inc(cmp_sb, 1)
            act(vc.rearrange("p g d -> p (g d)"), psM[0:N_CMP, 3, 128:384], ACT.Copy).then_inc(cmp_sb, 1)
            for u in range(2):
                a.wait_ge(w_used, FIRST["glu"] + u + 1)
                for m in range(4):
                    k = 4 * u + m
                    act(glu_s[:, k * T:(k + 1) * T], psW[:, 2 * u + m // 2, (m % 2) * T:(m % 2 + 1) * T], ACT.Sigmoid,
                        bias=const("b_glu", k)).then_inc(glu_sb, 1)
                a.wait_ge(glu_sb, 4 * (u + 1))
                a.sem_inc(bank_free, 1)
            root(1)
            for b in range(2):
                a.wait_ge(v_ps, b + 1)
                act(vnat[:, b, :, :, :].rearrange("p g s d -> p (g s d)"), psW[:, b, :], ACT.Copy).then_inc(v_sb, 1)
            for r in range(16 + 2):
                if r < 16:
                    nk = P * (r % 2 + 1)
                    a.wait_ge(negmax, r + 1)
                    for b in range(3):
                        l = logit[r % 3][:, b * 256:b * 256 + (nk if b < 2 else N_CMP)]
                        act(l, l, ACT.Exp, bias=mxb[:, r % 3, b:b + 1], accum_out=smb[:, r % 3, b:b + 1]).then_inc(exp_sb, 1)
                if 1 <= r <= 16:
                    q = r - 1
                    w = P * (q % 2 + 1)
                    a.wait_ge(probT_ps, q + 1)
                    src = psW[:, 2, :].rearrange("p (b s) -> p b s", b=2)[:, :, 0:w]
                    dst = probT[q % 2][:, 0:512].rearrange("p (b s) -> p b s", b=2)[:, :, 0:w]
                    if q >= 2:
                        a.wait_ge(att_ps, q - 1)
                    act(dst, src, ACT.Copy).then_inc(probT_sb, 1)
                    act(probT[q % 2][0:N_CMP, 512:640], psM[0:N_CMP, 2, 0:P], ACT.Copy).then_inc(probT_sb, 1)
                if r >= 2:
                    q = r - 2
                    h, qb = q // 2, q % 2
                    a.wait_ge(att_ps, q + 1)
                    act(J[:, (8 + h) * T + qb * P:(8 + h) * T + (qb + 1) * P], psW[:, 3, 0:P], ACT.Copy).then_inc(att_sb, 1)
            root(2)
            root(3)
            for k in range(KT):
                a.wait_ge(h_raw, k + 1)
                ins = act(tiles(H, k), tiles(H, k), ACT.Identity, bias=mod[:, 48 + k:49 + k])
                S.put(ins) if k < KT - 1 else ins.then_inc(h_ready, 1)
            take("peer_q", into(J, ACT.Copy))
            for c in range(8):
                a.wait_ge(key_ps, c + 1)
                act(key_scores(c).rearrange("p s n -> p (s n)"), psM[:, c % 2, :], ACT.Copy).then_inc(key_sb, 1)
            at = 0
            for qb, before_exp, before_turn in ((0, 12, 4), (1, 8, 4)):
                take("u0", into(A, ACT.Gelu_apprx_tanh, at), n=before_exp, first=at)
                a.wait_ge(topv, qb + 1)
                act(pick[:, 2, :], pick[:, 2, :], ACT.Exp).then_inc(gexp, 1)
                at += before_exp
                take("u0", into(A, ACT.Gelu_apprx_tanh, at), n=before_turn, first=at)
                at += before_turn
                a.wait_ge(pickT_ps, qb + 1)
                act(pickT[:, :, qb * P:(qb + 1) * P], psM[:, 2, 0:3 * P].rearrange("p (f t) -> p f t", f=3), ACT.Copy)\
                    .then_inc(pickT_sb, 1)
            take("u0", into(A, ACT.Gelu_apprx_tanh, at), first=at)
            take("u1", into(A, ACT.Gelu_apprx_tanh))
            root(4)
            root(5)
            take("z", into(J, ACT.Copy), n=8)
            take("z", into(J, ACT.Copy, 8), n=3, first=8)
            for n in range(11, 17):
                a.wait_ge(w_used, FIRST["z"] + n + 1)
                bank = n % 4 if n < 16 else 0
                for m in range(2):
                    k = 2 * (n - 11) + m
                    dst = tiles(J, 22 + k) if k < 6 else tiles(A, 48 + k - 6)
                    ins = act(dst, psW[:, bank, m * T:(m + 1) * T], ACT.Identity if k < 6 else ACT.Sigmoid,
                              bias=const("b_glu2", k))
                    if m == 0:
                        S.put(ins)
                ins.then_inc(bank_free, 1)

            def gate(j0):
                def put(i, j):
                    for m in range(2):
                        k = 2 * (j0 + j) + m
                        if isinstance(i, int):
                            dst, b = tiles(A, 8 * i + k), const("b_gate", 8 * i + k)
                        else:
                            dst = A[:, bass.ds(i * 8 * T + k * T, T)]
                            b = cst[:, bass.ds(i * 8 + (COL["b_gate"] + k), 1)]
                        ins = act(dst, psW[:, j, m * T:(m + 1) * T], ACT.Sigmoid, bias=b)
                    return ins
                return put
            take("gate", gate(0), n=16)
            a.wait_ge(pool_ps, 1)
            for g in range(4):
                act(tiles(J, 18 + g), psM[:, g // 2, (g % 2) * T:(g % 2 + 1) * T], ACT.Copy,
                    scale=const("pool_scale", g)).then_inc(act_seq, 1)
                S.n += 1
            S.wait()
            a.sem_inc(pool_sb, 1)
            take("gate", gate(16), n=4, first=16)
            root(6)
            a.wait_ge(ln_x, 1)
            for k in range(6):
                act(tiles(A, 54 + k), tiles(A, 54 + k), ACT.Silu, scale=const("ln_g", k), bias=const("ln_b", k))\
                    .then_inc(va_ready, 1)
            take("gate", gate(20), n=4, first=20)
            root(7)
            u0 = FIRST["up"]
            with a.Fori(0, 8) as i:
                for j in range(4):
                    a.wait_ge(w_used, i * 4 + (u0 + j + 1))
                    dst = A[:, bass.ds(i * 2048 + j * 512, 512)]
                    act(dst, psW[:, j, :], ACT.Relu).then_inc(bank_free, 1)
            root(8)

        @block.gpsimd
        def _(g):
            G = Chain(g, pool_seq)
            g.dma_start(cst[:, :], cst_d).then_inc(cst_in, 16)
            g.dma_start(onehot, onehot_d).then_inc(onehot_in, 16)
            g.dma_start(X[:, :], xT_d.rearrange("p k t -> p (k t)")).then_inc(x_in, 16)
            g.dma_start(dyn[:, 0:960], dyn1_d).then_inc(dyn_in, 16)
            G.put(g.memset(ident[:, :], 0.0))
            G.put(g.memset(cvalid.rearrange("p q n -> p (q n)"), 1.0))
            g.memset(ones[:, :], 1.0).then_inc(pool_const, 2)
            G.wait()
            g.affine_select(out=ident[:, :], in_=ident[:, :], compare_op=ALU.not_equal, fill=1.0, base=0,
                            pattern=[[-1, P]], channel_multiplier=1).then_inc(pool_const, 1)
            g.affine_select(out=cvalid, in_=cvalid, compare_op=ALU.is_ge, fill=0.0, base=-31,
                            pattern=[[P, 2], [-16, N_CMP]], channel_multiplier=1).then_inc(pool_const, 1)
            g.sem_inc(bank_free, 4)
            g.sem_inc(scan_free, 2)
            g.sem_inc(hot_used, 2)
            g.sem_inc(route_used, 2)
            g.wait_ge(bias_sb, HEADS)
            g.dma_start(skew_d.rearrange("h p w -> p h w"), skew_sb.rearrange("p (h w) -> p h w", h=HEADS))\
             .then_inc(skew_out, 16)
            g.wait_ge(h_ready, 1)
            g.dma_start(cmat, cmat_d).then_inc(cmat_in, 16)
            t3 = W[:, 1024:1536].rearrange("p (r t) -> p r t", r=2)
            t4 = W[:, 1536:2048].rearrange("p (r t) -> p r t", r=2)
            with G.loop(8, 12) as c:
                for j in range(4):
                    w = scanb[:, j % 2, :, :]
                    g.wait_ge(scan_out, c * 4 + (j + 1))
                    cosv = A[:, bass.ds(c * 2048 + j * 512, T)].unsqueeze(1).to_broadcast([P, 2, T])
                    sinv = A[:, bass.ds(c * 2048 + (j * 512 + T), T)].unsqueeze(1).to_broadcast([P, 2, T])
                    G.put(g.tensor_tensor(t3, w, cosv, ALU.mult))
                    G.put(g.tensor_tensor(t4, w, sinv, ALU.mult))
                    G.wait()
                    G.put(g.tensor_tensor(w[:, 0, :], t3[:, 0, :], t4[:, 1, :], ALU.subtract))
                    g.tensor_tensor(w[:, 1, :], t3[:, 1, :], t4[:, 0, :], ALU.add).then_inc(rotated, 1)
                    g.wait_ge(rotated, c * 4 + (j + 1))
            g.wait_ge(z_ready, 8)
            g.dma_start(X[:, :], xT_d.rearrange("p k t -> p (k t)")).then_inc(x_in, 16)
            g.wait_ge(att_sb, 16)
            g.dma_start(dyn[:, 0:256], dyn2_d).then_inc(dyn_in, 16)
            g.iota(iota[:, :], pattern=[[1, P]], base=0, channel_multiplier=0,
                   allow_small_or_imprecise_dtypes=True).then_inc(iota_ready, 1)
            g.wait_ge(iota_ready, 1)
            g.wait_ge(pickT_sb, 2)
            for half in range(2):
                with G.loop(16, 2) as i:
                    for b in range(2):
                        e2 = small[:, 18 + 8 * b:26 + 8 * b]
                        G.put(g.tensor_copy(e2, W[:, bass.ds(i * 16 + (1024 + T + 8 * b), 8)]))
                        g.wait_ge(hot_used, i * 2 + (32 * half + b + 1))
                        G.wait()
                        g.sem_inc(pool_tick, 1)
                        for t in range(8):
                            ins = g.tensor_scalar(hot2[b][:, t, :], iota[:, :], e2[:, t:t + 1], None, ALU.is_equal)
                        ins.then_inc(hot2_ready, 1)
            g.wait_ge(key_ps, 8)
            g.dma_start(dyn[:, 0:512], dyn3_d).then_inc(dyn_in, 16)
            g.wait_ge(bank_free, FIRST["z"] + 4 + 11)
            zb = [tiles(J, 18 + q) for q in range(4)]
            ping = [tiles(A, 60 + q) for q in range(4)]
            pong = [tiles(W, q) for q in range(4)]
            cur = zb
            for level in range(4):
                d = 1 << level
                nxt = ping if level % 2 == 0 else pong
                for q in range(level, 4):
                    G.put(g.tensor_copy(nxt[q][:, 0:d], cur[q][:, 0:d]))
                    G.put(g.tensor_tensor(nxt[q][:, d:T], cur[q][:, d:T], cur[q][:, 0:T - d], ALU.add))
                G.wait()
                q, w = level, 2 << level
                o = nxt[q]
                G.put(g.tensor_tensor(o[:, 0:w], o[:, 0:w], const("pool_rcnt", 16 * q, w), ALU.mult))
                G.put(g.tensor_scalar(o[:, w:T], o[:, w:T], 1.0 / w, None, ALU.mult))
                G.wait()
                ins = g.tensor_tensor(ping[q], o, zb[q], ALU.subtract)
                if level < 3:
                    G.put(ins)
                    G.wait()
                else:
                    ins.then_inc(pooled, 1)
                cur = nxt


def bass_skew(skew_d):
    return bass.AP(skew_d.tensor, 127, [[SKEW_W - 1, P], [P * SKEW_W, HEADS], [1, T]])


def bucket_onehot():
    def bucket(n):
        scaled = np.log(np.float32(max(n, 16)) / np.float32(16)).astype(np.float32) / np.float32(math.log(1024 / 16))
        large = 16 + int(np.float32(scaled) * np.float32(16))
        return n if n < 16 else min(large, 31)

    out = np.zeros((33, SKEW_W + ASC_W), np.float32)
    for c in range(SKEW_W):
        d = 255 - c
        out[32 if d < 0 else bucket(d), c] = 1
    for c in range(ASC_W):
        d = c - ASC_0
        out[32 if d < 0 else bucket(d), SKEW_W + c] = 1
    return out


def units_a(w):
    n = w.shape[1]
    return w.reshape(16, P, n // 256, 256).transpose(2, 1, 0, 3).reshape(n // 256, P, UNIT)


def units_b(w):
    n = w.shape[1]
    return w.reshape(2, 32, P, n // P, P).transpose(3, 0, 2, 1, 4).reshape(2 * (n // P), P, UNIT)


def cols(v):
    return np.ascontiguousarray(v.reshape(-1, P).T)


def layout(i):
    f = {k: np.asarray(v) for k, v in i.items()}
    w_in = f["w_in"][0]
    w_u = f["peer_u"][0].T
    w_v = f["peer_v"][0]
    z = f["w_in_2"][0]
    z = np.concatenate([z[:, 2048:4352], z[:, 1536:2048], z[:, 0:1536]], axis=1)
    abc = np.concatenate([f["w_a_out_2"][0], f["w_b_out_2"][0], f["w_c_out_2"][0]], axis=0)
    cmp_u = lambda w: w.reshape(2, 16, P, 256).transpose(0, 2, 1, 3).reshape(2, P, UNIT)
    glu = f["ssm_w_glu"][0].reshape(8, P, 2, 512).transpose(2, 1, 0, 3).reshape(2, P, UNIT)
    wst = np.concatenate([
        units_a(f["w_ada"][0]), units_a(w_in[:, 0:3584]), cmp_u(f["cmp_w1_k"][0]), cmp_u(f["cmp_w1_v"][0]), glu,
        units_a(f["w_out"][0]), units_a(f["peer_w_q"][0]),
        units_a(w_u[:, 0:8192]), units_b(w_v[0:8192]), units_a(w_u[:, 8192:]), units_b(w_v[8192:]),
        units_a(z), units_a(f["w_gate_2"][0]), units_a(abc), units_a(f["w_o_2"][0]),
        units_a(f["w_up_2"][0]), units_b(f["w_down_2"][0])], axis=0)
    rcnt = np.zeros((4, 16), np.float32)
    for g in range(4):
        rcnt[g] = 1 / np.minimum(np.arange(16) + 1, 2 << g).astype(np.float32)
    table = {
        "c": cols(f["c"][0]), "b_ada": cols(f["b_ada"][0]), "norm1_g": cols(f["norm1_g"][0]),
        "norm2_g": cols(f["norm2_g"][0]), "final_g": cols(f["final_g"]), "g_mix": cols(f["g_mix_2"][0]),
        "g_mlp": cols(f["g_mlp_2"][0]), "g_final": cols(f["g_final_2"]),
        "beta": np.concatenate([cols(f["beta_ssm"][0]), cols(f["beta_attn"][0])], axis=1),
        "lam_re": cols(f["ssm_lam_re"][0]), "lam_im": cols(f["ssm_lam_im"][0]),
        "log_dt": cols(np.repeat(f["ssm_log_dt"][0], 64)), "d_skip": cols(f["ssm_d"][0]),
        "b_glu": cols(f["ssm_b_glu"][0]), "b_gate": cols(f["b_gate_2"][0]), "b_glu2": cols(f["b_glu_2"][0]),
        "w_dw_a": f["w_dw_a_2"][0].reshape(31, 6, P).transpose(2, 1, 0).reshape(P, 186),
        "b_dw_a": cols(f["b_dw_a_2"][0]), "ln_g": cols(f["ln_g_a_2"][0]), "ln_b": cols(f["ln_b_a_2"][0]),
        "pool_scale": cols(f["pool_scale_2"][0]),
        "w_dw_c": f["w_dw_c_2"][0].reshape(3, 6, P).transpose(2, 1, 0).reshape(P, 18),
        "pool_rcnt": np.tile(rcnt.reshape(1, 64), (P, 1)),
    }
    cst = np.concatenate([table[n] for n, _ in CONST], axis=1)
    gcols = w_in[:, 3584:3608].reshape(D, 3, HEADS)[:, [1, 2, 0], :].transpose(0, 2, 1).reshape(D, 24)
    half = lambda w: w.reshape(2, P, P).transpose(1, 0, 2).reshape(P, 256)
    dyn1 = np.concatenate([gcols.reshape(KT, P, 24).transpose(1, 0, 2).reshape(P, 384),
                           half(f["cmp_w2_k"][0]), half(f["cmp_w2_v"][0]),
                           f["cmp_pe_k"][0].T, f["cmp_pe_v"][0].T], axis=1)
    dyn2 = np.concatenate([f["peer_k1"][0].T, f["peer_k2"][0].T], axis=1)
    dyn3 = f["w_pool_grp_2"][0].transpose(1, 0, 2).reshape(P, 512)
    rel = np.concatenate([f["rel_bias"], np.full((1, HEADS), NEG, np.float32)], axis=0)
    onehot = np.concatenate([bucket_onehot(), rel], axis=1)
    bm = np.zeros((2, 8, 4, 2, 16, 2, 64), np.float32)
    cm = np.zeros((2, 32, 2, 64, 2, 16), np.float32)
    for r, n in enumerate(("re", "im")):
        b = f["ssm_b_" + n][0].reshape(8, 4, 2, 64, 16).transpose(0, 1, 2, 4, 3)
        c = f["ssm_c_" + n][0].reshape(32, 2, 16, 64).transpose(0, 1, 3, 2)
        for g in range(2):
            bm[r, :, :, g, :, g, :] = b[:, :, g]
            cm[r, :, g, :, g, :] = c[:, g]
    bmat = bm.reshape(2, 8, P, P).transpose(2, 1, 0, 3)
    cmat = cm.reshape(2, 32, P, 32).transpose(2, 0, 1, 3)
    xT = f["x"][0].T.reshape(KT, P, T).transpose(1, 0, 2)
    arrays = {"xT": xT, "wst": wst, "cst": cst, "dyn1": dyn1, "dyn2": dyn2, "dyn3": dyn3, "onehot": onehot,
              "bmat": bmat, "cmat": cmat}
    return {k + "_dram": np.ascontiguousarray(v) for k, v in arrays.items()}


def kernel(**inputs):
    import concourse.bacc as bacc
    from concourse.bass_utils import run_bass_kernel_spmd

    arrays = layout(inputs)
    nc = bacc.Bacc("TRN2", target_bir_lowering=False, num_devices=1)
    aps = [nc.dram_tensor(k, a.shape, mybir.dt.from_np(a.dtype), kind="ExternalInput").ap() for k, a in arrays.items()]
    skew = nc.dram_tensor("bias_rows", (HEADS, P, SKEW_W), F32, kind="Internal").ap()
    out = nc.dram_tensor("out_dram", (P, KT, T), F32, kind="ExternalOutput").ap()
    program(nc, *aps, skew, out)
    r = run_bass_kernel_spmd(nc, [arrays], core_ids=[0])
    y = np.asarray(r.results[0]["out_dram"])
    return np.ascontiguousarray(y.transpose(1, 0, 2).reshape(D, T).T)[None]
```

```python
from contextlib import ExitStack, contextmanager
import math

import numpy as np

import concourse.bass as bass
from concourse import mybir

F32 = mybir.dt.float32
F16 = mybir.dt.float16
U32 = mybir.dt.uint32
ALU = mybir.AluOpType
ACT = mybir.ActivationFunctionType
AX_X = mybir.AxisListType.X

P = 128
T = 256
D = 2048
KT = D // P
UNIT = 4096
RING = 4
RAW = 2
ADA_DVE = 12
WSCALE = 256.0
HSCALE = 1 / 8
NSTATE_T = 32
N_CMP = 15
HEADS = 8
NEG = -1e30
EPS = 1e-6
SCALE = 128 ** -0.5
EXP_T = 64
TOPK = 16
SSM_RATE = 1.7
HOT_POOL = 4
SELECT_PIECES = 13

STREAM = [("ada", 48), ("w_in", 14), ("cmp", 4), ("glu", 2), ("w_out", 8), ("peer_q", 8),
          ("u0", 32), ("v0", 32), ("u1", 32), ("v1", 32),
          ("z", 17), ("gate", 24), ("abc", 8), ("w_o", 8), ("up", 32), ("down", 32)]
FIRST = {}
N_UNITS = 0
for _name, _n in STREAM:
    FIRST[_name] = N_UNITS
    N_UNITS += _n

SPLIT_0 = FIRST["peer_q"]



def slot_of(u):
    if u < SPLIT_0:
        return u % RING, u // RING + 1
    return u % RAW, SPLIT_0 // RING + (u - SPLIT_0) // RAW + 1


def per_turn(u):
    return 1 if u < SPLIT_0 else 2


def split_rank(u):
    return u - SPLIT_0 if u >= SPLIT_0 else None


CONST = [("c", 16), ("b_ada", 96), ("norm1_g", 16), ("norm2_g", 16), ("final_g", 16), ("g_mix", 16),
         ("g_mlp", 16), ("g_final", 16), ("beta", 16), ("lam_re", 32), ("lam_im", 32), ("log_dt", 32),
         ("d_skip", 8), ("b_glu", 8), ("b_gate", 48), ("b_glu2", 12), ("w_dw_a", 186), ("b_dw_a", 6),
         ("ln_g", 6), ("ln_b", 6), ("pool_scale", 4), ("w_dw_c", 18), ("pool_rcnt", 64)]
COL = {}
N_CONST = 0
for _name, _n in CONST:
    COL[_name] = N_CONST
    N_CONST += _n

SKEW_W = 384
ASC_0 = 255
ASC_W = 480

STATS = [16, 8, 8, 16, 16, 16, 6, 16, 16]
CHUNK = 4


def chunks_of(n):
    return [(a, min(CHUNK, n - a)) for a in range(0, n, CHUNK)]


STAT_CHUNK0 = [sum(len(chunks_of(m)) for m in STATS[:q]) for q in range(len(STATS))]


def early_schedule():
    out, x, y = [], 0, 0

    def ssm(upto):
        nonlocal x, y
        while x < min(upto, NSTATE_T):
            out.append(("x", x))
            x += 1
            if x - y > 3:
                out.append(("y", y))
                y += 1
    for v in range(4, 14):
        out.append(("half", v))
        ssm(round(SSM_RATE * (2 * (v - 4) + 1)))
        out.append(("unit", v))
        ssm(round(SSM_RATE * (2 * (v - 4) + 2)))
    ssm(NSTATE_T)
    out.append(("gates", 0))
    out += [("y", n) for n in range(y, NSTATE_T)]
    return out + [("cmp", v) for v in range(4)]


class Chain:

    def __init__(self, eng, sem):
        self.eng, self.sem, self.n, self.i, self.per = eng, sem, 0, None, 0

    def put(self, ins):
        ins.then_inc(self.sem, 1)
        self.n += 1
        return self.value()

    def value(self):
        return self.n if self.i is None else self.i * self.per + self.n

    def wait(self, back=0):
        self.eng.wait_ge(self.sem, self.value() - back)

    @contextmanager
    def loop(self, times, per, first=0):
        with self.eng.Fori(first, first + times) as i:
            n0, self.i, self.per = self.n, i, per
            self.n -= first * per
            yield i
            assert self.n - n0 + first * per == per, (self.n - n0, per)
        self.i = None
        self.n = n0 + per * times


def program(nc, xT_d, wst, cst_d, dyn1_d, dyn2_d, dyn3_d, onehot_d, bmat_d, cmat_d, skew_d, out_d):
    ctx = ExitStack()
    with ctx:
        def sb(name, cols, dt=F32):
            return ctx.enter_context(nc.sbuf_tensor(name, [P, cols], dt))

        def sem(name):
            return ctx.enter_context(nc.semaphore(name))

        ring = sb("ring", RING * UNIT)
        A = sb("arena", 64 * T)
        X = sb("x_res", KT * T)
        H = sb("h_act", KT * T)
        J = sb("proj", 28 * T)
        W = sb("work", 8 * T)
        cst = sb("cst", N_CONST)
        dyn = sb("dyn", 960)
        mod = sb("mod", 96)
        csilu = sb("csilu", KT)
        affine = sb("affine", KT)
        rs = sb("rs", T)
        mag = sb("mag", NSTATE_T)
        small = sb("small", 64)
        ident = sb("ident", P)
        ones = sb("ones", P)
        psW = ctx.enter_context(nc.psum_tensor("psW", [P, 4, 512], F32))
        psM = ctx.enter_context(nc.psum_tensor("psM", [P, 4, 512], F32))

        def const(name, a=0, n=1):
            return cst[:, COL[name] + a:COL[name] + a + n]

        def tiles(buf, a, n=1):
            return buf[:, a * T:(a + n) * T]

        def halves(buf, k):
            b = buf[:, k * T:(k + 1) * T].bitcast(F16)
            return b[:, 0:T], b[:, T:2 * T]

        whi = ring[:, 2 * UNIT:3 * UNIT].bitcast(F16)
        wlo = ring[:, 3 * UNIT:4 * UNIT].bitcast(F16)

        tab = A[:, :].rearrange("p (i r t) -> p i r t", i=NSTATE_T, r=2)
        cmat = X[:, 0:2048].rearrange("p (r i c) -> p r i c", r=2, i=NSTATE_T)
        scanb = X[:, 2048:3072].rearrange("p (b r t) -> p b r t", b=2, r=2)
        bmat = X[:, 3072:4096].rearrange("p (s r n) -> p s r n", s=4, r=2)
        onehot = J[0:33, 0:SKEW_W + ASC_W + HEADS]
        skew_sb = J[:, 1024:1024 + HEADS * SKEW_W]
        blk = H[:, 0:1920].rearrange("p (v o n) -> p v o n", v=2, o=32)
        cmp_hid = H[:, 1920:2040].rearrange("p (v m n) -> p v m n", v=2, m=2)
        bias = H[:, 2048:4096].rearrange("p (h s) -> p h s", h=HEADS)
        gate_w = dyn[:, 0:384].rearrange("p (k n) -> p k n", k=KT)
        kc = dyn[:, 0:30]
        vc = dyn[0:N_CMP, 32:32 + 256].rearrange("p (g d) -> p g d", g=2)
        w2 = dyn[:, 384:896].rearrange("p (v m d) -> p v m d", v=2, m=2)
        pe = dyn[:, 896:960].rearrange("p (v o) -> p v o", v=2)
        keys = dyn[:, 0:256].rearrange("p (f n) -> p f n", f=2)
        pool_w = dyn[:, 0:512].rearrange("p (g n) -> p g n", g=4)
        vnat = A[:, 0:1024].rearrange("p (b g s d) -> p b g s d", b=2, g=2, s=2)
        LW = 528
        logit = [A[:, 1024 + LW * i:1024 + LW * (i + 1)] for i in range(3)]
        probT = [A[:, 2816 + 640 * i:2816 + 640 * (i + 1)] for i in range(2)]
        acts16 = A[:, :].bitcast(F16).rearrange("p (e t r) -> p r e t", e=EXP_T, r=2)
        ada_acc = J[:, 5120:6144].rearrange("p (b a n) -> p b a n", b=2, a=2)
        glu_s = A[:, 8192:8192 + 8 * T]
        mxb = small[:, 0:9].rearrange("p (b c) -> p b c", b=3)
        smb = small[:, 9:18].rearrange("p (b c) -> p b c", b=3)
        gates = sb("gates", 48)[:, :].rearrange("p (q h c) -> p q h c", q=2, h=HEADS)
        cvalid = sb("cvalid", 30)[:, :].rearrange("p (q n) -> p q n", q=2)
        cbias = sb("cbias", 240)[:, :].rearrange("p (q n h) -> p q n h", q=2, n=N_CMP)
        cand = J[:, 0:2048].rearrange("p (h a b) -> p h a b", h=HEADS, a=TOPK)
        sel = J[:, 2048:4096]
        val = sel[:, 0:256].rearrange("p (h f k) -> p h f k", h=HEADS, f=2)
        idx = sel[:, 256:512].bitcast(U32).rearrange("p (h f k) -> p h f k", h=HEADS, f=2)
        idxf = sel[:, 512:768].rearrange("p (h f k) -> p h f k", h=HEADS, f=2)
        cval = sel[:, 768:896].rearrange("p (h k) -> p h k", h=HEADS)
        cidx = sel[:, 896:1024].bitcast(U32)
        part = sel[:, 1024:1280].bitcast(U32).rearrange("p (f n) -> p f n", f=2)
        partf = sel[:, 1280:1536].rearrange("p (f h k) -> p f h k", f=2, h=HEADS)
        pick = sel[:, 1536:1920].rearrange("p (f n) -> p f n", f=3)
        gsum = sel[:, 1920:1928]
        pickT = W[:, 1024:1792].rearrange("p (f t) -> p f t", f=3)
        hot2 = [J[:, 4096 + 1024 * b:4096 + 1024 * (b + 1)].rearrange("p (t e) -> p t e", t=8) for b in range(2)]
        hot1 = [J[:, 6144 + 512 * b:6144 + 512 * (b + 1)].rearrange("p (t e) -> p t e", t=8) for b in range(2)]
        iota = sb("iota", P)
        diag = iota

        def key_scores(c):
            buf = J[:, 4096 + 512 * c:4096 + 512 * (c + 1)] if c < 6 else W[:, 512 * (c - 6):512 * (c - 5)]
            return buf.rearrange("p (s n) -> p s n", s=4)

        cst_in, dyn_in, x_in, onehot_in = sem("cst_in"), sem("dyn_in"), sem("x_in"), sem("onehot_in")
        cmat_in, skew_out, skew_in, y_out = sem("cmat_in"), sem("skew_out"), sem("skew_in"), sem("y_out")
        bmat_in = [sem(f"bmat_in{i}") for i in range(4)]
        slot_full = [sem(f"slot_full{i}") for i in range(RING)]
        hi_done, split_done, ada_sum, tab_ready = sem("hi_done"), sem("split_done"), sem("ada_sum"), sem("tab_ready")
        route_hi = sem("route_hi")
        va_split, pool_split = sem("va_split"), sem("pool_split")
        t_raw, t_hi, acts_ready = sem("t_raw"), sem("t_hi"), sem("acts_ready")
        w_used, bank_free = sem("w_used"), sem("bank_free")
        pool_const = sem("pool_const")
        dve_seq, act_seq, pool_seq = sem("dve_seq"), sem("act_seq"), sem("pool_seq")
        stat_sq, stat_used, stat_ms, stat_rs = sem("stat_sq"), sem("stat_used"), sem("stat_ms"), sem("stat_rs")
        c_ready, act_trig, dve_trig = sem("c_ready"), sem("act_trig"), sem("dve_trig")
        h_ready, h_raw, cmat_ready = sem("h_ready"), sem("h_raw"), sem("cmat_ready")
        bias_ps, bias_sb, cbias_sb = sem("bias_ps"), sem("bias_sb"), sem("cbias_sb")
        x_ps, x_read, scan_out, rotated, scan_free = sem("x_ps"), sem("x_read"), sem("scan_out"), sem("rotated"), sem("scan_free")
        diag_ready, z_ready, gates_ps, gates_sb = sem("diag_ready"), sem("z_ready"), sem("gates_ps"), sem("gates_sb")
        blk_ready, cmp_hid_sb, cmp_ps, cmp_sb = sem("blk_ready"), sem("cmp_hid_sb"), sem("cmp_ps"), sem("cmp_sb")
        glu_sb, mix_ready = sem("glu_sb"), sem("mix_ready")
        v_ps, v_sb = sem("v_ps"), sem("v_sb")
        score_ps, logit_sb, negmax, exp_sb, prob_sb = sem("score_ps"), sem("logit_sb"), sem("negmax"), sem("exp_sb"), sem("prob_sb")
        probT_ps, probT_sb, att_ps, att_sb = sem("probT_ps"), sem("probT_sb"), sem("att_ps"), sem("att_sb")
        key_ps, key_sb, topv, gexp, picked, pickT_ps, pickT_sb = (
            sem("key_ps"), sem("key_sb"), sem("topv"), sem("gexp"), sem("picked"), sem("pickT_ps"), sem("pickT_sb"))
        hot2_ready, hot1_ready, hot_used, route_used = sem("hot2_ready"), sem("hot1_ready"), sem("hot_used"), sem("route_used")
        z_all, pooled, pool_ps, pool_sb = sem("z_all"), sem("pooled"), sem("pool_ps"), sem("pool_sb")
        conv_done, ln_ps, ln_mu, ln_x, va_ready, yc_ready = (
            sem("conv_done"), sem("ln_ps"), sem("ln_mu"), sem("ln_x"), sem("va_ready"), sem("yc_ready"))
        pool_tick = sem("pool_tick")
        iota_ready = sem("iota_ready")
        merged, out_ready, relu_sb = sem("merged"), sem("out_ready"), sem("relu_sb")

        block = ctx.enter_context(nc.Block())

        @block.sync
        def _(sp):
            def load(u, slot):
                sp.dma_start(ring[:, slot * UNIT:(slot + 1) * UNIT], wst[u, :, :]).then_inc(slot_full[slot], 16)

            for u in range(RING):
                load(u, u)
            with sp.Fori(1, SPLIT_0 // RING) as i:
                for s in range(RING):
                    sp.wait_ge(w_used, i * RING + (s + 1 - RING))
                    sp.dma_start(ring[:, s * UNIT:(s + 1) * UNIT],
                                 wst[bass.ds(i * RING + s, 1), :, :].rearrange("o p n -> (o p) n"))\
                      .then_inc(slot_full[s], 16)

            def loads(a, b, free, less):
                if a % 2:
                    sp.wait_ge(free, a - less)
                    load(a, 1)
                    a += 1
                with sp.Fori(a // 2, b // 2) as i:
                    for s in range(2):
                        sp.wait_ge(free, i * 2 + (s - less))
                        sp.dma_start(ring[:, s * UNIT:(s + 1) * UNIT],
                                     wst[bass.ds(i * 2 + s, 1), :, :].rearrange("o p n -> (o p) n"))\
                          .then_inc(slot_full[s], 16)
                if b % 2:
                    sp.wait_ge(free, b - 1 - less)
                    load(b - 1, 0)

            for u in range(2):
                sp.wait_ge(w_used, SPLIT_0 + u - RING + 1)
                load(SPLIT_0 + u, u)
            loads(SPLIT_0 + 2, N_UNITS, split_done, SPLIT_0 + 1)
            sp.wait_ge(out_ready, 1)
            sp.dma_start(out_d.rearrange("p k t -> p (k t)"), X[:, :]).then_inc(y_out, 16)
            sp.wait_ge(y_out, 16)

        @block.tensor
        def _(pe_):
            def slot_ready(u0, j, i):
                if split_rank(u0) is not None:
                    pe_.wait_ge(split_done, i * 4 + (split_rank(u0) + j + 1))
                    return (u0 + j) % RAW
                s, n = slot_of(u0 + j)
                pe_.wait_ge(slot_full[s], i * 16 * per_turn(u0) + 16 * n)
                return s

            def stage(name, emit, n=None, first=0, lead=1, drained=True):
                u0 = FIRST[name] + first
                n = n if n is not None else dict(STREAM)[name] - first
                if drained:
                    pe_.wait_ge(bank_free, u0 + 4)

                def body(i, js):
                    for j in js:
                        s = slot_ready(u0, j, i)
                        if lead != 2 or j % 2 == 0:
                            pe_.wait_ge(bank_free, i * 4 + (u0 + j + lead))
                        emit(s, j).then_inc(w_used, 1)

                turns = n // 4
                if turns > 1:
                    with pe_.Fori(0, turns) as i:
                        body(i, range(4))
                elif turns:
                    body(0, range(4))
                if n % 4:
                    body(turns, range(n % 4))

            def product(out, s, col, rhs, first, last):
                w0 = s * UNIT + col
                if not isinstance(rhs, tuple):
                    return nc.tensor.matmul(out, ring[:, w0:w0 + P], rhs, start=first, stop=last)
                xh, xl = rhs
                nc.tensor.matmul(out, whi[:, w0:w0 + P], xh, start=first, stop=False)
                nc.tensor.matmul(out, whi[:, w0:w0 + P], xl, start=False, stop=False)
                return nc.tensor.matmul(out, wlo[:, w0:w0 + P], xh, start=False, stop=last)

            def unit_a(s, bank, rhs, ms=(0, 1)):
                for m in ms:
                    for k in range(KT):
                        mm = product(psW[:, bank, m * T:(m + 1) * T], s, k * 256 + m * P, rhs(k), k == 0, k == KT - 1)
                return mm

            def unit_b(s, j, rhs):
                for k in range(32):
                    mm = product(psW[:, j // 2, 0:T], s, k * P, rhs(32 * (j % 2) + k),
                                 j % 2 == 0 and k == 0, j % 2 == 1 and k == 31)
                return mm

            def stat_sum(q):
                n = STATS[q]
                if q:
                    pe_.wait_ge(stat_ms, q)
                for ci, (a, m) in enumerate(chunks_of(n)):
                    g = STAT_CHUNK0[q] + ci
                    pe_.wait_ge(stat_sq, g + 1)
                    for k in range(m):
                        mm = nc.tensor.matmul(psM[:, 3, 0:T], ones[:, :], tiles(W, CHUNK * (ci % 2) + k),
                                              start=(a + k == 0), stop=(a + k == n - 1))
                    mm.then_inc(stat_used, 1)

            def ada(a, b):
                with pe_.Fori(a, b) as i:
                    for j in range(4):
                        pe_.wait_ge(ada_sum, i * 4 + (j + 1))
                        pe_.wait_ge(bank_free, i * 4 + (j + 1))
                        for m in range(2):
                            o = psW[:, j, m:m + 1]
                            for k in range(ADA_DVE, KT):
                                c0 = j * UNIT + k * 256 + m * P
                                nc.tensor.matmul(o, ring[:, c0:c0 + P], csilu[:, k:k + 1], start=(k == ADA_DVE), stop=False)
                            for a_ in range(2):
                                mm = nc.tensor.matmul(o, ada_acc[:, j % 2, a_, m * P:(m + 1) * P], ones[:, 0:1],
                                                      start=False, stop=(a_ == 1))
                        mm.then_inc(w_used, 1)

            pe_.wait_ge(c_ready, 1)
            pe_.wait_ge(pool_const, 4)
            ada(0, 2)
            pe_.wait_ge(onehot_in, 16)
            table = onehot[:, SKEW_W + ASC_W:SKEW_W + ASC_W + HEADS]
            for h in range(HEADS):
                if h >= 4:
                    pe_.wait_ge(bias_sb, h - 3)
                nc.tensor.matmul(psM[:, h % 4, 0:SKEW_W], table[:, h:h + 1].to_broadcast([33, P]),
                                 onehot[:, 0:SKEW_W], start=True, stop=True).then_inc(bias_ps, 1)
            pe_.wait_ge(bank_free, 8 + 4)
            for qb in range(2):
                for n in range(N_CMP):
                    a = SKEW_W + ASC_0 + qb * P - 16 * n - 31
                    mm = nc.tensor.matmul(psW[:, 0, (qb * N_CMP + n) * 8:(qb * N_CMP + n) * 8 + 8],
                                          onehot[:, a:a + P], table, start=True, stop=True)
            mm.then_inc(bias_ps, 1)
            pe_.wait_ge(bias_sb, HEADS)
            pe_.wait_ge(cbias_sb, 1)

            ada(2, 3)
            stat_sum(0)
            ada(3, FIRST["w_in"] // 4)
            pe_.wait_ge(h_ready, 1)
            h_rhs = lambda k: tiles(H, k)
            h_split = lambda k: halves(H, k)
            stage("w_in", lambda s, j: unit_a(s, j, h_rhs), n=4)

            pe_.wait_ge(bank_free, FIRST["w_in"] + 8)
            pe_.wait_ge(cmat_ready, 1)
            pe_.wait_ge(dyn_in, 16)
            for what, v in early_schedule():
                if what in ("half", "unit"):
                    u = FIRST["w_in"] + v
                    s = slot_of(u)[0]
                    if what == "half":
                        slot_ready(u, 0, 0)
                        pe_.wait_ge(bank_free, u + 1)
                        unit_a(s, v % 4, h_rhs, (0,))
                    else:
                        unit_a(s, v % 4, h_rhs, (1,)).then_inc(w_used, 1)
                elif what == "x":
                    ct, j = v // 4, v % 4
                    if j == 0:
                        pe_.wait_ge(bmat_in[ct % 4], 16 * (ct // 4 + 1))
                    if v >= 2:
                        pe_.wait_ge(x_read, v - 1)
                    for r in range(2):
                        mm = nc.tensor.matmul(psM[:, v % 2, r * T:(r + 1) * T],
                                              bmat[32 * j:32 * j + 32, ct % 4, r, :],
                                              J[32 * j:32 * j + 32, ct * T:(ct + 1) * T], start=True, stop=True)
                    mm.then_inc(x_ps, 1)
                elif what == "y":
                    ct, j = v // 4, v % 4
                    if j == 0:
                        pe_.wait_ge(diag_ready, ct + 1)
                        pe_.wait_ge(z_ready, ct) if ct else None
                        nc.tensor.matmul(psM[:, 2, 0:T], diag[:, :], tiles(J, ct), start=True, stop=False)
                    pe_.wait_ge(rotated, v + 1)
                    for r in range(2):
                        mm = nc.tensor.matmul(psM[32 * j:32 * j + 32, 2, 0:T], cmat[:, r, v, :], scanb[:, v % 2, r, :],
                                              start=False, stop=(r == 1))
                    mm.then_inc(scan_free, 1)
                elif what == "gates":
                    for qb in range(2):
                        for k in range(KT):
                            mm = nc.tensor.matmul(psM[:, 3, qb * 24:qb * 24 + 24],
                                                  H[:, k * T + qb * P:k * T + (qb + 1) * P], gate_w[:, k, :],
                                                  start=(k == 0), stop=(k == KT - 1))
                    mm.then_inc(gates_ps, 1)
                elif what == "cmp":
                    u = FIRST["cmp"] + v
                    if v == 0:
                        pe_.wait_ge(bank_free, u + 4)
                        pe_.wait_ge(blk_ready, 1)
                    s = slot_ready(u, 0, 0)
                    kv, part_ = v // 2, v % 2
                    for m in range(2):
                        for o in range(16):
                            mm = nc.tensor.matmul(psW[:, 2 * kv + m, 0:30],
                                                  ring[:, s * UNIT + o * 256 + m * P:s * UNIT + o * 256 + (m + 1) * P],
                                                  blk[:, kv, 16 * part_ + o, :],
                                                  start=(part_ == 0 and o == 0), stop=(part_ == 1 and o == 15))
                    mm.then_inc(w_used, 1)
            pe_.wait_ge(cmp_hid_sb, 2)
            pe_.wait_ge(gates_sb, 1)
            for m in range(2):
                nc.tensor.matmul(psM[:, 3, 0:30], w2[:, 0, m, :], cmp_hid[:, 0, m, :], start=(m == 0), stop=(m == 1))
            for g in range(2):
                for m in range(2):
                    mm = nc.tensor.matmul(psM[0:N_CMP, 3, 128 + 128 * g:256 + 128 * g], cmp_hid[:, 1, m, 15 * g:15 * g + 15],
                                          w2[:, 1, m, :], start=(m == 0), stop=(m == 1))
            mm.then_inc(cmp_ps, 1)

            pe_.wait_ge(z_ready, 8)

            def glu(s, j):
                for m in range(4):
                    for k in range(8):
                        mm = nc.tensor.matmul(psW[:, 2 * j + m // 2, (m % 2) * T:(m % 2 + 1) * T],
                                              ring[:, s * UNIT + k * 512 + m * P:s * UNIT + k * 512 + (m + 1) * P],
                                              tiles(J, k), start=(k == 0), stop=(k == 7))
                return mm
            stage("glu", glu)
            pe_.wait_ge(cmp_sb, 2)
            stat_sum(1)
            pe_.wait_ge(bank_free, FIRST["w_out"] + 4)
            for b in range(2):
                for g in range(2):
                    for s2 in range(2):
                        tile = 16 + 4 * (b + 1) + 2 + g
                        mm = nc.tensor.transpose(psW[:, b, (2 * g + s2) * P:(2 * g + s2 + 1) * P],
                                                 J[:, tile * T + s2 * P:tile * T + (s2 + 1) * P], ident[:, :])
                mm.then_inc(v_ps, 1)
            pe_.wait_ge(v_sb, 2)

            def scores(r):
                h, qb = r // 2, r % 2
                g, nk = h // 4, P * (qb + 1)
                q = J[:, (8 + h) * T + qb * P:(8 + h) * T + (qb + 1) * P]
                if r >= 2:
                    pe_.wait_ge(logit_sb, r - 1)
                for b in range(2):
                    kt = 16 + 4 * (b + 1) + g
                    nc.tensor.matmul(psW[:, r % 2, b * 256:b * 256 + nk], q, J[:, kt * T:kt * T + nk],
                                     start=True, stop=True)
                nc.tensor.matmul(psM[:, r % 2, 0:N_CMP], q, kc[:, 15 * g:15 * g + 15],
                                 start=True, stop=True).then_inc(score_ps, 1)

            def prob_turn(r):
                h, qb = r // 2, r % 2
                pe_.wait_ge(prob_sb, r + 1)
                if r >= 1:
                    pe_.wait_ge(probT_sb, 2 * r)
                for b in range(2):
                    for s2 in range(qb + 1):
                        nc.tensor.transpose(psW[:, 2, (2 * b + s2) * P:(2 * b + s2 + 1) * P],
                                            logit[r % 3][:, b * 256 + s2 * P:b * 256 + (s2 + 1) * P], ident[:, :])
                nc.tensor.transpose(psM[0:N_CMP, 2, 0:P], logit[r % 3][:, 512:512 + N_CMP], ident[:, :])\
                    .then_inc(probT_ps, 1)

            def att_out(r):
                h, qb = r // 2, r % 2
                g = h // 4
                pe_.wait_ge(probT_sb, 2 * (r + 1))
                if r >= 1:
                    pe_.wait_ge(att_sb, r)
                first = True
                for b in range(2):
                    for s2 in range(qb + 1):
                        nc.tensor.matmul(psW[:, 3, 0:P], vnat[:, b, g, s2, :],
                                         probT[r % 2][:, (2 * b + s2) * P:(2 * b + s2 + 1) * P], start=first, stop=False)
                        first = False
                nc.tensor.matmul(psW[:, 3, 0:P], vc[:, g, :], probT[r % 2][0:N_CMP, 512:512 + P],
                                 start=False, stop=True).then_inc(att_ps, 1)

            pe_.wait_ge(skew_in, 16)
            for r in range(16 + 3):
                if r < 16:
                    scores(r)
                if 2 <= r <= 17:
                    prob_turn(r - 2)
                if r >= 3:
                    att_out(r - 3)
            stat_sum(2)
            pe_.wait_ge(mix_ready, 2)
            stage("w_out", lambda s, j: unit_a(s, j, lambda k: tiles(J, k)))
            stat_sum(3)
            pe_.wait_ge(h_ready, 2)
            stage("peer_q", lambda s, j: unit_a(s, j, h_split))
            pe_.wait_ge(bank_free, FIRST["u0"] + 4)
            pe_.wait_ge(dyn_in, 32)
            for c in range(8):
                qb = c // 4
                if c >= 2:
                    pe_.wait_ge(key_sb, c - 1)
                for s4 in range(4):
                    t = 2 * (2 * (c % 4) + s4 // 2) + s4 % 2
                    mm = nc.tensor.matmul(psM[:, c % 2, s4 * P:(s4 + 1) * P], J[:, t * T + qb * P:t * T + (qb + 1) * P],
                                          keys[:, s4 % 2, :], start=True, stop=True)
                mm.then_inc(key_ps, 1)

            def turn_picks(qb):
                pe_.wait_ge(picked, qb + 1)
                if qb:
                    pe_.wait_ge(pickT_sb, 1)
                for f in range(3):
                    mm = nc.tensor.transpose(psM[:, 2, f * P:(f + 1) * P], pick[:, f, :], ident[:, :])
                mm.then_inc(pickT_ps, 1)

            from_h = lambda s, j: unit_a(s, j, h_split)
            for half in range(2):
                if half == 0:
                    stage("u0", from_h, n=16)
                    turn_picks(0)
                    stage("u0", from_h, first=16, n=12, drained=False)
                    turn_picks(1)
                    stage("u0", from_h, first=28, n=4, drained=False)
                else:
                    stage("u1", from_h)
                pe_.wait_ge(bank_free, FIRST[f"v{half}"] + 4)
                with pe_.Fori(0, 16) as i:
                    for b in range(2):
                        n = i * 2 + (32 * half + b + 1)
                        pe_.wait_ge(hot2_ready, n)
                        pe_.wait_ge(hot1_ready, n)
                        pe_.wait_ge(route_used, n)
                        for t in range(8):
                            mm = nc.tensor.matmul(psM[:, b, t * 64:(t + 1) * 64], hot2[b][:, t, :], hot1[b][:, t, :],
                                                  start=True, stop=True)
                        mm.then_inc(hot_used, 1)
                pe_.wait_ge(route_used, 32 * (half + 1) + 2)
                pe_.wait_ge(acts_ready, 32 * (half + 1))
                stage(f"v{half}", lambda s, j: unit_b(s, j, lambda k: (acts16[:, 0, k, :], acts16[:, 1, k, :])), lead=2)
            stat_sum(4)
            stat_sum(5)
            pe_.wait_ge(h_ready, 3)
            stage("z", from_h)
            stage("gate", from_h, n=16)
            pe_.wait_ge(dyn_in, 48)
            pe_.wait_ge(pooled, 1)
            for g in range(4):
                mm = nc.tensor.matmul(psM[:, g // 2, (g % 2) * T:(g % 2 + 1) * T], pool_w[:, g, :], tiles(A, 60 + g),
                                      start=True, stop=True)
            mm.then_inc(pool_ps, 1)
            pe_.wait_ge(conv_done, 6)
            pe_.wait_ge(stat_ms, 6)
            for k in range(6):
                mm = nc.tensor.matmul(psM[:, 3, 0:T], ones[:, :], tiles(A, 54 + k), start=(k == 0), stop=(k == 5))
            mm.then_inc(ln_ps, 1)
            stage("gate", from_h, first=16, n=4, drained=False)
            pe_.wait_ge(ln_mu, 1)
            stat_sum(6)
            stage("gate", from_h, first=20, n=4, drained=False)

            pe_.wait_ge(va_split, 1)
            pe_.wait_ge(pool_split, 1)
            pe_.wait_ge(yc_ready, 1)
            mix_rhs = [halves(J, k) for k in (22, 23, 24, 25, 26, 27, 18, 19, 20, 21, 6, 7, 8, 9, 10, 11)]

            def abc(s, j):
                ps = psW if j % 2 == 0 else psM
                for b, (k0, k1) in enumerate(((0, 6), (6, 10), (10, 16))):
                    for m in range(2):
                        for k in range(k0, k1):
                            mm = product(ps[:, b, m * T:(m + 1) * T], s, k * 256 + m * P, mix_rhs[k], k == k0, k == k1 - 1)
                return mm
            stage("abc", abc, lead=3)
            pe_.wait_ge(merged, 1)
            stage("w_o", from_h)
            stat_sum(7)
            pe_.wait_ge(h_ready, 4)
            stage("up", lambda s, j: unit_a(s, j, h_split))
            pe_.wait_ge(relu_sb, 32 + 4)
            stage("down", lambda s, j: unit_b(s, j, lambda k: halves(A, k)), lead=2)
            stat_sum(8)


        @block.vector
        def _(v):
            D = Chain(v, dve_seq)
            tt, ts, stt = v.tensor_tensor, v.tensor_scalar, v.scalar_tensor_tensor

            def low(u, i=0):
                for p2 in range(2):
                    v.wait_ge(hi_done, i * 8 + (2 * split_rank(u) + p2 + 1))
                    c = slice((u % RAW) * UNIT + p2 * (UNIT // 2), (u % RAW) * UNIT + (p2 + 1) * (UNIT // 2))
                    ins = stt(wlo[:, c], ring[:, c], WSCALE, whi[:, c], ALU.mult, ALU.subtract)
                ins.then_inc(split_done, 1)

            def lows(name, put, per=0):
                u0, n = FIRST[name], dict(STREAM)[name]
                last = u0 + n == N_UNITS

                def body(i, last_turn=False):
                    for j in range(4):
                        if put:
                            put(i, j)
                        if not (last_turn and j >= 2):
                            low(u0 + j + 2, i)
                turns = n // 4 - last
                with D.loop(turns, per) as i:
                    body(i)
                if last:
                    body(turns, True)

            def squares(q, src):
                for ci, (a, m) in enumerate(chunks_of(STATS[q])):
                    g = STAT_CHUNK0[q] + ci
                    if g >= 2:
                        v.wait_ge(stat_used, g - 1)
                    tt(tiles(W, CHUNK * (ci % 2), m), src(a, m), src(a, m), ALU.mult).then_inc(stat_sq, 1)

            def inverse_rms(q):
                v.wait_ge(stat_used, STAT_CHUNK0[q] + len(chunks_of(STATS[q])))
                D.put(ts(rs[:, :], psM[:, 3, 0:T], 1.0 / (STATS[q] * P), EPS, ALU.mult, ALU.add))
                D.wait()
                v.reciprocal(rs[:, :], rs[:, :]).then_inc(stat_ms, 1)
                v.wait_ge(stat_rs, q + 1)

            def par(k):
                return J[:, 4096 + 32 * k:4096 + 32 * (k + 1)]
            dt, lrdt, th, rnd, r, co, cos, sin, w_re, w_im, pr, pi, q1, q2, q3, npr, npi = (par(k) for k in range(17))
            lr, li = const("lam_re", 0, 32), const("lam_im", 0, 32)

            def step(ins):
                D.put(ins)
                D.wait()

            v.wait_ge(act_trig, 1)
            tt(lrdt, lr, dt, ALU.mult).then_inc(dve_trig, 1)
            step(tt(th, li, dt, ALU.mult))
            magic = 12582912.0
            c1 = 6.28125
            c2 = float(np.float32(int((2 * math.pi - c1) * 2 ** 20) / 2 ** 20))
            c3 = 2 * math.pi - c1 - c2
            step(ts(rnd, th, 1 / (2 * math.pi), magic, ALU.mult, ALU.add))
            step(ts(rnd, rnd, magic, None, ALU.subtract))
            step(stt(r, rnd, -c1, th, ALU.mult, ALU.add))
            step(stt(r, rnd, -c2, r, ALU.mult, ALU.add))
            step(stt(r, rnd, -c3, r, ALU.mult, ALU.add))
            step(ts(r, r, 3.1415925, -3.1415925, ALU.min, ALU.max))
            step(stt(co, r, -1.0, r, ALU.mult, ALU.max))
            ts(co, co, -1.0, math.pi / 2, ALU.mult, ALU.add).then_inc(dve_trig, 1)
            v.wait_ge(act_trig, 4)
            D.put(tt(q1, mag[:, :], cos, ALU.mult))
            step(tt(q2, mag[:, :], sin, ALU.mult))
            step(ts(q1, q1, 1.0, None, ALU.subtract))
            D.put(tt(w_re, q1, lr, ALU.mult))
            D.put(tt(q3, q2, li, ALU.mult))
            D.put(tt(w_im, q2, lr, ALU.mult))
            step(tt(npr, q1, li, ALU.mult))
            D.put(tt(w_re, w_re, q3, ALU.add))
            step(tt(w_im, w_im, npr, ALU.subtract))
            D.put(tt(q1, lr, lr, ALU.mult))
            step(tt(q2, li, li, ALU.mult))
            step(tt(q1, q1, q2, ALU.add))
            step(v.reciprocal(q1, q1))
            D.put(tt(w_re, w_re, q1, ALU.mult))
            D.put(tt(w_im, w_im, q1, ALU.mult))
            def ada(a_, b_):
                with D.loop(b_ - a_, 4 * (ADA_DVE - 1), a_) as i:
                    for j in range(4):
                        v.wait_ge(slot_full[j], i * 16 + 16)
                        if j >= 2:
                            v.wait_ge(w_used, i * 4 + (j - 1))
                        else:
                            v.wait_ge(bank_free, i * 4 + (j + 3))
                        for k in range(ADA_DVE):
                            row, acc = ring[:, j * UNIT + k * 256:j * UNIT + (k + 1) * 256], ada_acc[:, j % 2, k % 2, :]
                            if k < 2:
                                ins = ts(acc, row, csilu[:, k:k + 1], None, ALU.mult)
                            else:
                                D.wait(1)
                                ins = stt(acc, row, csilu[:, k:k + 1], acc, ALU.mult, ALU.add)
                            D.put(ins) if k < ADA_DVE - 1 else ins.then_inc(ada_sum, 1)

            v.wait_ge(c_ready, 1)
            ada(0, 3)
            v.wait_ge(x_in, 16)
            squares(0, lambda a, m: tiles(X, a, m))
            inverse_rms(0)
            ada(3, FIRST["w_in"] // 4)
            v.wait_ge(tab_ready, 1)
            v.wait_ge(bank_free, FIRST["w_in"] + 4)
            step(tt(mod[:, :], mod[:, :], const("b_ada", 0, 96), ALU.add))
            D.put(ts(mod[:, 80:96], mod[:, 80:96], 1 / WSCALE, None, ALU.mult))
            step(stt(affine[:, :], mod[:, 16:32], 1.0, const("norm1_g", 0, 16), ALU.add, ALU.mult))
            for k in range(KT):
                D.put(stt(tiles(H, k), tiles(X, k), affine[:, k:k + 1], rs[:, :], ALU.mult, ALU.mult))
            for k in range(KT):
                D.wait(KT - 1)
                ins = ts(tiles(H, k), tiles(H, k), mod[:, k:k + 1], None, ALU.add)
                if k < KT - 1:
                    D.put(ins)
                else:
                    ins.then_inc(h_ready, 1)
            v.wait_ge(cmat_in, 16)
            cre, cim = cmat[:, 0, :, :], cmat[:, 1, :, :]
            t_a = X[:, 2048:3072].rearrange("p (i c) -> p i c", i=NSTATE_T)
            t_b = X[:, 3072:4096].rearrange("p (i c) -> p i c", i=NSTATE_T)
            wr = w_re.unsqueeze(2).to_broadcast([P, NSTATE_T, 32])
            wi = w_im.unsqueeze(2).to_broadcast([P, NSTATE_T, 32])
            D.put(tt(t_a, cim, wi, ALU.mult))
            D.put(tt(t_b, cre, wi, ALU.mult))
            D.wait()
            D.put(tt(cre, cre, wr, ALU.mult))
            D.put(tt(cim, cim, wr, ALU.mult))
            D.wait()
            D.put(tt(cre, cre, t_a, ALU.subtract))
            stt(cim, cim, -1.0, t_b, ALU.mult, ALU.subtract).then_inc(cmat_ready, 1)
            v.wait_ge(cmat_ready, 1)

            t1 = W[:, 0:512].rearrange("p (r t) -> p r t", r=2)
            t2 = W[:, 512:1024].rearrange("p (r t) -> p r t", r=2)
            with D.loop(8, 16) as c:
                for j in range(4):
                    v.wait_ge(x_ps, c * 4 + (j + 1))
                    cosv = A[:, bass.ds(c * 2048 + j * 512, T)].unsqueeze(1).to_broadcast([P, 2, T])
                    sinv = A[:, bass.ds(c * 2048 + (j * 512 + T), T)].unsqueeze(1).to_broadcast([P, 2, T])
                    xp = psM[:, j % 2, :].rearrange("p (r t) -> p r t", r=2)
                    D.put(tt(t1, xp, cosv, ALU.mult))
                    tt(t2, xp, sinv, ALU.mult).then_inc(x_read, 1)
                    D.wait()
                    v.wait_ge(x_read, c * 4 + (j + 1))
                    D.put(tt(t1[:, 0, :], t1[:, 0, :], t2[:, 1, :], ALU.add))
                    D.put(tt(t1[:, 1, :], t1[:, 1, :], t2[:, 0, :], ALU.subtract))
                    v.wait_ge(scan_free, c * 4 + (j + 1))
                    m = mag[:, bass.ds(c * 4 + j, 1)].to_broadcast([P, T])
                    D.wait(1)
                    D.put(v.tensor_tensor_scan(out=scanb[:, j % 2, 0, :], data0=m, data1=t1[:, 0, :], initial=0.0,
                                               op0=ALU.mult, op1=ALU.add))
                    D.wait(1)
                    v.tensor_tensor_scan(out=scanb[:, j % 2, 1, :], data0=m, data1=t1[:, 1, :], initial=0.0,
                                         op0=ALU.mult, op1=ALU.add).then_inc(scan_out, 1)
                    v.wait_ge(scan_out, c * 4 + (j + 1))

            v.wait_ge(dyn_in, 16)
            v.wait_ge(gates_ps, 1)
            v.wait_ge(bank_free, FIRST["cmp"] + 4)
            for kv in range(2):
                for o in range(32):
                    src = J[:, (16 + 2 * kv) * T:(18 + 2 * kv) * T].rearrange("p (g n s) -> p g n s", g=2, s=16)
                    src = src[:, :, o // 16:o // 16 + N_CMP, o % 16]
                    ins = ts(blk[:, kv, o, :].rearrange("p (g n) -> p g n", g=2), src, pe[:, kv, o:o + 1], None, ALU.add)
            ins.then_inc(blk_ready, 1)

            v.wait_ge(glu_sb, 8)
            step(tt(J[:, 0:8 * T], J[:, 0:8 * T], glu_s, ALU.mult))
            squares(1, lambda a, m: tiles(J, a, m))
            inverse_rms(1)

            def scale_rms(buf, k0, n, name, g0, signal=None):
                for k in range(n):
                    ins = stt(tiles(buf, k0 + k), tiles(buf, k0 + k), const(name, g0 + k), rs[:, :], ALU.mult, ALU.mult)
                    if k == n - 1 and signal is not None:
                        ins.then_inc(signal, 1)
                    else:
                        D.put(ins)
            scale_rms(J, 0, 8, "beta", 0, mix_ready)

            v.wait_ge(skew_in, 16)
            v.wait_ge(gates_sb, 1)
            v.wait_ge(pool_const, 4)

            def views(r):
                nk = P * (r % 2 + 1)
                two = logit[r % 3][:, 0:512].rearrange("p (b s) -> p b s", b=2)[:, :, 0:nk]
                return nk, two, logit[r % 3][:, 512:512 + N_CMP]

            def logits(r):
                h, qb = r // 2, r % 2
                nk, two, lc = views(r)
                v.wait_ge(score_ps, r + 1)
                if r >= 3:
                    v.wait_ge(probT_ps, r - 2)
                ps = psW[:, r % 2, :].rearrange("p (b s) -> p b s", b=2)[:, :, 0:nk]
                D.put(stt(two, ps, SCALE, bias[:, h:h + 1, 256 - nk:256].to_broadcast([P, 2, nk]), ALU.mult, ALU.add))
                stt(lc, psM[:, r % 2, 0:N_CMP], SCALE, cbias[:, qb, :, h], ALU.mult, ALU.add).then_inc(logit_sb, 1)
                D.wait()
                D.put(v.tensor_reduce(mxb[:, r % 3, 0:2], two, AX_X, ALU.max))
                v.wait_ge(logit_sb, r + 1)
                D.put(v.tensor_reduce(mxb[:, r % 3, 2:3], lc, AX_X, ALU.max))
                D.wait()
                ts(mxb[:, r % 3, :], mxb[:, r % 3, :], -1.0, None, ALU.mult).then_inc(negmax, 1)

            def probs(r):
                h, qb = r // 2, r % 2
                nk, two, lc = views(r)
                v.wait_ge(exp_sb, 3 * (r + 1))
                step(v.reciprocal(smb[:, r % 3, :], smb[:, r % 3, :]))
                step(tt(smb[:, r % 3, :], smb[:, r % 3, :], gates[:, qb, h, :], ALU.mult))
                for b in range(2):
                    D.put(ts(two[:, b, :], two[:, b, :], smb[:, r % 3, b:b + 1], None, ALU.mult))
                stt(lc, lc, smb[:, r % 3, 2:3], cvalid[:, qb, :], ALU.mult, ALU.mult).then_inc(prob_sb, 1)

            for r in range(16 + 1):
                if r < 16:
                    logits(r)
                if r >= 1:
                    probs(r - 1)
            v.wait_ge(att_sb, 16)
            squares(2, lambda a, m: tiles(J, 8 + a, m))
            inverse_rms(2)
            scale_rms(J, 8, 8, "beta", 8, mix_ready)

            def residual_a(name, gain):
                u0, n = FIRST[name], dict(STREAM)[name]
                with v.Fori(0, n // 4) as i:
                    for j in range(4):
                        v.wait_ge(w_used, i * 4 + (u0 + j + 1))
                        for m in range(2):
                            x = X[:, bass.ds(i * 8 * T + (2 * j + m) * T, T)]
                            g = mod[:, bass.ds(i * 8 + (gain + 2 * j + m), 1)]
                            ins = stt(x, psW[:, j, m * T:(m + 1) * T], g, x, ALU.mult, ALU.add)
                        ins.then_inc(bank_free, 1)

            def residual_b(name, gain):
                u0 = FIRST[name]

                def put(i, j):
                    if j % 2:
                        v.wait_ge(w_used, i * 4 + (u0 + j + 1))
                        if isinstance(i, int):
                            x, g0 = tiles(X, 2 * i + j // 2), slice(2 * i + j // 2, 2 * i + j // 2 + 1)
                            g = gain if isinstance(gain, float) else mod[:, gain + g0.start:gain + g0.stop]
                        else:
                            x = X[:, bass.ds(i * 2 * T + (j // 2) * T, T)]
                            g = gain if isinstance(gain, float) else mod[:, bass.ds(i * 2 + (gain + j // 2), 1)]
                        stt(x, psW[:, j // 2, 0:T], g, x, ALU.mult, ALU.add).then_inc(bank_free, 2)
                lows(name, put)

            def norm_split(col, shift, before):
                def lo(k):
                    v.wait_ge(t_hi, before + k + 1)
                    w = tiles(W, k % 8)
                    if shift is None:
                        ins = tt(halves(H, k)[1], w, halves(H, k)[0], ALU.subtract)
                    else:
                        ins = stt(halves(H, k)[1], w, mod[:, shift + k:shift + k + 1], halves(H, k)[0], ALU.add, ALU.subtract)
                    D.put(ins) if k < KT - 1 else ins.then_inc(h_ready, 1)
                for k in range(KT + 3):
                    if k < KT:
                        if k >= 8:
                            D.wait(2)
                        stt(tiles(W, k % 8), tiles(X, k), col(k), rs[:, :], ALU.mult, ALU.mult).then_inc(t_raw, 1)
                    if k >= 3:
                        lo(k - 3)

            v.wait_ge(x_in, 32)
            residual_a("w_out", 32)
            v.wait_ge(bank_free, FIRST["peer_q"] + 4)
            squares(3, lambda a, m: tiles(X, a, m))
            low(SPLIT_0)
            inverse_rms(3)
            step(stt(affine[:, :], mod[:, 64:80], 1.0, const("norm2_g", 0, 16), ALU.add, ALU.mult))
            norm_split(lambda k: affine[:, k:k + 1], 48, 0)
            low(SPLIT_0 + 1)
            lows("peer_q", None)

            io16 = iota[:, 0:16].unsqueeze(1).unsqueeze(1)
            v.wait_ge(iota_ready, 1)
            def select(qb):
                v.wait_ge(key_sb, 8)
                for h in range(HEADS):
                    s4 = key_scores(4 * qb + h // 2)
                    for f in range(2):
                        s = s4[:, (h % 2) * 2 + f, :]
                        step(v.max(val[:, h, f, 0:8], s))
                        step(v.max_index(idx[:, h, f, 0:8], val[:, h, f, 0:8], s))
                        step(v.match_replace(s, val[:, h, f, 0:8], s, -3e38))
                        step(v.max(val[:, h, f, 8:16], s))
                        step(v.max_index(idx[:, h, f, 8:16], val[:, h, f, 8:16], s))
                    yield
                for h in range(HEADS):
                    D.put(tt(cand[:, h, :, :], val[:, h, 0, :].unsqueeze(2).to_broadcast([P, TOPK, TOPK]),
                             val[:, h, 1, :].unsqueeze(1).to_broadcast([P, TOPK, TOPK]), ALU.add))
                D.put(v.tensor_copy(sel[:, 512:768], sel[:, 256:512].bitcast(U32)))
                D.wait()
                for h in range(HEADS):
                    cf = cand[:, h, :, :].rearrange("p a b -> p (a b)")
                    ci = cidx[:, h * TOPK:(h + 1) * TOPK]
                    step(v.max(cval[:, h, 0:8], cf))
                    step(v.max_index(ci[:, 0:8], cval[:, h, 0:8], cf))
                    step(v.match_replace(cf, cval[:, h, 0:8], cf, -3e38))
                    step(v.max(cval[:, h, 8:16], cf))
                    step(v.max_index(ci[:, 8:16], cval[:, h, 8:16], cf))
                    if h % 4 == 3:
                        yield
                if qb:
                    v.wait_ge(pickT_ps, 1)
                pgate = pick[:, 2, :].rearrange("p (h k) -> p h k", h=HEADS)
                tt(pgate, cval, cval[:, :, 0:1].to_broadcast([P, HEADS, TOPK]), ALU.subtract).then_inc(topv, 1)
                D.put(ts(part[:, 0, :], cidx, 4, None, ALU.logical_shift_right))
                D.put(ts(part[:, 1, :], cidx, 15, None, ALU.bitwise_and))
                D.wait()
                step(v.tensor_copy(sel[:, 1280:1536], sel[:, 1024:1280].bitcast(U32)))
                for f in range(2):
                    step(tt(cand, partf[:, f, :, :].unsqueeze(3).to_broadcast([P, HEADS, TOPK, TOPK]),
                            io16.to_broadcast([P, HEADS, TOPK, TOPK]), ALU.is_equal))
                    yield
                    step(tt(cand, cand, idxf[:, :, f, :].unsqueeze(2).to_broadcast([P, HEADS, TOPK, TOPK]), ALU.mult))
                    step(v.tensor_reduce(pick[:, f, :].rearrange("p (h k) -> p h k", h=HEADS), cand, AX_X, ALU.add))
                v.wait_ge(gexp, qb + 1)
                step(v.tensor_reduce(gsum, pgate, AX_X, ALU.add))
                step(v.reciprocal(gsum, gsum))
                tt(pgate, pgate,
                   gsum.unsqueeze(2).to_broadcast([P, HEADS, TOPK]), ALU.mult).then_inc(picked, 1)
                yield

            assert SELECT_PIECES * 2 <= 32
            pieces = [select(0), select(1)]
            for u in range(32):
                if u < 2 * SELECT_PIECES:
                    next(pieces[u // SELECT_PIECES])
                low(FIRST["u0"] + u + 2)

            v.wait_ge(pickT_sb, 2)
            acts = A[:, :].rearrange("p (e t) -> p t e", e=EXP_T)
            for half in range(2):
                v.wait_ge(bank_free, FIRST[f"v{half}"] + 4)

                def hot(i, b, turn):
                    def cols(f, t0, n):
                        a0 = 1024 + f * T + 8 * b + 16 * turn + t0
                        c = W[:, a0:a0 + 8 - t0] if i is None else W[:, bass.ds(i * 16 + a0, 8 - t0)]
                        return c.unsqueeze(2).to_broadcast([P, 8 - t0, n])
                    step_n = 32 * half + 2 * turn + b + 1
                    v.wait_ge(hot_used, step_n if i is None else i * 2 + step_n)
                    D.put(tt(hot1[b], iota[:, 64 * half:64 * half + 64].unsqueeze(1).to_broadcast([P, 8, 64]),
                             cols(0, 0, 64), ALU.is_equal))
                    D.put(tt(hot2[b][:, HOT_POOL:8, :], iota[:, :].unsqueeze(1).to_broadcast([P, 8 - HOT_POOL, P]),
                             cols(1, HOT_POOL, P), ALU.is_equal))
                    D.wait(1)
                    tt(hot1[b], hot1[b], cols(2, 0, 64), ALU.mult).then_inc(hot1_ready, 1)

                def gated(i, b):
                    v.wait_ge(hot_used, i * 2 + (32 * half + b + 3))
                    w = W[:, 512 * b:512 * (b + 1)].rearrange("p (t e) -> p t e", t=8)
                    tok = slice(8 * (2 * i + b), 8 * (2 * i + b) + 8) if isinstance(i, int) else bass.ds(i * 16 + 8 * b, 8)
                    tt(w, acts[:, tok, :], psM[:, b, :].rearrange("p (t e) -> p t e", t=8), ALU.mult).then_inc(route_used, 1)

                def gated_low(i, b):
                    tok = slice(8 * (2 * i + b), 8 * (2 * i + b) + 8) if isinstance(i, int) else bass.ds(i * 16 + 8 * b, 8)
                    hl = acts16[:, :, :, tok].rearrange("p r e t -> p r t e")
                    w = W[:, 512 * b:512 * (b + 1)].rearrange("p (t e) -> p t e", t=8)
                    v.wait_ge(route_hi, i * 2 + (32 * half + b + 1))
                    tt(hl[:, 1, :, :], w, hl[:, 0, :, :], ALU.subtract).then_inc(acts_ready, 1)

                for b in range(2):
                    hot(None, b, 0)
                with D.loop(15, 4) as i:
                    for b in range(2):
                        gated(i, b)
                        hot(i, b, 1)
                        gated_low(i, b)
                    v.wait_ge(acts_ready, i * 2 + (32 * half + 2))
                for b in range(2):
                    gated(15, b)
                    gated_low(15, b)
                residual_b(f"v{half}", 80)
                if half == 0:
                    lows("u1", None)
            v.wait_ge(bank_free, FIRST["z"] + 4)
            squares(4, lambda a, m: tiles(X, a, m))
            inverse_rms(4)
            scale_rms(X, 0, KT, "final_g", 0)
            D.wait()
            squares(5, lambda a, m: tiles(X, a, m))
            inverse_rms(5)

            norm_split(lambda k: const("g_mix", k), None, KT)
            for n in range(17):
                low(FIRST["z"] + n + 2)

            def split(buf, k0, n, out, o0, signal):
                w = tiles(buf, k0, n).rearrange("p (m t) -> p m t", m=n)
                hl = tiles(out, o0, n).bitcast(F16).rearrange("p (m r t) -> p m r t", m=n, r=2)
                D.put(v.tensor_copy(hl[:, :, 0, :], w))
                D.wait()
                tt(hl[:, :, 1, :], w, hl[:, :, 0, :], ALU.subtract).then_inc(signal, 1)

            def branches():
                v.wait_ge(bank_free, FIRST["gate"] + 4)
                step(tt(tiles(J, 22, 6), tiles(J, 22, 6), tiles(A, 48, 6), ALU.mult))
                for k in range(6):
                    D.put(ts(tiles(A, 54 + k), tiles(J, 22 + k), const("w_dw_a", 31 * k + 30), const("b_dw_a", k),
                             ALU.mult, ALU.add))
                for tap in range(29, -1, -1):
                    d = 30 - tap
                    for k in range(6):
                        o = A[:, (54 + k) * T + d:(55 + k) * T]
                        D.wait(5 if tap else 5 - k)
                        ins = stt(o, J[:, (22 + k) * T:(23 + k) * T - d], const("w_dw_a", 31 * k + tap), o,
                                  ALU.mult, ALU.add)
                        if tap:
                            D.put(ins)
                        else:
                            ins.then_inc(conv_done, 1)
                    if tap % 3 == 0:
                        yield
                step(tt(tiles(J, 6, 6), tiles(J, 6, 6), tiles(J, 12, 6), ALU.mult))
                for k in range(6):
                    D.put(ts(tiles(J, 12 + k), tiles(J, 6 + k), const("w_dw_c", 3 * k + 2), None, ALU.mult))
                yield
                for tap in (1, 0):
                    d = 2 - tap
                    for k in range(6):
                        o = J[:, (12 + k) * T + d:(13 + k) * T]
                        D.wait(5)
                        D.put(stt(o, J[:, (6 + k) * T:(7 + k) * T - d], const("w_dw_c", 3 * k + tap), o, ALU.mult, ALU.add))
                yield
                D.wait()
                step(tt(tiles(J, 12, 6), tiles(J, 0, 6), tiles(J, 12, 6), ALU.mult))
                split(J, 12, 6, J, 6, yc_ready)
                v.wait_ge(yc_ready, 1)
                yield
                yield
                yield
                yield
                v.wait_ge(ln_ps, 1)
                step(ts(rs[:, :], psM[:, 3, 0:T], 1.0 / 768, None, ALU.mult))
                v.wait_ge(conv_done, 6)
                va = tiles(A, 54, 6).rearrange("p (k t) -> p k t", k=6)
                rs6 = rs[:, :].unsqueeze(1).to_broadcast([P, 6, T])
                tt(va, va, rs6, ALU.subtract).then_inc(ln_mu, 1)
                v.wait_ge(ln_mu, 1)
                v.wait_ge(pooled, 1)
                squares(6, lambda a, m: tiles(A, 54 + a, m))
                yield
                v.wait_ge(pool_sb, 4)
                split(J, 0, 4, J, 18, pool_split)
                yield
                yield
                yield
                inverse_rms(6)
                tt(va, va, rs6, ALU.mult).then_inc(ln_x, 1)
                yield
                v.wait_ge(va_ready, 6)
                split(J, 12, 6, J, 22, va_split)
                yield

            pieces = branches()
            for n in range(24):
                next(pieces, None)
                low(FIRST["gate"] + n + 2)
            assert next(pieces, "end") == "end"

            u0 = FIRST["abc"]
            v.wait_ge(bank_free, u0 + 4)
            def merge(i, j):
                ps = psW if j % 2 == 0 else psM
                D.wait()
                v.wait_ge(w_used, i * 4 + (u0 + j + 1))
                for b in range(3):
                    g = A[:, bass.ds(i * 8 * T + (16 * b + 2 * j) * T, 2 * T)]
                    ins = stt(tiles(W, 2 * b, 2), ps[:, b, :], 1 / WSCALE, g, ALU.mult, ALU.mult)
                    if b < 2:
                        D.put(ins)
                    else:
                        ins.then_inc(bank_free, 1)
                D.wait()
                D.put(tt(tiles(W, 0, 2), tiles(W, 0, 2), tiles(W, 2, 2), ALU.add))
                D.wait()
                v.wait_ge(bank_free, i * 4 + (u0 + j + 5))
                step(tt(tiles(W, 0, 2), tiles(W, 0, 2), tiles(W, 4, 2), ALU.add))
                w = tiles(W, 0, 2).rearrange("p (m t) -> p m t", m=2)
                hl = H[:, :].bitcast(F16)[:, bass.ds(i * 4096 + j * 1024, 1024)].rearrange("p (m r t) -> p m r t", m=2, r=2)
                step(v.tensor_copy(hl[:, :, 0, :], w))
                D.put(tt(hl[:, :, 1, :], w, hl[:, :, 0, :], ALU.subtract))
            lows("abc", merge, 24)
            D.wait()
            v.sem_inc(merged, 1)

            def residual_o(i, j):
                v.wait_ge(w_used, i * 4 + (FIRST["w_o"] + j + 1))
                x = X[:, bass.ds(i * 8 * T + 2 * j * T, 2 * T)]
                stt(x, psW[:, j, :], 1 / WSCALE, x, ALU.mult, ALU.add).then_inc(bank_free, 1)
            lows("w_o", residual_o)
            v.wait_ge(bank_free, FIRST["up"] + 4)
            squares(7, lambda a, m: tiles(X, a, m))
            inverse_rms(7)
            norm_split(lambda k: const("g_mlp", k), None, 2 * KT)
            u0 = FIRST["up"]

            def square(i, j):
                w = tiles(W, 2 * j, 2).rearrange("p (m t) -> p m t", m=2)
                hl = A[:, :].bitcast(F16)[:, bass.ds(i * 4096 + j * 1024, 1024)].rearrange("p (m r t) -> p m r t", m=2, r=2)
                v.wait_ge(bank_free, i * 4 + (u0 + j + 5))
                D.put(tt(w, w, w, ALU.mult))
                D.wait()
                D.put(v.tensor_copy(hl[:, :, 0, :], w))
                D.wait()
                tt(hl[:, :, 1, :], w, hl[:, :, 0, :], ALU.subtract).then_inc(relu_sb, 1)
            lows("up", square, 8)
            residual_b("down", 1 / (WSCALE * HSCALE ** 2))
            v.wait_ge(bank_free, N_UNITS + 4)
            squares(8, lambda a, m: tiles(X, a, m))
            inverse_rms(8)
            scale_rms(X, 0, KT, "g_final", 0, out_ready)

        @block.scalar
        def _(a):
            act = a.activation
            S = Chain(a, act_seq)

            def root(q):
                a.wait_ge(stat_ms, q + 1)
                act(rs[:, :], rs[:, :], ACT.Sqrt).then_inc(stat_rs, 1)

            def hi(u, i=0):
                s, n = slot_of(u)
                a.wait_ge(slot_full[s], i * 32 + 16 * n)
                a.wait_ge(w_used, i * 4 + (u - 1))
                for p2 in range(2):
                    c = slice(s * UNIT + p2 * (UNIT // 2), s * UNIT + (p2 + 1) * (UNIT // 2))
                    act(whi[:, c], ring[:, c], ACT.Copy, scale=WSCALE).then_inc(hi_done, 1)

            def his(name, put, n=None, first=0):
                u0 = FIRST[name] + first
                n = n if n is not None else dict(STREAM)[name] - first
                last = u0 + n == N_UNITS

                def body(i, last_turn=False):
                    for j in range(4):
                        if put:
                            a.wait_ge(w_used, i * 4 + (u0 + j + 1))
                            put(i, j).then_inc(bank_free, 1)
                        if not (last_turn and j >= 2):
                            hi(u0 + j + 2, i)
                turns = n // 4 - last
                if turns > 1:
                    with a.Fori(0, turns) as i:
                        body(i)
                elif turns:
                    body(0)
                if last:
                    body(turns, True)

            def take(name, put, n=None, first=0, loop=True):
                u0 = FIRST[name] + first
                n = n if n is not None else dict(STREAM)[name] - first

                def body(i, js):
                    for j in js:
                        a.wait_ge(w_used, i * 4 + (u0 + j + 1))
                        put(i, j).then_inc(bank_free, 1)
                if n >= 8:
                    with a.Fori(0, n // 4) as i:
                        body(i, range(4))
                elif n >= 4:
                    body(0, range(4))
                if n % 4:
                    body(n // 4, range(n % 4))

            def into(buf, func, j0=0, scale=1.0):
                return lambda i, j: act(buf[:, bass.ds(i * 4 * 512 + (j0 + j) * 512, 512)]
                                        if not isinstance(i, int) else buf[:, (4 * i + j0 + j) * 512:(4 * i + j0 + j + 1) * 512],
                                        psW[:, j, :], func, scale=scale)

            def par(k):
                return J[:, 4096 + 32 * k:4096 + 32 * (k + 1)]
            dt, lrdt, th, rnd, r_, co, cos, sin = (par(k) for k in range(8))
            a.wait_ge(cst_in, 16)
            act(csilu[:, :], const("c", 0, KT), ACT.Silu).then_inc(c_ready, 1)
            act(dt, const("log_dt", 0, 32), ACT.Exp).then_inc(act_trig, 1)
            a.wait_ge(dve_trig, 1)
            act(mag[:, :], lrdt, ACT.Exp).then_inc(act_trig, 1)
            a.wait_ge(dve_trig, 2)
            act(sin, r_, ACT.Sin).then_inc(act_trig, 1)
            act(cos, co, ACT.Sin).then_inc(act_trig, 1)

            def ada(i, j):
                return act(mod[:, bass.ds(i * 8 + 2 * j, 2)], psW[:, j, 0:2], ACT.Copy)

            def take_ada(a_, b_):
                with a.Fori(a_, b_) as i:
                    for j in range(4):
                        a.wait_ge(w_used, i * 4 + (j + 1))
                        ada(i, j).then_inc(bank_free, 1)
            take_ada(0, 2)
            for h in range(HEADS):
                a.wait_ge(bias_ps, h + 1)
                act(skew_sb[:, h * SKEW_W:(h + 1) * SKEW_W], psM[:, h % 4, 0:SKEW_W], ACT.Copy).then_inc(bias_sb, 1)
            a.wait_ge(bias_ps, HEADS + 1)
            act(cbias.rearrange("p q n h -> p (q n h)"), psW[:, 0, 0:240], ACT.Copy).then_inc(cbias_sb, 1)
            take_ada(2, 3)
            root(0)
            take_ada(3, FIRST["w_in"] // 4)
            a.wait_ge(cmat_ready, 1)
            for ct in range(4):
                a.dma_start(bmat[:, ct, :, :], bmat_d[:, ct, :, :]).then_inc(bmat_in[ct], 16)
            a.wait_ge(pool_const, 4)
            a.wait_ge(dyn_in, 16)
            a.wait_ge(skew_out, 16)
            take("w_in", into(J, ACT.Copy), n=4)
            act(diag[:, :], ident[:, :], ACT.Copy, scale=const("d_skip", 0)).then_inc(diag_ready, 1)
            for what, n in early_schedule():
                if what == "unit":
                    a.wait_ge(w_used, FIRST["w_in"] + n + 1)
                    act(J[:, n * 512:(n + 1) * 512], psW[:, n % 4, :], ACT.Copy).then_inc(bank_free, 1)
                elif what == "y" and n % 4 == 3:
                    ct = n // 4
                    a.wait_ge(scan_free, 2 + n + 1)
                    act(tiles(J, ct), psM[:, 2, 0:T], ACT.Gelu_apprx_tanh).then_inc(z_ready, 1)
                    if ct < 4:
                        a.dma_start(bmat[:, ct, :, :], bmat_d[:, ct + 4, :, :]).then_inc(bmat_in[ct], 16)
                    if ct < 7:
                        act(diag[:, :], ident[:, :], ACT.Copy, scale=const("d_skip", ct + 1)).then_inc(diag_ready, 1)
                elif what == "gates":
                    a.wait_ge(gates_ps, 1)
                    act(gates.rearrange("p q h c -> p (q h c)"), psM[:, 3, 0:48], ACT.Sigmoid).then_inc(gates_sb, 1)
                    a.dma_start(bias, bass_skew(skew_d)).then_inc(skew_in, 16)
                elif what == "cmp" and n % 2:
                    kv = n // 2
                    a.wait_ge(w_used, FIRST["cmp"] + n + 1)
                    act(cmp_hid[:, kv, :, :], psW[:, 2 * kv:2 * kv + 2, 0:30], ACT.Gelu_apprx_tanh).then_inc(cmp_hid_sb, 1)
                    a.wait_ge(cmp_hid_sb, kv + 1)
                    a.sem_inc(bank_free, 2)
            a.wait_ge(cmp_ps, 1)
            act(kc, psM[:, 3, 0:30], ACT.Copy).then_inc(cmp_sb, 1)
            act(vc.rearrange("p g d -> p (g d)"), psM[0:N_CMP, 3, 128:384], ACT.Copy).then_inc(cmp_sb, 1)
            for u in range(2):
                a.wait_ge(w_used, FIRST["glu"] + u + 1)
                for m in range(4):
                    k = 4 * u + m
                    act(glu_s[:, k * T:(k + 1) * T], psW[:, 2 * u + m // 2, (m % 2) * T:(m % 2 + 1) * T], ACT.Sigmoid,
                        bias=const("b_glu", k)).then_inc(glu_sb, 1)
                a.wait_ge(glu_sb, 4 * (u + 1))
                a.sem_inc(bank_free, 1)
            root(1)
            for b in range(2):
                a.wait_ge(v_ps, b + 1)
                act(vnat[:, b, :, :, :].rearrange("p g s d -> p (g s d)"), psW[:, b, :], ACT.Copy).then_inc(v_sb, 1)
            for r in range(16 + 2):
                if r < 16:
                    nk = P * (r % 2 + 1)
                    a.wait_ge(negmax, r + 1)
                    for b in range(3):
                        l = logit[r % 3][:, b * 256:b * 256 + (nk if b < 2 else N_CMP)]
                        act(l, l, ACT.Exp, bias=mxb[:, r % 3, b:b + 1], accum_out=smb[:, r % 3, b:b + 1]).then_inc(exp_sb, 1)
                if 1 <= r <= 16:
                    q = r - 1
                    w = P * (q % 2 + 1)
                    a.wait_ge(probT_ps, q + 1)
                    src = psW[:, 2, :].rearrange("p (b s) -> p b s", b=2)[:, :, 0:w]
                    dst = probT[q % 2][:, 0:512].rearrange("p (b s) -> p b s", b=2)[:, :, 0:w]
                    if q >= 2:
                        a.wait_ge(att_ps, q - 1)
                    act(dst, src, ACT.Copy).then_inc(probT_sb, 1)
                    act(probT[q % 2][0:N_CMP, 512:640], psM[0:N_CMP, 2, 0:P], ACT.Copy).then_inc(probT_sb, 1)
                if r >= 2:
                    q = r - 2
                    h, qb = q // 2, q % 2
                    a.wait_ge(att_ps, q + 1)
                    act(J[:, (8 + h) * T + qb * P:(8 + h) * T + (qb + 1) * P], psW[:, 3, 0:P], ACT.Copy).then_inc(att_sb, 1)
            root(2)
            def high(n, shift):
                for k in range(KT):
                    a.wait_ge(t_raw, KT * n + k + 1)
                    b = {} if shift is None else {"bias": mod[:, shift + k:shift + k + 1]}
                    act(halves(H, k)[0], tiles(W, k % 8), ACT.Copy if shift is None else ACT.Identity, **b).then_inc(t_hi, 1)
            hi(SPLIT_0)
            root(3)
            high(0, 48)
            hi(SPLIT_0 + 1)
            his("peer_q", into(J, ACT.Copy, scale=1 / WSCALE))
            for c in range(8):
                a.wait_ge(key_ps, c + 1)
                act(key_scores(c).rearrange("p s n -> p (s n)"), psM[:, c % 2, :], ACT.Copy).then_inc(key_sb, 1)
            for u in range(32):
                a.wait_ge(w_used, FIRST["u0"] + u + 1)
                act(A[:, u * 512:(u + 1) * 512], psW[:, u % 4, :], ACT.Gelu_apprx_tanh, scale=1 / WSCALE).then_inc(bank_free, 1)
                hi(FIRST["u0"] + u + 2)
                for qb in range(2):
                    if u == SELECT_PIECES * (qb + 1) - 3:
                        a.wait_ge(topv, qb + 1)
                        act(pick[:, 2, :], pick[:, 2, :], ACT.Exp).then_inc(gexp, 1)
                    if u == 15 + 12 * qb:
                        a.wait_ge(pickT_ps, qb + 1)
                        act(pickT[:, :, qb * P:(qb + 1) * P], psM[:, 2, 0:3 * P].rearrange("p (f t) -> p f t", f=3), ACT.Copy)\
                            .then_inc(pickT_sb, 1)
            for half in range(2):
                if half:
                    his("u1", into(A, ACT.Gelu_apprx_tanh, scale=1 / WSCALE))
                with a.Fori(0, 16) as i:
                    for b in range(2):
                        a.wait_ge(route_used, i * 2 + (32 * half + b + 3))
                        act(acts16[:, 0, :, bass.ds(i * 16 + 8 * b, 8)].rearrange("p e t -> p t e"),
                            W[:, 512 * b:512 * (b + 1)].rearrange("p (t e) -> p t e", t=8), ACT.Copy).then_inc(route_hi, 1)
                his(f"v{half}", None)
            root(4)
            root(5)
            high(1, None)
            for n in range(17):
                a.wait_ge(w_used, FIRST["z"] + n + 1)
                bank = n % 4 if n < 16 else 0
                if n < 11:
                    act(J[:, n * 512:(n + 1) * 512], psW[:, bank, :], ACT.Copy, scale=1 / WSCALE).then_inc(bank_free, 1)
                else:
                    for m in range(2):
                        k = 2 * (n - 11) + m
                        dst = tiles(J, 22 + k) if k < 6 else tiles(A, 48 + k - 6)
                        ins = act(dst, psW[:, bank, m * T:(m + 1) * T], ACT.Identity if k < 6 else ACT.Sigmoid,
                                  bias=const("b_glu2", k), scale=1 / WSCALE)
                    ins.then_inc(bank_free, 1)
                hi(FIRST["z"] + n + 2)
            for n in range(24):
                a.wait_ge(w_used, FIRST["gate"] + n + 1)
                for m in range(2):
                    k = 2 * n + m
                    ins = act(tiles(A, k), psW[:, n % 4, m * T:(m + 1) * T], ACT.Sigmoid, bias=const("b_gate", k),
                              scale=1 / WSCALE)
                ins.then_inc(bank_free, 1)
                hi(FIRST["gate"] + n + 2)
                if n == 15:
                    a.wait_ge(yc_ready, 1)
                    a.wait_ge(pool_ps, 1)
                    for g in range(4):
                        act(tiles(J, g), psM[:, g // 2, (g % 2) * T:(g % 2 + 1) * T], ACT.Copy,
                            scale=const("pool_scale", g)).then_inc(pool_sb, 1)
                if n == 20:
                    root(6)
                    a.wait_ge(ln_x, 1)
                    for k in range(6):
                        act(tiles(J, 12 + k), tiles(A, 54 + k), ACT.Silu, scale=const("ln_g", k), bias=const("ln_b", k))\
                            .then_inc(va_ready, 1)
            his("abc", None)
            his("w_o", None)
            root(7)
            high(2, None)
            def relu(i, j):
                a.wait_ge(relu_sb, i * 4 + (j + 1))
                return act(tiles(W, 2 * j, 2), psW[:, j, :], ACT.Relu, scale=HSCALE / WSCALE)
            his("up", relu)
            his("down", None)
            root(8)

        @block.gpsimd
        def _(g):
            G = Chain(g, pool_seq)
            g.dma_start(cst[:, :], cst_d).then_inc(cst_in, 16)
            g.dma_start(onehot, onehot_d).then_inc(onehot_in, 16)
            g.dma_start(X[:, :], xT_d.rearrange("p k t -> p (k t)")).then_inc(x_in, 16)
            g.dma_start(dyn[:, 0:960], dyn1_d).then_inc(dyn_in, 16)
            G.put(g.memset(ident[:, :], 0.0))
            G.put(g.memset(cvalid.rearrange("p q n -> p (q n)"), 1.0))
            g.memset(ones[:, :], 1.0).then_inc(pool_const, 2)
            G.wait()
            g.affine_select(out=ident[:, :], in_=ident[:, :], compare_op=ALU.not_equal, fill=1.0, base=0,
                            pattern=[[-1, P]], channel_multiplier=1).then_inc(pool_const, 1)
            g.affine_select(out=cvalid, in_=cvalid, compare_op=ALU.is_ge, fill=0.0, base=-31,
                            pattern=[[P, 2], [-16, N_CMP]], channel_multiplier=1).then_inc(pool_const, 1)
            g.sem_inc(bank_free, 4)
            g.sem_inc(scan_free, 2)
            g.sem_inc(hot_used, 2)
            g.sem_inc(relu_sb, 4)
            g.sem_inc(route_used, 2)
            par = lambda k: J[:, 4096 + 32 * k:4096 + 32 * (k + 1)]
            cos, sin, pr, pi, npr, q1 = par(6), par(7), par(17), par(18), par(19), par(20)
            g.wait_ge(act_trig, 4)
            G.put(g.memset(tab[:, :, 0, 0:1], 1.0))
            G.put(g.memset(tab[:, :, 1, 0:1], 0.0))
            G.put(g.tensor_copy(pr, cos))
            G.put(g.tensor_copy(pi, sin))
            G.wait()
            tmp = H[:, :].rearrange("p (i t) -> p i t", i=NSTATE_T)
            k = 1
            while k < T:
                def wide(x):
                    return x.unsqueeze(2).to_broadcast([P, NSTATE_T, k])
                c0, s0, cd, sd = tab[:, :, 0, 0:k], tab[:, :, 1, 0:k], tab[:, :, 0, k:2 * k], tab[:, :, 1, k:2 * k]
                G.put(g.tensor_tensor(cd, c0, wide(pr), ALU.mult))
                G.put(g.tensor_tensor(tmp[:, :, 0:k], s0, wide(pi), ALU.mult))
                G.wait()
                G.put(g.tensor_tensor(cd, cd, tmp[:, :, 0:k], ALU.subtract))
                G.put(g.tensor_tensor(sd, c0, wide(pi), ALU.mult))
                G.wait(1)
                G.put(g.tensor_tensor(tmp[:, :, 0:k], s0, wide(pr), ALU.mult))
                G.wait()
                ins = g.tensor_tensor(sd, sd, tmp[:, :, 0:k], ALU.add)
                if 2 * k == T:
                    ins.then_inc(tab_ready, 1)
                    break
                G.put(ins)
                G.put(g.tensor_tensor(npr, pr, pr, ALU.mult))
                G.put(g.tensor_tensor(q1, pi, pi, ALU.mult))
                G.put(g.tensor_tensor(pi, pr, pi, ALU.mult))
                G.wait()
                G.put(g.tensor_tensor(pr, npr, q1, ALU.subtract))
                G.put(g.tensor_tensor(pi, pi, pi, ALU.add))
                G.wait()
                k *= 2
            g.wait_ge(bias_sb, HEADS)
            g.dma_start(skew_d.rearrange("h p w -> p h w"), skew_sb.rearrange("p (h w) -> p h w", h=HEADS))\
             .then_inc(skew_out, 16)
            g.wait_ge(h_ready, 1)
            g.dma_start(cmat, cmat_d).then_inc(cmat_in, 16)
            t3 = W[:, 1024:1536].rearrange("p (r t) -> p r t", r=2)
            t4 = W[:, 1536:2048].rearrange("p (r t) -> p r t", r=2)
            with G.loop(8, 12) as c:
                for j in range(4):
                    w = scanb[:, j % 2, :, :]
                    g.wait_ge(scan_out, c * 4 + (j + 1))
                    cosv = A[:, bass.ds(c * 2048 + j * 512, T)].unsqueeze(1).to_broadcast([P, 2, T])
                    sinv = A[:, bass.ds(c * 2048 + (j * 512 + T), T)].unsqueeze(1).to_broadcast([P, 2, T])
                    G.put(g.tensor_tensor(t3, w, cosv, ALU.mult))
                    G.put(g.tensor_tensor(t4, w, sinv, ALU.mult))
                    G.wait()
                    G.put(g.tensor_tensor(w[:, 0, :], t3[:, 0, :], t4[:, 1, :], ALU.subtract))
                    g.tensor_tensor(w[:, 1, :], t3[:, 1, :], t4[:, 0, :], ALU.add).then_inc(rotated, 1)
                    g.wait_ge(rotated, c * 4 + (j + 1))
            g.wait_ge(z_ready, 8)
            g.dma_start(X[:, :], xT_d.rearrange("p k t -> p (k t)")).then_inc(x_in, 16)
            g.wait_ge(att_sb, 16)
            g.dma_start(dyn[:, 0:256], dyn2_d).then_inc(dyn_in, 16)
            g.iota(iota[:, :], pattern=[[1, P]], base=0, channel_multiplier=0,
                   allow_small_or_imprecise_dtypes=True).then_inc(iota_ready, 1)
            g.wait_ge(iota_ready, 1)
            g.wait_ge(pickT_sb, 2)
            for half in range(2):
                with G.loop(16, 2) as i:
                    for b in range(2):
                        e2 = small[:, 18 + 8 * b:26 + 8 * b]
                        G.put(g.tensor_copy(e2, W[:, bass.ds(i * 16 + (1024 + T + 8 * b), 8)]))
                        g.wait_ge(hot_used, i * 2 + (32 * half + b + 1))
                        G.wait()
                        g.sem_inc(pool_tick, 1)
                        for t in range(HOT_POOL):
                            ins = g.tensor_scalar(hot2[b][:, t, :], iota[:, :], e2[:, t:t + 1], None, ALU.is_equal)
                        ins.then_inc(hot2_ready, 1)
            g.wait_ge(key_ps, 8)
            g.dma_start(dyn[:, 0:512], dyn3_d).then_inc(dyn_in, 16)
            g.wait_ge(bank_free, FIRST["z"] + 4 + 11)
            zb = [tiles(J, 18 + q) for q in range(4)]
            ping = [tiles(A, 60 + q) for q in range(4)]
            pong = [tiles(W, q) for q in range(4)]
            cur = zb
            for level in range(4):
                d = 1 << level
                nxt = ping if level % 2 == 0 else pong
                for q in range(level, 4):
                    G.put(g.tensor_copy(nxt[q][:, 0:d], cur[q][:, 0:d]))
                    G.put(g.tensor_tensor(nxt[q][:, d:T], cur[q][:, d:T], cur[q][:, 0:T - d], ALU.add))
                G.wait()
                q, w = level, 2 << level
                o = nxt[q]
                G.put(g.tensor_tensor(o[:, 0:w], o[:, 0:w], const("pool_rcnt", 16 * q, w), ALU.mult))
                G.put(g.tensor_scalar(o[:, w:T], o[:, w:T], 1.0 / w, None, ALU.mult))
                G.wait()
                ins = g.tensor_tensor(ping[q], o, zb[q], ALU.subtract)
                if level < 3:
                    G.put(ins)
                    G.wait()
                else:
                    ins.then_inc(pooled, 1)
                cur = nxt


def bass_skew(skew_d):
    return bass.AP(skew_d.tensor, 127, [[SKEW_W - 1, P], [P * SKEW_W, HEADS], [1, T]])


def bucket_onehot():
    def bucket(n):
        scaled = np.log(np.float32(max(n, 16)) / np.float32(16)).astype(np.float32) / np.float32(math.log(1024 / 16))
        large = 16 + int(np.float32(scaled) * np.float32(16))
        return n if n < 16 else min(large, 31)

    out = np.zeros((33, SKEW_W + ASC_W), np.float32)
    for c in range(SKEW_W):
        d = 255 - c
        out[32 if d < 0 else bucket(d), c] = 1
    for c in range(ASC_W):
        d = c - ASC_0
        out[32 if d < 0 else bucket(d), SKEW_W + c] = 1
    return out


def units_a(w):
    n = w.shape[1]
    return w.reshape(16, P, n // 256, 256).transpose(2, 1, 0, 3).reshape(n // 256, P, UNIT)


def units_b(w):
    n = w.shape[1]
    return w.reshape(2, 32, P, n // P, P).transpose(3, 0, 2, 1, 4).reshape(2 * (n // P), P, UNIT)


def cols(v):
    return np.ascontiguousarray(v.reshape(-1, P).T)


def layout(i):
    f = {k: np.asarray(v) for k, v in i.items()}
    w_in = f["w_in"][0]
    w_u = f["peer_u"][0].T
    w_v = f["peer_v"][0]
    z = f["w_in_2"][0]
    z = np.concatenate([z[:, 2048:4352], z[:, 1536:2048], z[:, 0:1536]], axis=1)
    abc = np.concatenate([f["w_a_out_2"][0], f["w_b_out_2"][0], f["w_c_out_2"][0]], axis=0)
    cmp_u = lambda w: w.reshape(2, 16, P, 256).transpose(0, 2, 1, 3).reshape(2, P, UNIT)
    glu = f["ssm_w_glu"][0].reshape(8, P, 2, 512).transpose(2, 1, 0, 3).reshape(2, P, UNIT)
    wst = np.concatenate([
        units_a(f["w_ada"][0]), units_a(w_in[:, 0:3584]), cmp_u(f["cmp_w1_k"][0]), cmp_u(f["cmp_w1_v"][0]), glu,
        units_a(f["w_out"][0]), units_a(f["peer_w_q"][0]),
        units_a(w_u[:, 0:8192]), units_b(w_v[0:8192]), units_a(w_u[:, 8192:]), units_b(w_v[8192:]),
        units_a(z), units_a(f["w_gate_2"][0]), units_a(abc), units_a(f["w_o_2"][0]),
        units_a(f["w_up_2"][0]), units_b(f["w_down_2"][0])], axis=0)
    rcnt = np.zeros((4, 16), np.float32)
    for g in range(4):
        rcnt[g] = 1 / np.minimum(np.arange(16) + 1, 2 << g).astype(np.float32)
    table = {
        "c": cols(f["c"][0]), "b_ada": cols(f["b_ada"][0]), "norm1_g": cols(f["norm1_g"][0]),
        "norm2_g": cols(f["norm2_g"][0]), "final_g": cols(f["final_g"]), "g_mix": cols(f["g_mix_2"][0]),
        "g_mlp": cols(f["g_mlp_2"][0]), "g_final": cols(f["g_final_2"]),
        "beta": np.concatenate([cols(f["beta_ssm"][0]), cols(f["beta_attn"][0])], axis=1),
        "lam_re": cols(f["ssm_lam_re"][0]), "lam_im": cols(f["ssm_lam_im"][0]),
        "log_dt": cols(np.repeat(f["ssm_log_dt"][0], 64)), "d_skip": cols(f["ssm_d"][0]),
        "b_glu": cols(f["ssm_b_glu"][0]), "b_gate": cols(f["b_gate_2"][0]), "b_glu2": cols(f["b_glu_2"][0]),
        "w_dw_a": f["w_dw_a_2"][0].reshape(31, 6, P).transpose(2, 1, 0).reshape(P, 186),
        "b_dw_a": cols(f["b_dw_a_2"][0]), "ln_g": cols(f["ln_g_a_2"][0]), "ln_b": cols(f["ln_b_a_2"][0]),
        "pool_scale": cols(f["pool_scale_2"][0]),
        "w_dw_c": f["w_dw_c_2"][0].reshape(3, 6, P).transpose(2, 1, 0).reshape(P, 18),
        "pool_rcnt": np.tile(rcnt.reshape(1, 64), (P, 1)),
    }
    cst = np.concatenate([table[n] for n, _ in CONST], axis=1)
    gcols = w_in[:, 3584:3608].reshape(D, 3, HEADS)[:, [1, 2, 0], :].transpose(0, 2, 1).reshape(D, 24)
    half = lambda w: w.reshape(2, P, P).transpose(1, 0, 2).reshape(P, 256)
    dyn1 = np.concatenate([gcols.reshape(KT, P, 24).transpose(1, 0, 2).reshape(P, 384),
                           half(f["cmp_w2_k"][0]), half(f["cmp_w2_v"][0]),
                           f["cmp_pe_k"][0].T, f["cmp_pe_v"][0].T], axis=1)
    dyn2 = np.concatenate([f["peer_k1"][0].T, f["peer_k2"][0].T], axis=1)
    dyn3 = f["w_pool_grp_2"][0].transpose(1, 0, 2).reshape(P, 512)
    rel = np.concatenate([f["rel_bias"], np.full((1, HEADS), NEG, np.float32)], axis=0)
    onehot = np.concatenate([bucket_onehot(), rel], axis=1)
    bm = np.zeros((2, 8, 4, 2, 16, 2, 64), np.float32)
    cm = np.zeros((2, 32, 2, 64, 2, 16), np.float32)
    for r, n in enumerate(("re", "im")):
        b = f["ssm_b_" + n][0].reshape(8, 4, 2, 64, 16).transpose(0, 1, 2, 4, 3)
        c = f["ssm_c_" + n][0].reshape(32, 2, 16, 64).transpose(0, 1, 3, 2)
        for g in range(2):
            bm[r, :, :, g, :, g, :] = b[:, :, g]
            cm[r, :, g, :, g, :] = c[:, g]
    bmat = bm.reshape(2, 8, P, P).transpose(2, 1, 0, 3)
    cmat = cm.reshape(2, 32, P, 32).transpose(2, 0, 1, 3)
    xT = f["x"][0].T.reshape(KT, P, T).transpose(1, 0, 2)
    arrays = {"xT": xT, "wst": wst, "cst": cst, "dyn1": dyn1, "dyn2": dyn2, "dyn3": dyn3, "onehot": onehot,
              "bmat": bmat, "cmat": cmat}
    return {k + "_dram": np.ascontiguousarray(v) for k, v in arrays.items()}


def kernel(**inputs):
    import concourse.bacc as bacc
    from concourse.bass_utils import run_bass_kernel_spmd

    arrays = layout(inputs)
    nc = bacc.Bacc("TRN2", target_bir_lowering=False, num_devices=1)
    aps = [nc.dram_tensor(k, a.shape, mybir.dt.from_np(a.dtype), kind="ExternalInput").ap() for k, a in arrays.items()]
    skew = nc.dram_tensor("bias_rows", (HEADS, P, SKEW_W), F32, kind="Internal").ap()
    out = nc.dram_tensor("out_dram", (P, KT, T), F32, kind="ExternalOutput").ap()
    program(nc, *aps, skew, out)
    r = run_bass_kernel_spmd(nc, [arrays], core_ids=[0])
    y = np.asarray(r.results[0]["out_dram"])
    return np.ascontiguousarray(y.transpose(1, 0, 2).reshape(D, T).T)[None]
```

```python
from contextlib import ExitStack, contextmanager
import math

import numpy as np

import concourse.bass as bass
from concourse import mybir

F32 = mybir.dt.float32
F16 = mybir.dt.float16
U32 = mybir.dt.uint32
ALU = mybir.AluOpType
ACT = mybir.ActivationFunctionType
AX_X = mybir.AxisListType.X

P = 128
T = 256
D_MODEL = 2048
KT = D_MODEL // P
UNIT = 4096
RING = 4
RAW = 2
ADA_DVE = 12
WSCALE = 256.0
HSCALE = 1 / 8
NSTATE_T = 32
N_CMP = 15
HEADS = 8
NEG = -1e30
EPS = 1e-6
SCALE = 128 ** -0.5
EXP_T = 64
TOPK = 16
SSM_RATE = 1.7
GSCALE = 4096.0
SELECT_PIECES = 13

STREAM = [("ada", 48), ("w_in", 14), ("glu", 2), ("cmp", 4), ("w_out", 8), ("peer_q", 8),
          ("u0", 32), ("v0", 32), ("u1", 32), ("v1", 32),
          ("z", 17), ("gate", 24), ("abc", 8), ("w_o", 8), ("up", 32), ("down", 32)]
FIRST = {}
N_UNITS = 0
for _name, _n in STREAM:
    FIRST[_name] = N_UNITS
    N_UNITS += _n

SPLIT_0 = FIRST["cmp"]



def slot_of(u):
    if u < SPLIT_0:
        return u % RING, u // RING + 1
    return u % RAW, SPLIT_0 // RING + (u - SPLIT_0) // RAW + 1


def per_turn(u):
    return 1 if u < SPLIT_0 else 2


def split_rank(u):
    return u - SPLIT_0 if u >= SPLIT_0 else None


CONST = [("c", 16), ("b_ada", 96), ("norm1_g", 16), ("norm2_g", 16), ("final_g", 16), ("g_mix", 16),
         ("g_mlp", 16), ("g_final", 16), ("beta", 16), ("lam_re", 32), ("lam_im", 32), ("log_dt", 32),
         ("d_skip", 8), ("b_glu", 8), ("b_gate", 48), ("b_glu2", 12), ("w_dw_a", 186), ("b_dw_a", 6),
         ("ln_g", 6), ("ln_b", 6), ("pool_scale", 4), ("w_dw_c", 18), ("pool_rcnt", 64)]
COL = {}
N_CONST = 0
for _name, _n in CONST:
    COL[_name] = N_CONST
    N_CONST += _n

SKEW_W = 384
ASC_0 = 255
ASC_W = 480

STATS = [16, 8, 8, 16, 32, 0, 6, 16, 16]
CHUNK = 4


def chunks_of(n):
    return [(a, min(CHUNK, n - a)) for a in range(0, n, CHUNK)]


STAT_CHUNK0 = [sum(len(chunks_of(m)) for m in STATS[:q]) for q in range(len(STATS))]


def early_schedule():
    out, x, y = [], 0, 0

    def ssm(upto):
        nonlocal x, y
        while x < min(upto, NSTATE_T):
            out.append(("x", x))
            x += 1
            if x - y > 3:
                out.append(("y", y))
                y += 1
    for v in range(4, 14):
        out.append(("half", v))
        ssm(round(SSM_RATE * (2 * (v - 4) + 1)))
        out.append(("unit", v))
        ssm(round(SSM_RATE * (2 * (v - 4) + 2)))
    ssm(NSTATE_T)
    out.append(("gates", 0))
    out += [("y", n) for n in range(y, NSTATE_T)]
    return out + [("cmp", v) for v in range(4)]


class Chain:

    def __init__(self, eng, sem):
        self.eng, self.sem, self.n, self.i, self.per = eng, sem, 0, None, 0

    def put(self, ins):
        ins.then_inc(self.sem, 1)
        self.n += 1
        return self.value()

    def value(self):
        return self.n if self.i is None else self.i * self.per + self.n

    def wait(self, back=0):
        self.eng.wait_ge(self.sem, self.value() - back)

    @contextmanager
    def loop(self, times, per, first=0):
        with self.eng.Fori(first, first + times) as i:
            n0, self.i, self.per = self.n, i, per
            self.n -= first * per
            yield i
            assert self.n - n0 + first * per == per, (self.n - n0, per)
        self.i = None
        self.n = n0 + per * times


def program(nc, xT_d, wst, cst_d, dyn1_d, dyn2_d, dyn3_d, onehot_d, bmat_d, cmat_d, skew_d, out_d):
    ctx = ExitStack()
    with ctx:
        def sb(name, cols, dt=F32):
            return ctx.enter_context(nc.sbuf_tensor(name, [P, cols], dt))

        def sem(name):
            return ctx.enter_context(nc.semaphore(name))

        ring = sb("ring", RING * UNIT)
        A = sb("arena", 64 * T)
        X = sb("x_res", KT * T)
        H = sb("h_act", KT * T)
        J = sb("proj", 28 * T)
        W = sb("work", 8 * T)
        cst = sb("cst", N_CONST)
        dyn = sb("dyn", 960)
        mod = sb("mod", 96)
        csilu = sb("csilu", KT)
        affine = sb("affine", KT)
        rs = sb("rs", T)
        mag = sb("mag", NSTATE_T)
        small = sb("small", 64)
        ident = sb("ident", P)
        ones = sb("ones", P)
        psW = ctx.enter_context(nc.psum_tensor("psW", [P, 4, 512], F32))
        psM = ctx.enter_context(nc.psum_tensor("psM", [P, 4, 512], F32))

        def const(name, a=0, n=1):
            return cst[:, COL[name] + a:COL[name] + a + n]

        def tiles(buf, a, n=1):
            return buf[:, a * T:(a + n) * T]

        def halves(buf, k):
            b = buf[:, k * T:(k + 1) * T].bitcast(F16)
            return b[:, 0:T], b[:, T:2 * T]

        split_w = ring[:, 2 * UNIT:4 * UNIT].bitcast(F16)

        def whi(s, a, n):
            return split_w[:, 2 * s * UNIT + a:2 * s * UNIT + a + n]

        def wlo(s, a, n):
            return split_w[:, (2 * s + 1) * UNIT + a:(2 * s + 1) * UNIT + a + n]

        tab = A[:, :].rearrange("p (i r t) -> p i r t", i=NSTATE_T, r=2)
        cmat = X[:, 0:2048].rearrange("p (r i c) -> p r i c", r=2, i=NSTATE_T)
        scanb = X[:, 2048:3072].rearrange("p (b r t) -> p b r t", b=2, r=2)
        bmat = X[:, 3072:4096].rearrange("p (s r n) -> p s r n", s=4, r=2)
        onehot = J[0:33, 0:SKEW_W + ASC_W + HEADS]
        skew_sb = J[:, 1024:1024 + HEADS * SKEW_W]
        blk = H[:, 0:1920].rearrange("p (v o n) -> p v o n", v=2, o=32)
        blk16 = W[:, 0:1920].bitcast(F16).rearrange("p (r v o n) -> p r v o n", r=2, v=2, o=32)
        cmp_hid = H[:, 1920:2040].rearrange("p (v m n) -> p v m n", v=2, m=2)
        bias = H[:, 2048:4096].rearrange("p (h s) -> p h s", h=HEADS)
        gate_w = dyn[:, 0:384].rearrange("p (k n) -> p k n", k=KT)
        kc = dyn[:, 0:30]
        vc = dyn[0:N_CMP, 32:32 + 256].rearrange("p (g d) -> p g d", g=2)
        w2 = dyn[:, 384:896].rearrange("p (v m d) -> p v m d", v=2, m=2)
        pe = dyn[:, 896:960].rearrange("p (v o) -> p v o", v=2)
        keys = dyn[:, 0:256].rearrange("p (f n) -> p f n", f=2)
        pool_w = dyn[:, 0:512].rearrange("p (g n) -> p g n", g=4)
        vnat = A[:, 0:1024].rearrange("p (b g s d) -> p b g s d", b=2, g=2, s=2)
        LW = 528
        logit = [A[:, 1024 + LW * i:1024 + LW * (i + 1)] for i in range(3)]
        probT = [A[:, 2816 + 640 * i:2816 + 640 * (i + 1)] for i in range(2)]
        acts16 = A[:, :].bitcast(F16).rearrange("p (e t r) -> p r e t", e=EXP_T, r=2)
        ada_acc = J[:, 5120:6144].rearrange("p (b a n) -> p b a n", b=2, a=2)
        glu_s = A[:, 8192:8192 + 8 * T]
        mxb = small[:, 0:9].rearrange("p (b c) -> p b c", b=3)
        smb = small[:, 9:18].rearrange("p (b c) -> p b c", b=3)
        gates = sb("gates", 48)[:, :].rearrange("p (q h c) -> p q h c", q=2, h=HEADS)
        cvalid = sb("cvalid", 30)[:, :].rearrange("p (q n) -> p q n", q=2)
        cbias = sb("cbias", 240)[:, :].rearrange("p (q n h) -> p q n h", q=2, n=N_CMP)
        cand = J[:, 0:2048].rearrange("p (h a b) -> p h a b", h=HEADS, a=TOPK)
        sel = J[:, 2048:4096]
        val = sel[:, 0:256].rearrange("p (h f k) -> p h f k", h=HEADS, f=2)
        idx = sel[:, 256:512].bitcast(U32).rearrange("p (h f k) -> p h f k", h=HEADS, f=2)
        idxf = sel[:, 512:768].rearrange("p (h f k) -> p h f k", h=HEADS, f=2)
        cval = sel[:, 768:896].rearrange("p (h k) -> p h k", h=HEADS)
        cidx = sel[:, 896:1024].bitcast(U32)
        part = sel[:, 1024:1280].bitcast(U32).rearrange("p (f n) -> p f n", f=2)
        partf = sel[:, 1280:1536].rearrange("p (f h k) -> p f h k", f=2, h=HEADS)
        pick = sel[:, 1536:1920].rearrange("p (f n) -> p f n", f=3)
        gsum = sel[:, 1920:1928]
        pickT = W[:, 1024:1792].rearrange("p (f t) -> p f t", f=3)
        e16 = J[:, 2048:2304].bitcast(F16).rearrange("p (f t) -> p f t", f=2)
        g16 = J[:, 2304:2560].bitcast(F16).rearrange("p (r t) -> p r t", r=2)
        iota16 = J[:, 2560:2624].bitcast(F16)
        hot2 = [J[:, 4096 + 512 * b:4096 + 512 * (b + 1)].bitcast(F16).rearrange("p (t e) -> p t e", t=8) for b in range(2)]
        first1 = [J[:, 5120 + 256 * b:5120 + 256 * (b + 1)].bitcast(F16).rearrange("p (t e) -> p t e", t=8) for b in range(2)]
        hot1 = [J[:, 5632 + 512 * b:5632 + 512 * (b + 1)].bitcast(F16).rearrange("p (t r e) -> p t r e", t=8, r=2)
                for b in range(2)]
        iota = sb("iota", P)
        diag = iota

        def key_scores(c):
            buf = J[:, 4096 + 512 * c:4096 + 512 * (c + 1)] if c < 6 else W[:, 512 * (c - 6):512 * (c - 5)]
            return buf.rearrange("p (s n) -> p s n", s=4)

        cst_in, dyn_in, x_in, onehot_in = sem("cst_in"), sem("dyn_in"), sem("x_in"), sem("onehot_in")
        cmat_in, skew_out, skew_in, y_out = sem("cmat_in"), sem("skew_out"), sem("skew_in"), sem("y_out")
        bmat_in = [sem(f"bmat_in{i}") for i in range(4)]
        slot_full = [sem(f"slot_full{i}") for i in range(RING)]
        hi_done, split_done, ada_sum, tab_ready = sem("hi_done"), sem("split_done"), sem("ada_sum"), sem("tab_ready")
        route_hi, first1_ready = sem("route_hi"), sem("first1_ready")
        va_split, pool_split = sem("va_split"), sem("pool_split")
        h_tile, h_first = sem("h_tile"), sem("h_first")
        t_raw, t_hi, acts_ready = sem("t_raw"), sem("t_hi"), sem("acts_ready")
        w_used, bank_free = sem("w_used"), sem("bank_free")
        pool_const = sem("pool_const")
        dve_seq, act_seq, pool_seq = sem("dve_seq"), sem("act_seq"), sem("pool_seq")
        stat_sq, stat_used, stat_ms, stat_rs = sem("stat_sq"), sem("stat_used"), sem("stat_ms"), sem("stat_rs")
        c_ready, act_trig, dve_trig = sem("c_ready"), sem("act_trig"), sem("dve_trig")
        cmat_ready = sem("cmat_ready")
        bias_ps, bias_sb, cbias_sb = sem("bias_ps"), sem("bias_sb"), sem("cbias_sb")
        x_ps, x_read, scan_out, rotated, scan_free = sem("x_ps"), sem("x_read"), sem("scan_out"), sem("rotated"), sem("scan_free")
        diag_ready, z_ready, gates_ps, gates_sb = sem("diag_ready"), sem("z_ready"), sem("gates_ps"), sem("gates_sb")
        blk_ready, cmp_hid_sb, cmp_ps, cmp_sb = sem("blk_ready"), sem("cmp_hid_sb"), sem("cmp_ps"), sem("cmp_sb")
        glu_sb, mix_ready = sem("glu_sb"), sem("mix_ready")
        v_ps, v_sb = sem("v_ps"), sem("v_sb")
        score_ps, logit_sb, negmax, exp_sb, prob_sb = sem("score_ps"), sem("logit_sb"), sem("negmax"), sem("exp_sb"), sem("prob_sb")
        probT_ps, probT_sb, att_ps, att_sb = sem("probT_ps"), sem("probT_sb"), sem("att_ps"), sem("att_sb")
        key_ps, key_sb, topv, gexp, picked, pickT_ps, pickT_sb = (
            sem("key_ps"), sem("key_sb"), sem("topv"), sem("gexp"), sem("picked"), sem("pickT_ps"), sem("pickT_sb"))
        hot2_ready, hot1_ready, hot_used, route_used = sem("hot2_ready"), sem("hot1_ready"), sem("hot_used"), sem("route_used")
        pooled, pool_ps, pool_sb = sem("pooled"), sem("pool_ps"), sem("pool_sb")
        conv_done, ln_ps, ln_mu, ln_x, va_ready, yc_ready = (
            sem("conv_done"), sem("ln_ps"), sem("ln_mu"), sem("ln_x"), sem("va_ready"), sem("yc_ready"))
        iota_ready = sem("iota_ready")
        merged, out_ready, relu_sb = sem("merged"), sem("out_ready"), sem("relu_sb")

        block = ctx.enter_context(nc.Block())

        @block.sync
        def _(sp):
            def load(u, slot):
                sp.dma_start(ring[:, slot * UNIT:(slot + 1) * UNIT], wst[u, :, :]).then_inc(slot_full[slot], 16)

            for u in range(RING):
                load(u, u)
            with sp.Fori(1, SPLIT_0 // RING) as i:
                for s in range(RING):
                    sp.wait_ge(w_used, i * RING + (s + 1 - RING))
                    sp.dma_start(ring[:, s * UNIT:(s + 1) * UNIT],
                                 wst[bass.ds(i * RING + s, 1), :, :].rearrange("o p n -> (o p) n"))\
                      .then_inc(slot_full[s], 16)

            def loads(a, b, free, less):
                if a % 2:
                    sp.wait_ge(free, a - less)
                    load(a, 1)
                    a += 1
                with sp.Fori(a // 2, b // 2) as i:
                    for s in range(2):
                        sp.wait_ge(free, i * 2 + (s - less))
                        sp.dma_start(ring[:, s * UNIT:(s + 1) * UNIT],
                                     wst[bass.ds(i * 2 + s, 1), :, :].rearrange("o p n -> (o p) n"))\
                          .then_inc(slot_full[s], 16)
                if b % 2:
                    sp.wait_ge(free, b - 1 - less)
                    load(b - 1, 0)

            for u in range(2):
                sp.wait_ge(w_used, SPLIT_0 + u - RING + 1)
                load(SPLIT_0 + u, u)
            loads(SPLIT_0 + 2, N_UNITS, split_done, SPLIT_0 + 1)
            for c in range(4):
                sp.wait_ge(out_ready, c + 1)
                sp.dma_start(out_d[:, 4 * c:4 * c + 4, :], tiles(X, 4 * c, 4).rearrange("p (k t) -> p k t", k=4))\
                  .then_inc(y_out, 16)
            sp.wait_ge(y_out, 64)

        @block.tensor
        def _(pe_):
            def slot_ready(u0, j, i):
                if split_rank(u0) is not None:
                    pe_.wait_ge(split_done, i * 4 + (split_rank(u0) + j + 1))
                    return (u0 + j) % RAW
                s, n = slot_of(u0 + j)
                pe_.wait_ge(slot_full[s], i * 16 * per_turn(u0) + 16 * n)
                return s

            def stage(name, emit, n=None, first=0, lead=1, drained=True, head=None):
                u0 = FIRST[name] + first
                n = n if n is not None else dict(STREAM)[name] - first
                if drained:
                    pe_.wait_ge(bank_free, u0 + 4)

                def body(i, js):
                    for j in js:
                        s = slot_ready(u0, j, i)
                        if lead != 2 or j % 2 == 0:
                            pe_.wait_ge(bank_free, i * 4 + (u0 + j + lead))
                        (head if head and isinstance(i, int) and i + j == 0 else emit)(s, j).then_inc(w_used, 1)

                turns = n // 4
                if head:
                    body(0, range(4))
                if turns > 1:
                    with pe_.Fori(1 if head else 0, turns) as i:
                        body(i, range(4))
                elif turns and not head:
                    body(0, range(4))
                if n % 4:
                    body(turns, range(n % 4))

            def product(out, s, col, rhs, first, last):
                if not isinstance(rhs, tuple):
                    w0 = s * UNIT + col
                    return nc.tensor.matmul(out, ring[:, w0:w0 + P], rhs, start=first, stop=last)
                xh, xl = rhs
                nc.tensor.matmul(out, whi(s, col, P), xh, start=first, stop=False)
                nc.tensor.matmul(out, whi(s, col, P), xl, start=False, stop=False)
                return nc.tensor.matmul(out, wlo(s, col, P), xh, start=False, stop=last)

            def unit_a(s, bank, rhs, ms=(0, 1), before=None, tile_ready=None):
                for m in ms:
                    for k in range(KT):
                        if m == 0 and before is not None:
                            pe_.wait_ge(tile_ready or h_tile, before + k + 1)
                        mm = product(psW[:, bank, m * T:(m + 1) * T], s, k * 256 + m * P, rhs(k), k == 0, k == KT - 1)
                return mm

            def unit_b(s, j, rhs):
                for k in range(32):
                    mm = product(psW[:, j // 2, 0:T], s, k * P, rhs(32 * (j % 2) + k),
                                 j % 2 == 0 and k == 0, j % 2 == 1 and k == 31)
                return mm

            def stat_sum(q, cis=range(CHUNK)):
                n = STATS[q]
                if q and 0 in cis:
                    pe_.wait_ge(stat_ms, q)
                for ci, (a, m) in enumerate(chunks_of(n)):
                    if ci not in cis:
                        continue
                    g = STAT_CHUNK0[q] + ci
                    pe_.wait_ge(stat_sq, g + 1)
                    for k in range(m):
                        mm = nc.tensor.matmul(psM[:, 3, 0:T], ones[:, :], tiles(W, CHUNK * (ci % 2) + k),
                                              start=(a + k == 0), stop=(a + k == n - 1))
                    mm.then_inc(stat_used, 1)

            def ada(a, b):
                with pe_.Fori(a, b) as i:
                    for j in range(4):
                        pe_.wait_ge(ada_sum, i * 4 + (j + 1))
                        pe_.wait_ge(bank_free, i * 4 + (j + 1))
                        for m in range(2):
                            o = psW[:, j, m:m + 1]
                            for k in range(ADA_DVE, KT):
                                c0 = j * UNIT + k * 256 + m * P
                                nc.tensor.matmul(o, ring[:, c0:c0 + P], csilu[:, k:k + 1], start=(k == ADA_DVE), stop=False)
                            for a_ in range(2):
                                mm = nc.tensor.matmul(o, ada_acc[:, j % 2, a_, m * P:(m + 1) * P], ones[:, 0:1],
                                                      start=False, stop=(a_ == 1))
                        mm.then_inc(w_used, 1)

            pe_.wait_ge(c_ready, 1)
            pe_.wait_ge(pool_const, 4)
            ada(0, 2)
            pe_.wait_ge(onehot_in, 16)
            table = onehot[:, SKEW_W + ASC_W:SKEW_W + ASC_W + HEADS]
            for h in range(HEADS):
                if h >= 4:
                    pe_.wait_ge(bias_sb, h - 3)
                nc.tensor.matmul(psM[:, h % 4, 0:SKEW_W], table[:, h:h + 1].to_broadcast([33, P]),
                                 onehot[:, 0:SKEW_W], start=True, stop=True).then_inc(bias_ps, 1)
            pe_.wait_ge(bank_free, 8 + 4)
            for qb in range(2):
                for n in range(N_CMP):
                    a = SKEW_W + ASC_0 + qb * P - 16 * n - 31
                    mm = nc.tensor.matmul(psW[:, 0, (qb * N_CMP + n) * 8:(qb * N_CMP + n) * 8 + 8],
                                          onehot[:, a:a + P], table, start=True, stop=True)
            mm.then_inc(bias_ps, 1)
            pe_.wait_ge(bias_sb, HEADS)
            pe_.wait_ge(cbias_sb, 1)

            ada(2, 3)
            stat_sum(0)
            ada(3, FIRST["w_in"] // 4)
            h_rhs = lambda k: tiles(H, k)
            h_split = lambda k: halves(H, k)
            from_h = lambda s, j: unit_a(s, j, h_split)
            stage("w_in", lambda s, j: unit_a(s, j, h_rhs), n=4,
                  head=lambda s, j: unit_a(s, j, h_rhs, before=0, tile_ready=h_first))

            def glu(s, j):
                for m in range(4):
                    for k in range(8):
                        mm = nc.tensor.matmul(psW[:, 2 * j + m // 2, (m % 2) * T:(m % 2 + 1) * T],
                                              ring[:, s * UNIT + k * 512 + m * P:s * UNIT + k * 512 + (m + 1) * P],
                                              tiles(J, k), start=(k == 0), stop=(k == 7))
                return mm
            pe_.wait_ge(bank_free, FIRST["w_in"] + 8)
            pe_.wait_ge(cmat_ready, 1)
            pe_.wait_ge(dyn_in, 16)
            for what, v in early_schedule():
                if what in ("half", "unit"):
                    u = FIRST["w_in"] + v
                    s = slot_of(u)[0]
                    if what == "half":
                        slot_ready(u, 0, 0)
                        pe_.wait_ge(bank_free, u + 1)
                        unit_a(s, v % 4, h_rhs, (0,))
                    else:
                        unit_a(s, v % 4, h_rhs, (1,)).then_inc(w_used, 1)
                elif what == "x":
                    ct, j = v // 4, v % 4
                    if j == 0:
                        pe_.wait_ge(bmat_in[ct % 4], 16 * (ct // 4 + 1))
                    if v >= 2:
                        pe_.wait_ge(x_read, v - 1)
                    for r in range(2):
                        mm = nc.tensor.matmul(psM[:, v % 2, r * T:(r + 1) * T],
                                              bmat[32 * j:32 * j + 32, ct % 4, r, :],
                                              J[32 * j:32 * j + 32, ct * T:(ct + 1) * T], start=True, stop=True)
                    mm.then_inc(x_ps, 1)
                elif what == "y":
                    ct, j = v // 4, v % 4
                    if j == 0:
                        pe_.wait_ge(diag_ready, ct + 1)
                        pe_.wait_ge(z_ready, ct) if ct else None
                        nc.tensor.matmul(psM[:, 2, 0:T], diag[:, :], tiles(J, ct), start=True, stop=False)
                    pe_.wait_ge(rotated, v + 1)
                    for r in range(2):
                        mm = nc.tensor.matmul(psM[32 * j:32 * j + 32, 2, 0:T], cmat[:, r, v, :], scanb[:, v % 2, r, :],
                                              start=False, stop=(r == 1))
                    mm.then_inc(scan_free, 1)
                elif what == "gates":
                    for qb in range(2):
                        for k in range(KT):
                            mm = nc.tensor.matmul(psM[:, 3, qb * 24:qb * 24 + 24],
                                                  H[:, k * T + qb * P:k * T + (qb + 1) * P], gate_w[:, k, :],
                                                  start=(k == 0), stop=(k == KT - 1))
                    mm.then_inc(gates_ps, 1)
                elif what == "cmp":
                    u = FIRST["cmp"] + v
                    if v == 0:
                        pe_.wait_ge(z_ready, 8)
                        stage("glu", glu)
                        pe_.wait_ge(bank_free, u + 4)
                        pe_.wait_ge(blk_ready, 1)
                    s = slot_ready(u, 0, 0)
                    kv, part_ = v // 2, v % 2
                    for m in range(2):
                        for o in range(16):
                            po = 16 * part_ + o
                            mm = product(psW[:, 2 * kv + m, 0:30], s, o * 256 + m * P,
                                         (blk16[:, 0, kv, po, :], blk16[:, 1, kv, po, :]), po == 0, po == 31)
                    mm.then_inc(w_used, 1)
            pe_.wait_ge(cmp_hid_sb, 2)
            pe_.wait_ge(gates_sb, 1)
            for m in range(2):
                nc.tensor.matmul(psM[:, 3, 0:30], w2[:, 0, m, :], cmp_hid[:, 0, m, :], start=(m == 0), stop=(m == 1))
            for g in range(2):
                for m in range(2):
                    mm = nc.tensor.matmul(psM[0:N_CMP, 3, 128 + 128 * g:256 + 128 * g], cmp_hid[:, 1, m, 15 * g:15 * g + 15],
                                          w2[:, 1, m, :], start=(m == 0), stop=(m == 1))
            mm.then_inc(cmp_ps, 1)

            pe_.wait_ge(cmp_sb, 2)
            stat_sum(1)
            pe_.wait_ge(bank_free, FIRST["w_out"] + 4)
            for b in range(2):
                for g in range(2):
                    for s2 in range(2):
                        tile = 16 + 4 * (b + 1) + 2 + g
                        mm = nc.tensor.transpose(psW[:, b, (2 * g + s2) * P:(2 * g + s2 + 1) * P],
                                                 J[:, tile * T + s2 * P:tile * T + (s2 + 1) * P], ident[:, :])
                mm.then_inc(v_ps, 1)
            pe_.wait_ge(v_sb, 2)

            def scores(r):
                h, qb = r // 2, r % 2
                g, nk = h // 4, P * (qb + 1)
                q = J[:, (8 + h) * T + qb * P:(8 + h) * T + (qb + 1) * P]
                if r >= 2:
                    pe_.wait_ge(logit_sb, r - 1)
                for b in range(2):
                    kt = 16 + 4 * (b + 1) + g
                    nc.tensor.matmul(psW[:, r % 2, b * 256:b * 256 + nk], q, J[:, kt * T:kt * T + nk],
                                     start=True, stop=True)
                nc.tensor.matmul(psM[:, r % 2, 0:N_CMP], q, kc[:, 15 * g:15 * g + 15],
                                 start=True, stop=True).then_inc(score_ps, 1)

            def prob_turn(r):
                h, qb = r // 2, r % 2
                pe_.wait_ge(prob_sb, r + 1)
                if r >= 1:
                    pe_.wait_ge(probT_sb, 2 * r)
                for b in range(2):
                    for s2 in range(qb + 1):
                        nc.tensor.transpose(psW[:, 2, (2 * b + s2) * P:(2 * b + s2 + 1) * P],
                                            logit[r % 3][:, b * 256 + s2 * P:b * 256 + (s2 + 1) * P], ident[:, :])
                nc.tensor.transpose(psM[0:N_CMP, 2, 0:P], logit[r % 3][:, 512:512 + N_CMP], ident[:, :])\
                    .then_inc(probT_ps, 1)

            def att_out(r):
                h, qb = r // 2, r % 2
                g = h // 4
                pe_.wait_ge(probT_sb, 2 * (r + 1))
                if r >= 1:
                    pe_.wait_ge(att_sb, r)
                first = True
                for b in range(2):
                    for s2 in range(qb + 1):
                        nc.tensor.matmul(psW[:, 3, 0:P], vnat[:, b, g, s2, :],
                                         probT[r % 2][:, (2 * b + s2) * P:(2 * b + s2 + 1) * P], start=first, stop=False)
                        first = False
                nc.tensor.matmul(psW[:, 3, 0:P], vc[:, g, :], probT[r % 2][0:N_CMP, 512:512 + P],
                                 start=False, stop=True).then_inc(att_ps, 1)

            pe_.wait_ge(skew_in, 16)
            for r in range(16 + 3):
                if r < 16:
                    scores(r)
                if 2 <= r <= 17:
                    prob_turn(r - 2)
                if r >= 3:
                    att_out(r - 3)
            stat_sum(2)
            pe_.wait_ge(mix_ready, 2)
            stage("w_out", lambda s, j: unit_a(s, j, h_split))
            stat_sum(3)
            stage("peer_q", from_h, head=lambda s, j: unit_a(s, j, h_split, before=0))
            pe_.wait_ge(bank_free, FIRST["u0"] + 4)
            pe_.wait_ge(dyn_in, 32)
            for c in range(8):
                qb = c // 4
                if c >= 2:
                    pe_.wait_ge(key_sb, c - 1)
                for s4 in range(4):
                    t = 2 * (2 * (c % 4) + s4 // 2) + s4 % 2
                    mm = nc.tensor.matmul(psM[:, c % 2, s4 * P:(s4 + 1) * P], J[:, t * T + qb * P:t * T + (qb + 1) * P],
                                          keys[:, s4 % 2, :], start=True, stop=True)
                mm.then_inc(key_ps, 1)

            def turn_picks(qb):
                pe_.wait_ge(picked, qb + 1)
                if qb:
                    pe_.wait_ge(pickT_sb, 1)
                for f in range(3):
                    mm = nc.tensor.transpose(psM[:, 2, f * P:(f + 1) * P], pick[:, f, :], ident[:, :])
                mm.then_inc(pickT_ps, 1)

            def two_sums(c):
                if c == 0:
                    pe_.wait_ge(stat_ms, 4)
                for f in range(2):
                    pe_.wait_ge(stat_sq, STAT_CHUNK0[4] + 2 * c + f + 1)
                    for k in range(CHUNK):
                        mm = nc.tensor.matmul(psM[:, 3 - f, 0:T], ones[:, :], tiles(W, CHUNK * f + k),
                                              start=(c + k == 0), stop=(c == 3 and k == CHUNK - 1))
                    mm.then_inc(stat_used, 1)

            def stage_sums(name, emit, q):
                stage(name, emit, n=24, lead=2)
                stat_sum(q, (0, 1))
                stage(name, emit, n=8, first=24, lead=2, drained=False)
                stat_sum(q, (2, 3))

            for half in range(2):
                if half == 0:
                    stage("u0", from_h, n=16)
                    turn_picks(0)
                    stage("u0", from_h, first=16, n=12, drained=False)
                    turn_picks(1)
                    stage("u0", from_h, first=28, n=4, drained=False)
                else:
                    stage("u1", from_h)
                pe_.wait_ge(bank_free, FIRST[f"v{half}"] + 4)
                with pe_.Fori(0, 16) as i:
                    for b in range(2):
                        n = i * 2 + (32 * half + b + 1)
                        pe_.wait_ge(hot2_ready, n)
                        pe_.wait_ge(hot1_ready, n)
                        pe_.wait_ge(route_used, n)
                        for t in range(8):
                            for r in range(2):
                                mm = nc.tensor.matmul(psM[:, b, t * 64:(t + 1) * 64], hot2[b][:, t, :], hot1[b][:, t, r, :],
                                                      start=(r == 0), stop=(r == 1))
                        mm.then_inc(hot_used, 1)
                pe_.wait_ge(route_used, 32 * (half + 1) + 2)
                pe_.wait_ge(acts_ready, 32 * (half + 1))
                experts_out = lambda s, j: unit_b(s, j, lambda k: (acts16[:, 0, k, :], acts16[:, 1, k, :]))
                if half == 0:
                    stage("v0", experts_out, lead=2)
                else:
                    for c in range(4):
                        stage("v1", experts_out, n=8, first=8 * c, lead=2, drained=(c == 0))
                        if c:
                            two_sums(c - 1)
                    two_sums(3)
            stage("z", from_h, head=lambda s, j: unit_a(s, j, h_split, before=KT))
            stage("gate", from_h, n=16)
            pe_.wait_ge(dyn_in, 48)
            pe_.wait_ge(pooled, 1)
            for g in range(4):
                mm = nc.tensor.matmul(psM[:, g // 2, (g % 2) * T:(g % 2 + 1) * T], pool_w[:, g, :], tiles(A, 60 + g),
                                      start=True, stop=True)
            mm.then_inc(pool_ps, 1)
            pe_.wait_ge(conv_done, 6)
            pe_.wait_ge(stat_ms, 6)
            for k in range(6):
                mm = nc.tensor.matmul(psM[:, 3, 0:T], ones[:, :], tiles(A, 54 + k), start=(k == 0), stop=(k == 5))
            mm.then_inc(ln_ps, 1)
            stage("gate", from_h, first=16, n=4, drained=False)
            pe_.wait_ge(ln_mu, 1)
            stat_sum(6)
            stage("gate", from_h, first=20, n=4, drained=False)

            pe_.wait_ge(va_split, 1)
            pe_.wait_ge(pool_split, 1)
            pe_.wait_ge(yc_ready, 1)
            mix_rhs = [halves(J, k) for k in (22, 23, 24, 25, 26, 27, 18, 19, 20, 21, 6, 7, 8, 9, 10, 11)]

            def abc(s, j):
                ps = psW if j % 2 == 0 else psM
                for b, (k0, k1) in enumerate(((0, 6), (6, 10), (10, 16))):
                    for m in range(2):
                        for k in range(k0, k1):
                            mm = product(ps[:, b, m * T:(m + 1) * T], s, k * 256 + m * P, mix_rhs[k], k == k0, k == k1 - 1)
                return mm
            stage("abc", abc, lead=3)
            pe_.wait_ge(merged, 1)
            stage("w_o", from_h)
            stat_sum(7)
            stage("up", from_h, head=lambda s, j: unit_a(s, j, h_split, before=2 * KT))
            pe_.wait_ge(relu_sb, 32 + 4)
            stage_sums("down", lambda s, j: unit_b(s, j, lambda k: halves(A, k)), 8)


        @block.vector
        def _(v):
            D = Chain(v, dve_seq)
            tt, ts, stt = v.tensor_tensor, v.tensor_scalar, v.scalar_tensor_tensor

            def low(u, i=0):
                for p2 in range(2):
                    v.wait_ge(hi_done, i * 8 + (2 * split_rank(u) + p2 + 1))
                    s, c, n = u % RAW, p2 * (UNIT // 2), UNIT // 2
                    ins = stt(wlo(s, c, n), ring[:, s * UNIT + c:s * UNIT + c + n], WSCALE, whi(s, c, n), ALU.mult, ALU.subtract)
                ins.then_inc(split_done, 1)

            def lows(name, put, per=0, first=0, n=None):
                u0 = FIRST[name] + first
                n = n if n is not None else dict(STREAM)[name] - first
                last = u0 + n == N_UNITS

                def body(i, last_turn=False):
                    for j in range(4):
                        if put:
                            put(i, j)
                        if not (last_turn and j >= 2):
                            low(u0 + j + 2, i)
                turns = n // 4 - last
                if turns > 1:
                    with D.loop(turns, per) as i:
                        body(i)
                elif turns:
                    body(0)
                if last:
                    body(turns, True)

            def squares(q, src, cis=range(CHUNK)):
                for ci, (a, m) in enumerate(chunks_of(STATS[q])):
                    if ci not in cis:
                        continue
                    g = STAT_CHUNK0[q] + ci
                    if g >= 2:
                        v.wait_ge(stat_used, g - 1)
                    tt(tiles(W, CHUNK * (ci % 2), m), src(a, m), src(a, m), ALU.mult).then_inc(stat_sq, 1)

            def inverse_rms(q):
                v.wait_ge(stat_used, STAT_CHUNK0[q] + len(chunks_of(STATS[q])))
                D.put(ts(rs[:, :], psM[:, 3, 0:T], 1.0 / (min(STATS[q], KT) * P), EPS, ALU.mult, ALU.add))
                D.wait()
                v.reciprocal(rs[:, :], rs[:, :]).then_inc(stat_ms, 1)
                v.wait_ge(stat_rs, q + 1)

            def par(k):
                return J[:, 4096 + 32 * k:4096 + 32 * (k + 1)]
            dt, lrdt, th, rnd, r, co, cos, sin, w_re, w_im, pr, pi, q1, q2, q3, npr, npi = (par(k) for k in range(17))
            lr, li = const("lam_re", 0, 32), const("lam_im", 0, 32)

            def step(ins):
                D.put(ins)
                D.wait()

            v.wait_ge(act_trig, 1)
            tt(lrdt, lr, dt, ALU.mult).then_inc(dve_trig, 1)
            step(tt(th, li, dt, ALU.mult))
            magic = 12582912.0
            c1 = 6.28125
            c2 = float(np.float32(int((2 * math.pi - c1) * 2 ** 20) / 2 ** 20))
            c3 = 2 * math.pi - c1 - c2
            step(ts(rnd, th, 1 / (2 * math.pi), magic, ALU.mult, ALU.add))
            step(ts(rnd, rnd, magic, None, ALU.subtract))
            step(stt(r, rnd, -c1, th, ALU.mult, ALU.add))
            step(stt(r, rnd, -c2, r, ALU.mult, ALU.add))
            step(stt(r, rnd, -c3, r, ALU.mult, ALU.add))
            step(ts(r, r, 3.1415925, -3.1415925, ALU.min, ALU.max))
            step(stt(co, r, -1.0, r, ALU.mult, ALU.max))
            ts(co, co, -1.0, math.pi / 2, ALU.mult, ALU.add).then_inc(dve_trig, 1)
            v.wait_ge(act_trig, 4)
            D.put(tt(q1, mag[:, :], cos, ALU.mult))
            step(tt(q2, mag[:, :], sin, ALU.mult))
            step(ts(q1, q1, 1.0, None, ALU.subtract))
            D.put(tt(w_re, q1, lr, ALU.mult))
            D.put(tt(q3, q2, li, ALU.mult))
            D.put(tt(w_im, q2, lr, ALU.mult))
            step(tt(npr, q1, li, ALU.mult))
            D.put(tt(w_re, w_re, q3, ALU.add))
            step(tt(w_im, w_im, npr, ALU.subtract))
            D.put(tt(q1, lr, lr, ALU.mult))
            step(tt(q2, li, li, ALU.mult))
            step(tt(q1, q1, q2, ALU.add))
            step(v.reciprocal(q1, q1))
            D.put(tt(w_re, w_re, q1, ALU.mult))
            D.put(tt(w_im, w_im, q1, ALU.mult))
            def ada(a_, b_):
                with D.loop(b_ - a_, 4 * (ADA_DVE - 1), a_) as i:
                    for j in range(4):
                        v.wait_ge(slot_full[j], i * 16 + 16)
                        if j >= 2:
                            v.wait_ge(w_used, i * 4 + (j - 1))
                        else:
                            v.wait_ge(bank_free, i * 4 + (j + 3))
                        for k in range(ADA_DVE):
                            row, acc = ring[:, j * UNIT + k * 256:j * UNIT + (k + 1) * 256], ada_acc[:, j % 2, k % 2, :]
                            if k < 2:
                                ins = ts(acc, row, csilu[:, k:k + 1], None, ALU.mult)
                            else:
                                D.wait(1)
                                ins = stt(acc, row, csilu[:, k:k + 1], acc, ALU.mult, ALU.add)
                            D.put(ins) if k < ADA_DVE - 1 else ins.then_inc(ada_sum, 1)

            v.wait_ge(c_ready, 1)
            ada(0, 3)
            v.wait_ge(x_in, 16)
            squares(0, lambda a, m: tiles(X, a, m))
            inverse_rms(0)
            ada(3, FIRST["w_in"] // 4)
            v.wait_ge(tab_ready, 1)
            v.wait_ge(bank_free, FIRST["w_in"] + 4)
            step(tt(mod[:, :], mod[:, :], const("b_ada", 0, 96), ALU.add))
            for g0 in (32, 80):
                D.put(ts(mod[:, g0:g0 + KT], mod[:, g0:g0 + KT], 1 / WSCALE, None, ALU.mult))
            step(stt(affine[:, :], mod[:, 16:32], 1.0, const("norm1_g", 0, 16), ALU.add, ALU.mult))
            for k in range(KT + 3):
                if k < KT:
                    D.put(stt(tiles(H, k), tiles(X, k), affine[:, k:k + 1], rs[:, :], ALU.mult, ALU.mult))
                if k >= 3:
                    D.wait(min(3, KT + 2 - k))
                    ts(tiles(H, k - 3), tiles(H, k - 3), mod[:, k - 3:k - 2], None, ALU.add).then_inc(h_first, 1)
            v.wait_ge(cmat_in, 16)
            cre, cim = cmat[:, 0, :, :], cmat[:, 1, :, :]
            t_a = X[:, 2048:3072].rearrange("p (i c) -> p i c", i=NSTATE_T)
            t_b = X[:, 3072:4096].rearrange("p (i c) -> p i c", i=NSTATE_T)
            wr = w_re.unsqueeze(2).to_broadcast([P, NSTATE_T, 32])
            wi = w_im.unsqueeze(2).to_broadcast([P, NSTATE_T, 32])
            D.put(tt(t_a, cim, wi, ALU.mult))
            D.put(tt(t_b, cre, wi, ALU.mult))
            D.wait()
            D.put(tt(cre, cre, wr, ALU.mult))
            D.put(tt(cim, cim, wr, ALU.mult))
            D.wait()
            D.put(tt(cre, cre, t_a, ALU.subtract))
            stt(cim, cim, -1.0, t_b, ALU.mult, ALU.subtract).then_inc(cmat_ready, 1)
            v.wait_ge(cmat_ready, 1)

            t1 = W[:, 0:512].rearrange("p (r t) -> p r t", r=2)
            t2 = W[:, 512:1024].rearrange("p (r t) -> p r t", r=2)
            with D.loop(8, 16) as c:
                for j in range(4):
                    v.wait_ge(x_ps, c * 4 + (j + 1))
                    cosv = A[:, bass.ds(c * 2048 + j * 512, T)].unsqueeze(1).to_broadcast([P, 2, T])
                    sinv = A[:, bass.ds(c * 2048 + (j * 512 + T), T)].unsqueeze(1).to_broadcast([P, 2, T])
                    xp = psM[:, j % 2, :].rearrange("p (r t) -> p r t", r=2)
                    D.put(tt(t1, xp, cosv, ALU.mult))
                    tt(t2, xp, sinv, ALU.mult).then_inc(x_read, 1)
                    D.wait()
                    v.wait_ge(x_read, c * 4 + (j + 1))
                    D.put(tt(t1[:, 0, :], t1[:, 0, :], t2[:, 1, :], ALU.add))
                    D.put(tt(t1[:, 1, :], t1[:, 1, :], t2[:, 0, :], ALU.subtract))
                    v.wait_ge(scan_free, c * 4 + (j + 1))
                    m = mag[:, bass.ds(c * 4 + j, 1)].to_broadcast([P, T])
                    D.wait(1)
                    D.put(v.tensor_tensor_scan(out=scanb[:, j % 2, 0, :], data0=m, data1=t1[:, 0, :], initial=0.0,
                                               op0=ALU.mult, op1=ALU.add))
                    D.wait(1)
                    v.tensor_tensor_scan(out=scanb[:, j % 2, 1, :], data0=m, data1=t1[:, 1, :], initial=0.0,
                                         op0=ALU.mult, op1=ALU.add).then_inc(scan_out, 1)
                    v.wait_ge(scan_out, c * 4 + (j + 1))

            v.wait_ge(dyn_in, 16)
            v.wait_ge(gates_ps, 1)
            v.wait_ge(bank_free, FIRST["glu"] + 4)
            for kv in range(2):
                for o in range(32):
                    src = J[:, (16 + 2 * kv) * T:(18 + 2 * kv) * T].rearrange("p (g n s) -> p g n s", g=2, s=16)
                    src = src[:, :, o // 16:o // 16 + N_CMP, o % 16]
                    ins = ts(blk[:, kv, o, :].rearrange("p (g n) -> p g n", g=2), src, pe[:, kv, o:o + 1], None, ALU.add)
            D.put(ins)
            v.wait_ge(rotated, NSTATE_T)
            D.wait()
            step(v.tensor_copy(W[:, 0:960].bitcast(F16), H[:, 0:1920]))
            tt(W[:, 960:1920].bitcast(F16), H[:, 0:1920], W[:, 0:960].bitcast(F16), ALU.subtract).then_inc(blk_ready, 1)
            for u in range(2):
                low(SPLIT_0 + u)

            v.wait_ge(glu_sb, 8)
            step(tt(J[:, 0:8 * T], J[:, 0:8 * T], glu_s, ALU.mult))
            lows("cmp", None)
            v.wait_ge(w_used, FIRST["w_out"])
            squares(1, lambda a, m: tiles(J, a, m))
            inverse_rms(1)

            def scale_rms(buf, k0, n, name, g0, signal=None):
                for k in range(n):
                    ins = stt(tiles(buf, k0 + k), tiles(buf, k0 + k), const(name, g0 + k), rs[:, :], ALU.mult, ALU.mult)
                    if k == n - 1 and signal is not None:
                        ins.then_inc(signal, 1)
                    else:
                        D.put(ins)
            def split(buf, k0, n, out, o0, signal):
                w = tiles(buf, k0, n).rearrange("p (m t) -> p m t", m=n)
                hl = tiles(out, o0, n).bitcast(F16).rearrange("p (m r t) -> p m r t", m=n, r=2)
                D.put(v.tensor_copy(hl[:, :, 0, :], w))
                D.wait()
                tt(hl[:, :, 1, :], w, hl[:, :, 0, :], ALU.subtract).then_inc(signal, 1)

            scale_rms(J, 0, 8, "beta", 0)
            D.wait()
            split(J, 0, 8, H, 0, mix_ready)

            v.wait_ge(skew_in, 16)
            v.wait_ge(gates_sb, 1)
            v.wait_ge(pool_const, 4)

            def views(r):
                nk = P * (r % 2 + 1)
                two = logit[r % 3][:, 0:512].rearrange("p (b s) -> p b s", b=2)[:, :, 0:nk]
                return nk, two, logit[r % 3][:, 512:512 + N_CMP]

            def logits(r):
                h, qb = r // 2, r % 2
                nk, two, lc = views(r)
                v.wait_ge(score_ps, r + 1)
                if r >= 3:
                    v.wait_ge(probT_ps, r - 2)
                ps = psW[:, r % 2, :].rearrange("p (b s) -> p b s", b=2)[:, :, 0:nk]
                D.put(stt(two, ps, SCALE, bias[:, h:h + 1, 256 - nk:256].to_broadcast([P, 2, nk]), ALU.mult, ALU.add))
                stt(lc, psM[:, r % 2, 0:N_CMP], SCALE, cbias[:, qb, :, h], ALU.mult, ALU.add).then_inc(logit_sb, 1)
                D.wait()
                D.put(v.tensor_reduce(mxb[:, r % 3, 0:2], two, AX_X, ALU.max))
                v.wait_ge(logit_sb, r + 1)
                D.put(v.tensor_reduce(mxb[:, r % 3, 2:3], lc, AX_X, ALU.max))
                D.wait()
                ts(mxb[:, r % 3, :], mxb[:, r % 3, :], -1.0, None, ALU.mult).then_inc(negmax, 1)

            def probs(r):
                h, qb = r // 2, r % 2
                nk, two, lc = views(r)
                v.wait_ge(exp_sb, 3 * (r + 1))
                step(v.reciprocal(smb[:, r % 3, :], smb[:, r % 3, :]))
                step(tt(smb[:, r % 3, :], smb[:, r % 3, :], gates[:, qb, h, :], ALU.mult))
                for b in range(2):
                    D.put(ts(two[:, b, :], two[:, b, :], smb[:, r % 3, b:b + 1], None, ALU.mult))
                stt(lc, lc, smb[:, r % 3, 2:3], cvalid[:, qb, :], ALU.mult, ALU.mult).then_inc(prob_sb, 1)

            for r in range(16 + 1):
                if r < 16:
                    logits(r)
                if r >= 1:
                    probs(r - 1)
            v.wait_ge(att_sb, 16)
            squares(2, lambda a, m: tiles(J, 8 + a, m))
            inverse_rms(2)
            scale_rms(J, 8, 8, "beta", 8)
            D.wait()
            split(J, 8, 8, H, 8, mix_ready)

            def residual_a(name, gain, first=0, n=None):
                u0 = FIRST[name] + first

                def put(i, j):
                    v.wait_ge(w_used, i * 4 + (u0 + j + 1))
                    if gain is None:
                        x = X[:, (2 * first + 2 * j) * T:(2 * first + 2 * j + 2) * T]
                        stt(x, psW[:, j, :], 1 / WSCALE, x, ALU.mult, ALU.add).then_inc(bank_free, 1)
                        return
                    for m in range(2):
                        k = 2 * first + 2 * j + m
                        ins = stt(tiles(X, k), psW[:, j, m * T:(m + 1) * T], mod[:, gain + k:gain + k + 1], tiles(X, k),
                                  ALU.mult, ALU.add)
                    ins.then_inc(bank_free, 1)
                lows(name, put, 0, first, 4)

            def residual_b(name, gain, first=0, n=None):
                u0, k0 = FIRST[name] + first, first // 2

                def put(i, j):
                    if j % 2:
                        v.wait_ge(w_used, i * 4 + (u0 + j + 1))
                        if isinstance(i, int):
                            k = k0 + 2 * i + j // 2
                            x, g = tiles(X, k), gain if isinstance(gain, float) else mod[:, gain + k:gain + k + 1]
                        else:
                            k = k0 + j // 2
                            x = X[:, bass.ds(i * 2 * T + k * T, T)]
                            g = gain if isinstance(gain, float) else mod[:, bass.ds(i * 2 + (gain + k), 1)]
                        stt(x, psW[:, j // 2, 0:T], g, x, ALU.mult, ALU.add).then_inc(bank_free, 2)
                lows(name, put, 0, first, n)

            def residual_squares(name, gain, q):
                for first, n, cis in ((0, 16, (0, 1)), (16, 8, (2,)), (24, 8, (3,))):
                    residual_b(name, gain, first, n)
                    v.wait_ge(bank_free, FIRST[name] + first + n + 4)
                    squares(q, lambda a, m: tiles(X, a, m), cis)

            def norm_split(col, shift, before):
                def lo(k):
                    v.wait_ge(t_hi, before + k + 1)
                    w = tiles(W, k % 8)
                    if shift is None:
                        ins = tt(halves(H, k)[1], w, halves(H, k)[0], ALU.subtract)
                    else:
                        ins = stt(halves(H, k)[1], w, mod[:, shift + k:shift + k + 1], halves(H, k)[0], ALU.add, ALU.subtract)
                    ins.then_inc(h_tile, 1)
                for k in range(KT + 3):
                    if k < KT:
                        if k >= 8:
                            v.wait_ge(h_tile, before + k - 7)
                        stt(tiles(W, k % 8), tiles(X, k), col(k), rs[:, :], ALU.mult, ALU.mult).then_inc(t_raw, 1)
                    if k >= 3:
                        lo(k - 3)

            v.wait_ge(x_in, 32)
            for first in (0, 4):
                residual_a("w_out", 32, first)
                v.wait_ge(bank_free, FIRST["w_out"] + first + 8)
                squares(3, lambda a, m: tiles(X, a, m), (first // 2, first // 2 + 1))
            inverse_rms(3)
            step(stt(affine[:, :], mod[:, 64:80], 1.0, const("norm2_g", 0, 16), ALU.add, ALU.mult))
            norm_split(lambda k: affine[:, k:k + 1], 48, 0)
            lows("peer_q", None)

            io16 = iota[:, 0:16].unsqueeze(1).unsqueeze(1)
            v.wait_ge(iota_ready, 1)
            def select(qb):
                v.wait_ge(key_sb, 8)
                for h in range(HEADS):
                    s4 = key_scores(4 * qb + h // 2)
                    for f in range(2):
                        s = s4[:, (h % 2) * 2 + f, :]
                        step(v.max(val[:, h, f, 0:8], s))
                        step(v.max_index(idx[:, h, f, 0:8], val[:, h, f, 0:8], s))
                        step(v.match_replace(s, val[:, h, f, 0:8], s, -3e38))
                        step(v.max(val[:, h, f, 8:16], s))
                        step(v.max_index(idx[:, h, f, 8:16], val[:, h, f, 8:16], s))
                    yield
                for h in range(HEADS):
                    D.put(tt(cand[:, h, :, :], val[:, h, 0, :].unsqueeze(2).to_broadcast([P, TOPK, TOPK]),
                             val[:, h, 1, :].unsqueeze(1).to_broadcast([P, TOPK, TOPK]), ALU.add))
                D.put(v.tensor_copy(sel[:, 512:768], sel[:, 256:512].bitcast(U32)))
                D.wait()
                for h in range(HEADS):
                    cf = cand[:, h, :, :].rearrange("p a b -> p (a b)")
                    ci = cidx[:, h * TOPK:(h + 1) * TOPK]
                    step(v.max(cval[:, h, 0:8], cf))
                    step(v.max_index(ci[:, 0:8], cval[:, h, 0:8], cf))
                    step(v.match_replace(cf, cval[:, h, 0:8], cf, -3e38))
                    step(v.max(cval[:, h, 8:16], cf))
                    step(v.max_index(ci[:, 8:16], cval[:, h, 8:16], cf))
                    if h % 4 == 3:
                        yield
                if qb:
                    v.wait_ge(pickT_ps, 1)
                pgate = pick[:, 2, :].rearrange("p (h k) -> p h k", h=HEADS)
                tt(pgate, cval, cval[:, :, 0:1].to_broadcast([P, HEADS, TOPK]), ALU.subtract).then_inc(topv, 1)
                D.put(ts(part[:, 0, :], cidx, 4, None, ALU.logical_shift_right))
                D.put(ts(part[:, 1, :], cidx, 15, None, ALU.bitwise_and))
                D.wait()
                step(v.tensor_copy(sel[:, 1280:1536], sel[:, 1024:1280].bitcast(U32)))
                for f in range(2):
                    step(tt(cand, partf[:, f, :, :].unsqueeze(3).to_broadcast([P, HEADS, TOPK, TOPK]),
                            io16.to_broadcast([P, HEADS, TOPK, TOPK]), ALU.is_equal))
                    yield
                    step(tt(cand, cand, idxf[:, :, f, :].unsqueeze(2).to_broadcast([P, HEADS, TOPK, TOPK]), ALU.mult))
                    step(v.tensor_reduce(pick[:, f, :].rearrange("p (h k) -> p h k", h=HEADS), cand, AX_X, ALU.add))
                v.wait_ge(gexp, qb + 1)
                step(v.tensor_reduce(gsum, pgate, AX_X, ALU.add))
                step(v.reciprocal(gsum, gsum))
                tt(pgate, pgate,
                   gsum.unsqueeze(2).to_broadcast([P, HEADS, TOPK]), ALU.mult).then_inc(picked, 1)
                yield

            assert SELECT_PIECES * 2 <= 32
            pieces = [select(0), select(1)]
            for u in range(32):
                if u < 2 * SELECT_PIECES:
                    next(pieces[u // SELECT_PIECES])
                low(FIRST["u0"] + u + 2)

            v.wait_ge(pickT_sb, 2)
            acts = A[:, :].rearrange("p (e t) -> p t e", e=EXP_T)
            D.put(v.tensor_copy(J[:, 2048:2304].bitcast(F16), W[:, 1024:1536]))
            D.put(v.tensor_copy(iota16, iota[:, :]))
            step(ts(g16[:, 0, :], pickT[:, 2, :], GSCALE, None, ALU.mult))
            step(stt(g16[:, 1, :], pickT[:, 2, :], GSCALE, g16[:, 0, :], ALU.mult, ALU.subtract))
            for half in range(2):
                v.wait_ge(bank_free, FIRST[f"v{half}"] + 4)

                def hot(i, b, turn):
                    def cols(f, n):
                        a0 = 8 * b + 16 * turn
                        c = e16[:, f, a0:a0 + 8] if i is None else e16[:, f, bass.ds(i * 16 + a0, 8)]
                        return c.unsqueeze(2).to_broadcast([P, 8, n])
                    step_n = 32 * half + 2 * turn + b + 1
                    v.wait_ge(hot_used, step_n if i is None else i * 2 + step_n)
                    tt(first1[b], iota16[:, 64 * half:64 * half + 64].unsqueeze(1).to_broadcast([P, 8, 64]),
                       cols(0, 64), ALU.is_equal).then_inc(first1_ready, 1)
                    tt(hot2[b], iota16.unsqueeze(1).to_broadcast([P, 8, P]), cols(1, P), ALU.is_equal).then_inc(hot2_ready, 1)

                def gated(i, b):
                    v.wait_ge(hot_used, i * 2 + (32 * half + b + 3))
                    w = W[:, 512 * b:512 * (b + 1)].rearrange("p (t e) -> p t e", t=8)
                    tok = slice(8 * (2 * i + b), 8 * (2 * i + b) + 8) if isinstance(i, int) else bass.ds(i * 16 + 8 * b, 8)
                    stt(w, psM[:, b, :].rearrange("p (t e) -> p t e", t=8), 1 / GSCALE, acts[:, tok, :], ALU.mult, ALU.mult)\
                        .then_inc(route_used, 1)

                def gated_low(i, b):
                    tok = slice(8 * (2 * i + b), 8 * (2 * i + b) + 8) if isinstance(i, int) else bass.ds(i * 16 + 8 * b, 8)
                    hl = acts16[:, :, :, tok].rearrange("p r e t -> p r t e")
                    w = W[:, 512 * b:512 * (b + 1)].rearrange("p (t e) -> p t e", t=8)
                    v.wait_ge(route_hi, i * 2 + (32 * half + b + 1))
                    tt(hl[:, 1, :, :], w, hl[:, 0, :, :], ALU.subtract).then_inc(acts_ready, 1)

                for b in range(2):
                    hot(None, b, 0)
                with D.loop(15, 0) as i:
                    for b in range(2):
                        gated(i, b)
                        hot(i, b, 1)
                        gated_low(i, b)
                    v.wait_ge(acts_ready, i * 2 + (32 * half + 2))
                for b in range(2):
                    gated(15, b)
                    gated_low(15, b)
                if half == 0:
                    residual_b("v0", 80)
                    lows("u1", None)
                else:
                    for c in range(4):
                        residual_b("v1", 80, 8 * c, 8)
                        v.wait_ge(bank_free, FIRST["v1"] + 8 * c + 8 + 4)
                        for f in range(2):
                            g = STAT_CHUNK0[4] + 2 * c + f
                            v.wait_ge(stat_used, g - 1)
                            x = tiles(X, CHUNK * c, CHUNK)
                            tt(tiles(W, CHUNK * f, CHUNK), x, x, ALU.mult).then_inc(stat_sq, 1)
                            if f == 0:
                                v.wait_ge(stat_sq, g + 1)
                                for k in range(CHUNK * c, CHUNK * c + CHUNK):
                                    D.put(ts(tiles(X, k), tiles(X, k), const("final_g", k), None, ALU.mult))
                                D.wait()
            inverse_rms(4)
            rs_final = tiles(A, 47)
            D.put(v.tensor_copy(rs_final, rs[:, :]))
            step(stt(tiles(A, 46), psM[:, 2, 0:T], 1.0 / D_MODEL, rs[:, :], ALU.mult, ALU.mult))
            step(tt(rs[:, :], tiles(A, 46), rs[:, :], ALU.mult))
            step(ts(rs[:, :], rs[:, :], EPS, None, ALU.add))
            v.reciprocal(rs[:, :], rs[:, :]).then_inc(stat_ms, 1)
            v.wait_ge(stat_rs, 6)
            step(tt(rs[:, :], rs[:, :], rs_final, ALU.mult))
            norm_split(lambda k: const("g_mix", k), None, KT)
            D.wait()
            v.wait_ge(h_tile, 2 * KT)
            for n in range(17):
                if n < 4:
                    x = tiles(X, 4 * n, 4).rearrange("p (k t) -> p k t", k=4)
                    D.put(tt(x, x, rs_final.unsqueeze(1).to_broadcast([P, 4, T]), ALU.mult))
                low(FIRST["z"] + n + 2)

            def branches():
                v.wait_ge(bank_free, FIRST["gate"] + 4)
                step(tt(tiles(J, 22, 6), tiles(J, 22, 6), tiles(A, 48, 6), ALU.mult))
                for k in range(6):
                    D.put(ts(tiles(A, 54 + k), tiles(J, 22 + k), const("w_dw_a", 31 * k + 30), const("b_dw_a", k),
                             ALU.mult, ALU.add))
                for tap in range(29, -1, -1):
                    d = 30 - tap
                    for k in range(6):
                        o = A[:, (54 + k) * T + d:(55 + k) * T]
                        D.wait(5 if tap else 5 - k)
                        ins = stt(o, J[:, (22 + k) * T:(23 + k) * T - d], const("w_dw_a", 31 * k + tap), o,
                                  ALU.mult, ALU.add)
                        if tap:
                            D.put(ins)
                        else:
                            ins.then_inc(conv_done, 1)
                    if tap % 3 == 0:
                        yield
                step(tt(tiles(J, 6, 6), tiles(J, 6, 6), tiles(J, 12, 6), ALU.mult))
                for k in range(6):
                    D.put(ts(tiles(J, 12 + k), tiles(J, 6 + k), const("w_dw_c", 3 * k + 2), None, ALU.mult))
                yield
                for tap in (1, 0):
                    d = 2 - tap
                    for k in range(6):
                        o = J[:, (12 + k) * T + d:(13 + k) * T]
                        D.wait(5)
                        D.put(stt(o, J[:, (6 + k) * T:(7 + k) * T - d], const("w_dw_c", 3 * k + tap), o, ALU.mult, ALU.add))
                yield
                D.wait()
                step(tt(tiles(J, 12, 6), tiles(J, 0, 6), tiles(J, 12, 6), ALU.mult))
                split(J, 12, 6, J, 6, yc_ready)
                v.wait_ge(yc_ready, 1)
                yield
                yield
                yield
                yield
                v.wait_ge(ln_ps, 1)
                step(ts(rs[:, :], psM[:, 3, 0:T], 1.0 / 768, None, ALU.mult))
                v.wait_ge(conv_done, 6)
                va = tiles(A, 54, 6).rearrange("p (k t) -> p k t", k=6)
                rs6 = rs[:, :].unsqueeze(1).to_broadcast([P, 6, T])
                tt(va, va, rs6, ALU.subtract).then_inc(ln_mu, 1)
                v.wait_ge(ln_mu, 1)
                v.wait_ge(pooled, 1)
                squares(6, lambda a, m: tiles(A, 54 + a, m))
                yield
                v.wait_ge(pool_sb, 4)
                split(J, 0, 4, J, 18, pool_split)
                yield
                yield
                yield
                inverse_rms(6)
                tt(va, va, rs6, ALU.mult).then_inc(ln_x, 1)
                yield
                v.wait_ge(va_ready, 6)
                split(J, 12, 6, J, 22, va_split)
                yield

            pieces = branches()
            for n in range(24):
                next(pieces, None)
                low(FIRST["gate"] + n + 2)
            assert next(pieces, "end") == "end"

            u0 = FIRST["abc"]
            v.wait_ge(bank_free, u0 + 4)
            def merge(i, j):
                ps = psW if j % 2 == 0 else psM
                D.wait()
                v.wait_ge(w_used, i * 4 + (u0 + j + 1))
                for b in range(3):
                    g = A[:, bass.ds(i * 8 * T + (16 * b + 2 * j) * T, 2 * T)]
                    ins = stt(tiles(W, 2 * b, 2), ps[:, b, :], 1 / WSCALE, g, ALU.mult, ALU.mult)
                    if b < 2:
                        D.put(ins)
                    else:
                        ins.then_inc(bank_free, 1)
                D.wait()
                D.put(tt(tiles(W, 0, 2), tiles(W, 0, 2), tiles(W, 2, 2), ALU.add))
                D.wait()
                v.wait_ge(bank_free, i * 4 + (u0 + j + 5))
                step(tt(tiles(W, 0, 2), tiles(W, 0, 2), tiles(W, 4, 2), ALU.add))
                w = tiles(W, 0, 2).rearrange("p (m t) -> p m t", m=2)
                hl = H[:, :].bitcast(F16)[:, bass.ds(i * 4096 + j * 1024, 1024)].rearrange("p (m r t) -> p m r t", m=2, r=2)
                step(v.tensor_copy(hl[:, :, 0, :], w))
                D.put(tt(hl[:, :, 1, :], w, hl[:, :, 0, :], ALU.subtract))
            lows("abc", merge, 24)
            D.wait()
            v.sem_inc(merged, 1)

            for first in (0, 4):
                residual_a("w_o", None, first)
                v.wait_ge(bank_free, FIRST["w_o"] + first + 8)
                squares(7, lambda a, m: tiles(X, a, m), (first // 2, first // 2 + 1))
            inverse_rms(7)
            norm_split(lambda k: const("g_mlp", k), None, 2 * KT)
            u0 = FIRST["up"]

            def square(i, j):
                w = tiles(W, 2 * j, 2).rearrange("p (m t) -> p m t", m=2)
                hl = A[:, :].bitcast(F16)[:, bass.ds(i * 4096 + j * 1024, 1024)].rearrange("p (m r t) -> p m r t", m=2, r=2)
                v.wait_ge(bank_free, i * 4 + (u0 + j + 5))
                D.put(tt(w, w, w, ALU.mult))
                D.wait()
                D.put(v.tensor_copy(hl[:, :, 0, :], w))
                D.wait()
                tt(hl[:, :, 1, :], w, hl[:, :, 0, :], ALU.subtract).then_inc(relu_sb, 1)
            lows("up", square, 8)
            residual_squares("down", 1 / (WSCALE * HSCALE ** 2), 8)
            inverse_rms(8)
            for c in range(4):
                scale_rms(X, 4 * c, 4, "g_final", 4 * c, out_ready)

        @block.scalar
        def _(a):
            act = a.activation
            S = Chain(a, act_seq)

            def root(q):
                a.wait_ge(stat_ms, q + 1)
                act(rs[:, :], rs[:, :], ACT.Sqrt).then_inc(stat_rs, 1)

            def hi(u, i=0):
                s, n = slot_of(u)
                a.wait_ge(slot_full[s], i * 32 + 16 * n)
                a.wait_ge(w_used, i * 4 + (u - 1))
                for p2 in range(2):
                    c = slice(s * UNIT + p2 * (UNIT // 2), s * UNIT + (p2 + 1) * (UNIT // 2))
                    act(whi(s, p2 * (UNIT // 2), UNIT // 2), ring[:, c], ACT.Copy, scale=WSCALE).then_inc(hi_done, 1)

            def his(name, put, n=None, first=0):
                u0 = FIRST[name] + first
                n = n if n is not None else dict(STREAM)[name] - first
                last = u0 + n == N_UNITS

                def body(i, last_turn=False):
                    for j in range(4):
                        if put:
                            a.wait_ge(w_used, i * 4 + (u0 + j + 1))
                            put(i, j).then_inc(bank_free, 1)
                        if not (last_turn and j >= 2):
                            hi(u0 + j + 2, i)
                turns = n // 4 - last
                if turns > 1:
                    with a.Fori(0, turns) as i:
                        body(i)
                elif turns:
                    body(0)
                if last:
                    body(turns, True)

            def take(name, put, n=None, first=0, loop=True):
                u0 = FIRST[name] + first
                n = n if n is not None else dict(STREAM)[name] - first

                def body(i, js):
                    for j in js:
                        a.wait_ge(w_used, i * 4 + (u0 + j + 1))
                        put(i, j).then_inc(bank_free, 1)
                if n >= 8:
                    with a.Fori(0, n // 4) as i:
                        body(i, range(4))
                elif n >= 4:
                    body(0, range(4))
                if n % 4:
                    body(n // 4, range(n % 4))

            def into(buf, func, j0=0, scale=1.0):
                return lambda i, j: act(buf[:, bass.ds(i * 4 * 512 + (j0 + j) * 512, 512)]
                                        if not isinstance(i, int) else buf[:, (4 * i + j0 + j) * 512:(4 * i + j0 + j + 1) * 512],
                                        psW[:, j, :], func, scale=scale)

            def par(k):
                return J[:, 4096 + 32 * k:4096 + 32 * (k + 1)]
            dt, lrdt, th, rnd, r_, co, cos, sin = (par(k) for k in range(8))
            a.wait_ge(cst_in, 16)
            act(csilu[:, :], const("c", 0, KT), ACT.Silu).then_inc(c_ready, 1)
            act(dt, const("log_dt", 0, 32), ACT.Exp).then_inc(act_trig, 1)
            a.wait_ge(dve_trig, 1)
            act(mag[:, :], lrdt, ACT.Exp).then_inc(act_trig, 1)
            a.wait_ge(dve_trig, 2)
            act(sin, r_, ACT.Sin).then_inc(act_trig, 1)
            act(cos, co, ACT.Sin).then_inc(act_trig, 1)

            def ada(i, j):
                return act(mod[:, bass.ds(i * 8 + 2 * j, 2)], psW[:, j, 0:2], ACT.Copy)

            def take_ada(a_, b_):
                with a.Fori(a_, b_) as i:
                    for j in range(4):
                        a.wait_ge(w_used, i * 4 + (j + 1))
                        ada(i, j).then_inc(bank_free, 1)
            take_ada(0, 2)
            for h in range(HEADS):
                a.wait_ge(bias_ps, h + 1)
                act(skew_sb[:, h * SKEW_W:(h + 1) * SKEW_W], psM[:, h % 4, 0:SKEW_W], ACT.Copy).then_inc(bias_sb, 1)
            a.wait_ge(bias_ps, HEADS + 1)
            act(cbias.rearrange("p q n h -> p (q n h)"), psW[:, 0, 0:240], ACT.Copy).then_inc(cbias_sb, 1)
            take_ada(2, 3)
            root(0)
            take_ada(3, FIRST["w_in"] // 4)
            a.wait_ge(cmat_ready, 1)
            for ct in range(4):
                a.dma_start(bmat[:, ct, :, :], bmat_d[:, ct, :, :]).then_inc(bmat_in[ct], 16)
            a.wait_ge(pool_const, 4)
            a.wait_ge(dyn_in, 16)
            a.wait_ge(skew_out, 16)
            take("w_in", into(J, ACT.Copy), n=4)
            act(diag[:, :], ident[:, :], ACT.Copy, scale=const("d_skip", 0)).then_inc(diag_ready, 1)
            for what, n in early_schedule():
                if what == "unit":
                    a.wait_ge(w_used, FIRST["w_in"] + n + 1)
                    act(J[:, n * 512:(n + 1) * 512], psW[:, n % 4, :], ACT.Copy).then_inc(bank_free, 1)
                elif what == "y" and n % 4 == 3:
                    ct = n // 4
                    a.wait_ge(scan_free, 2 + n + 1)
                    act(tiles(J, ct), psM[:, 2, 0:T], ACT.Gelu_apprx_tanh).then_inc(z_ready, 1)
                    if ct < 4:
                        a.dma_start(bmat[:, ct, :, :], bmat_d[:, ct + 4, :, :]).then_inc(bmat_in[ct], 16)
                    if ct < 7:
                        act(diag[:, :], ident[:, :], ACT.Copy, scale=const("d_skip", ct + 1)).then_inc(diag_ready, 1)
                elif what == "gates":
                    a.wait_ge(gates_ps, 1)
                    act(gates.rearrange("p q h c -> p (q h c)"), psM[:, 3, 0:48], ACT.Sigmoid).then_inc(gates_sb, 1)
                    a.dma_start(bias, bass_skew(skew_d)).then_inc(skew_in, 16)
                elif what == "cmp":
                    if n == 0:
                        for u in range(2):
                            a.wait_ge(w_used, FIRST["glu"] + u + 1)
                            for m in range(4):
                                k = 4 * u + m
                                act(glu_s[:, k * T:(k + 1) * T], psW[:, 2 * u + m // 2, (m % 2) * T:(m % 2 + 1) * T], ACT.Sigmoid,
                                    bias=const("b_glu", k)).then_inc(glu_sb, 1)
                            a.wait_ge(glu_sb, 4 * (u + 1))
                            a.sem_inc(bank_free, 1)
                            hi(SPLIT_0 + u)
                    if n % 2:
                        kv = n // 2
                        a.wait_ge(w_used, FIRST["cmp"] + n + 1)
                        act(cmp_hid[:, kv, :, :], psW[:, 2 * kv:2 * kv + 2, 0:30], ACT.Gelu_apprx_tanh, scale=1 / WSCALE)\
                            .then_inc(cmp_hid_sb, 1)
                        a.wait_ge(cmp_hid_sb, kv + 1)
                        a.sem_inc(bank_free, 2)
                    hi(FIRST["cmp"] + n + 2)
            a.wait_ge(cmp_ps, 1)
            act(kc, psM[:, 3, 0:30], ACT.Copy).then_inc(cmp_sb, 1)
            act(vc.rearrange("p g d -> p (g d)"), psM[0:N_CMP, 3, 128:384], ACT.Copy).then_inc(cmp_sb, 1)
            root(1)
            for b in range(2):
                a.wait_ge(v_ps, b + 1)
                act(vnat[:, b, :, :, :].rearrange("p g s d -> p (g s d)"), psW[:, b, :], ACT.Copy).then_inc(v_sb, 1)
            for r in range(16 + 2):
                if r < 16:
                    nk = P * (r % 2 + 1)
                    a.wait_ge(negmax, r + 1)
                    for b in range(3):
                        l = logit[r % 3][:, b * 256:b * 256 + (nk if b < 2 else N_CMP)]
                        act(l, l, ACT.Exp, bias=mxb[:, r % 3, b:b + 1], accum_out=smb[:, r % 3, b:b + 1]).then_inc(exp_sb, 1)
                if 1 <= r <= 16:
                    q = r - 1
                    w = P * (q % 2 + 1)
                    a.wait_ge(probT_ps, q + 1)
                    src = psW[:, 2, :].rearrange("p (b s) -> p b s", b=2)[:, :, 0:w]
                    dst = probT[q % 2][:, 0:512].rearrange("p (b s) -> p b s", b=2)[:, :, 0:w]
                    if q >= 2:
                        a.wait_ge(att_ps, q - 1)
                    act(dst, src, ACT.Copy).then_inc(probT_sb, 1)
                    act(probT[q % 2][0:N_CMP, 512:640], psM[0:N_CMP, 2, 0:P], ACT.Copy).then_inc(probT_sb, 1)
                if r >= 2:
                    q = r - 2
                    h, qb = q // 2, q % 2
                    a.wait_ge(att_ps, q + 1)
                    act(J[:, (8 + h) * T + qb * P:(8 + h) * T + (qb + 1) * P], psW[:, 3, 0:P], ACT.Copy).then_inc(att_sb, 1)
            root(2)
            def high(n, shift):
                for k in range(KT):
                    a.wait_ge(t_raw, KT * n + k + 1)
                    b = {} if shift is None else {"bias": mod[:, shift + k:shift + k + 1]}
                    act(halves(H, k)[0], tiles(W, k % 8), ACT.Copy if shift is None else ACT.Identity, **b).then_inc(t_hi, 1)
            his("w_out", None)
            root(3)
            high(0, 48)
            his("peer_q", into(J, ACT.Copy, scale=1 / WSCALE))
            for c in range(8):
                a.wait_ge(key_ps, c + 1)
                act(key_scores(c).rearrange("p s n -> p (s n)"), psM[:, c % 2, :], ACT.Copy).then_inc(key_sb, 1)
            for u in range(32):
                a.wait_ge(w_used, FIRST["u0"] + u + 1)
                act(A[:, u * 512:(u + 1) * 512], psW[:, u % 4, :], ACT.Gelu_apprx_tanh, scale=1 / WSCALE).then_inc(bank_free, 1)
                hi(FIRST["u0"] + u + 2)
                for qb in range(2):
                    if u == SELECT_PIECES * (qb + 1) - 3:
                        a.wait_ge(topv, qb + 1)
                        act(pick[:, 2, :], pick[:, 2, :], ACT.Exp).then_inc(gexp, 1)
                    if u == 15 + 12 * qb:
                        a.wait_ge(pickT_ps, qb + 1)
                        act(pickT[:, :, qb * P:(qb + 1) * P], psM[:, 2, 0:3 * P].rearrange("p (f t) -> p f t", f=3), ACT.Copy)\
                            .then_inc(pickT_sb, 1)
            for half in range(2):
                if half:
                    his("u1", into(A, ACT.Gelu_apprx_tanh, scale=1 / WSCALE))
                with a.Fori(0, 16) as i:
                    for b in range(2):
                        a.wait_ge(route_used, i * 2 + (32 * half + b + 3))
                        act(acts16[:, 0, :, bass.ds(i * 16 + 8 * b, 8)].rearrange("p e t -> p t e"),
                            W[:, 512 * b:512 * (b + 1)].rearrange("p (t e) -> p t e", t=8), ACT.Copy).then_inc(route_hi, 1)
                his(f"v{half}", None)
            root(4)
            root(5)
            high(1, None)
            for n in range(17):
                a.wait_ge(w_used, FIRST["z"] + n + 1)
                bank = n % 4 if n < 16 else 0
                if n < 11:
                    act(J[:, n * 512:(n + 1) * 512], psW[:, bank, :], ACT.Copy, scale=1 / WSCALE).then_inc(bank_free, 1)
                else:
                    for m in range(2):
                        k = 2 * (n - 11) + m
                        dst = tiles(J, 22 + k) if k < 6 else tiles(A, 48 + k - 6)
                        ins = act(dst, psW[:, bank, m * T:(m + 1) * T], ACT.Identity if k < 6 else ACT.Sigmoid,
                                  bias=const("b_glu2", k), scale=1 / WSCALE)
                    ins.then_inc(bank_free, 1)
                hi(FIRST["z"] + n + 2)
            for n in range(24):
                a.wait_ge(w_used, FIRST["gate"] + n + 1)
                for m in range(2):
                    k = 2 * n + m
                    ins = act(tiles(A, k), psW[:, n % 4, m * T:(m + 1) * T], ACT.Sigmoid, bias=const("b_gate", k),
                              scale=1 / WSCALE)
                ins.then_inc(bank_free, 1)
                hi(FIRST["gate"] + n + 2)
                if n == 15:
                    a.wait_ge(yc_ready, 1)
                    a.wait_ge(pool_ps, 1)
                    for g in range(4):
                        act(tiles(J, g), psM[:, g // 2, (g % 2) * T:(g % 2 + 1) * T], ACT.Copy,
                            scale=const("pool_scale", g)).then_inc(pool_sb, 1)
                if n == 20:
                    root(6)
                    a.wait_ge(ln_x, 1)
                    for k in range(6):
                        act(tiles(J, 12 + k), tiles(A, 54 + k), ACT.Silu, scale=const("ln_g", k), bias=const("ln_b", k))\
                            .then_inc(va_ready, 1)
            his("abc", None)
            his("w_o", None)
            root(7)
            high(2, None)
            def relu(i, j):
                a.wait_ge(relu_sb, i * 4 + (j + 1))
                return act(tiles(W, 2 * j, 2), psW[:, j, :], ACT.Relu, scale=HSCALE / WSCALE)
            his("up", relu)
            his("down", None)
            root(8)

        @block.gpsimd
        def _(g):
            G = Chain(g, pool_seq)
            g.dma_start(cst[:, :], cst_d).then_inc(cst_in, 16)
            g.dma_start(onehot, onehot_d).then_inc(onehot_in, 16)
            g.dma_start(X[:, :], xT_d.rearrange("p k t -> p (k t)")).then_inc(x_in, 16)
            g.dma_start(dyn[:, 0:960], dyn1_d).then_inc(dyn_in, 16)
            G.put(g.memset(ident[:, :], 0.0))
            G.put(g.memset(cvalid.rearrange("p q n -> p (q n)"), 1.0))
            g.memset(ones[:, :], 1.0).then_inc(pool_const, 2)
            G.wait()
            g.affine_select(out=ident[:, :], in_=ident[:, :], compare_op=ALU.not_equal, fill=1.0, base=0,
                            pattern=[[-1, P]], channel_multiplier=1).then_inc(pool_const, 1)
            g.affine_select(out=cvalid, in_=cvalid, compare_op=ALU.is_ge, fill=0.0, base=-31,
                            pattern=[[P, 2], [-16, N_CMP]], channel_multiplier=1).then_inc(pool_const, 1)
            g.sem_inc(bank_free, 4)
            g.sem_inc(scan_free, 2)
            g.sem_inc(hot_used, 2)
            g.sem_inc(relu_sb, 4)
            g.sem_inc(route_used, 2)
            par = lambda k: J[:, 4096 + 32 * k:4096 + 32 * (k + 1)]
            cos, sin, pr, pi, npr, q1 = par(6), par(7), par(17), par(18), par(19), par(20)
            g.wait_ge(act_trig, 4)
            G.put(g.memset(tab[:, :, 0, 0:1], 1.0))
            G.put(g.memset(tab[:, :, 1, 0:1], 0.0))
            G.put(g.tensor_copy(pr, cos))
            G.put(g.tensor_copy(pi, sin))
            G.wait()
            tmp = H[:, :].rearrange("p (i t) -> p i t", i=NSTATE_T)
            k = 1
            while k < T:
                def wide(x):
                    return x.unsqueeze(2).to_broadcast([P, NSTATE_T, k])
                c0, s0, cd, sd = tab[:, :, 0, 0:k], tab[:, :, 1, 0:k], tab[:, :, 0, k:2 * k], tab[:, :, 1, k:2 * k]
                G.put(g.tensor_tensor(cd, c0, wide(pr), ALU.mult))
                G.put(g.tensor_tensor(tmp[:, :, 0:k], s0, wide(pi), ALU.mult))
                G.wait()
                G.put(g.tensor_tensor(cd, cd, tmp[:, :, 0:k], ALU.subtract))
                G.put(g.tensor_tensor(sd, c0, wide(pi), ALU.mult))
                G.wait(1)
                G.put(g.tensor_tensor(tmp[:, :, 0:k], s0, wide(pr), ALU.mult))
                G.wait()
                ins = g.tensor_tensor(sd, sd, tmp[:, :, 0:k], ALU.add)
                if 2 * k == T:
                    ins.then_inc(tab_ready, 1)
                    break
                G.put(ins)
                G.put(g.tensor_tensor(npr, pr, pr, ALU.mult))
                G.put(g.tensor_tensor(q1, pi, pi, ALU.mult))
                G.put(g.tensor_tensor(pi, pr, pi, ALU.mult))
                G.wait()
                G.put(g.tensor_tensor(pr, npr, q1, ALU.subtract))
                G.put(g.tensor_tensor(pi, pi, pi, ALU.add))
                G.wait()
                k *= 2
            g.wait_ge(bias_sb, HEADS)
            g.dma_start(skew_d.rearrange("h p w -> p h w"), skew_sb.rearrange("p (h w) -> p h w", h=HEADS))\
             .then_inc(skew_out, 16)
            g.wait_ge(h_first, KT)
            g.dma_start(cmat, cmat_d).then_inc(cmat_in, 16)
            t3 = W[:, 1024:1536].rearrange("p (r t) -> p r t", r=2)
            t4 = W[:, 1536:2048].rearrange("p (r t) -> p r t", r=2)
            with G.loop(8, 12) as c:
                for j in range(4):
                    w = scanb[:, j % 2, :, :]
                    g.wait_ge(scan_out, c * 4 + (j + 1))
                    cosv = A[:, bass.ds(c * 2048 + j * 512, T)].unsqueeze(1).to_broadcast([P, 2, T])
                    sinv = A[:, bass.ds(c * 2048 + (j * 512 + T), T)].unsqueeze(1).to_broadcast([P, 2, T])
                    G.put(g.tensor_tensor(t3, w, cosv, ALU.mult))
                    G.put(g.tensor_tensor(t4, w, sinv, ALU.mult))
                    G.wait()
                    G.put(g.tensor_tensor(w[:, 0, :], t3[:, 0, :], t4[:, 1, :], ALU.subtract))
                    g.tensor_tensor(w[:, 1, :], t3[:, 1, :], t4[:, 0, :], ALU.add).then_inc(rotated, 1)
                    g.wait_ge(rotated, c * 4 + (j + 1))
            g.wait_ge(z_ready, 8)
            g.dma_start(X[:, :], xT_d.rearrange("p k t -> p (k t)")).then_inc(x_in, 16)
            g.wait_ge(att_sb, 16)
            g.dma_start(dyn[:, 0:256], dyn2_d).then_inc(dyn_in, 16)
            g.iota(iota[:, :], pattern=[[1, P]], base=0, channel_multiplier=0,
                   allow_small_or_imprecise_dtypes=True).then_inc(iota_ready, 1)
            g.wait_ge(iota_ready, 1)
            for half in range(2):
                with G.loop(16, 0) as i:
                    for b in range(2):
                        g.wait_ge(first1_ready, i * 2 + (32 * half + b + 1))
                        for r in range(2):
                            ins = g.tensor_tensor(hot1[b][:, :, r, :], first1[b],
                                                  g16[:, r, bass.ds(i * 16 + 8 * b, 8)].unsqueeze(2).to_broadcast([P, 8, 64]),
                                                  ALU.mult)
                        ins.then_inc(hot1_ready, 1)
            g.wait_ge(key_ps, 8)
            g.dma_start(dyn[:, 0:512], dyn3_d).then_inc(dyn_in, 16)
            g.wait_ge(bank_free, FIRST["z"] + 4 + 11)
            zb = [tiles(J, 18 + q) for q in range(4)]
            ping = [tiles(A, 60 + q) for q in range(4)]
            pong = [tiles(W, q) for q in range(4)]
            cur = zb
            for level in range(4):
                d = 1 << level
                nxt = ping if level % 2 == 0 else pong
                for q in range(level, 4):
                    G.put(g.tensor_copy(nxt[q][:, 0:d], cur[q][:, 0:d]))
                    G.put(g.tensor_tensor(nxt[q][:, d:T], cur[q][:, d:T], cur[q][:, 0:T - d], ALU.add))
                G.wait()
                q, w = level, 2 << level
                o = nxt[q]
                G.put(g.tensor_tensor(o[:, 0:w], o[:, 0:w], const("pool_rcnt", 16 * q, w), ALU.mult))
                G.put(g.tensor_scalar(o[:, w:T], o[:, w:T], 1.0 / w, None, ALU.mult))
                G.wait()
                ins = g.tensor_tensor(ping[q], o, zb[q], ALU.subtract)
                if level < 3:
                    G.put(ins)
                    G.wait()
                else:
                    ins.then_inc(pooled, 1)
                cur = nxt


def bass_skew(skew_d):
    return bass.AP(skew_d.tensor, 127, [[SKEW_W - 1, P], [P * SKEW_W, HEADS], [1, T]])


def bucket_onehot():
    def bucket(n):
        scaled = np.log(np.float32(max(n, 16)) / np.float32(16)).astype(np.float32) / np.float32(math.log(1024 / 16))
        large = 16 + int(np.float32(scaled) * np.float32(16))
        return n if n < 16 else min(large, 31)

    out = np.zeros((33, SKEW_W + ASC_W), np.float32)
    for c in range(SKEW_W):
        d = 255 - c
        out[32 if d < 0 else bucket(d), c] = 1
    for c in range(ASC_W):
        d = c - ASC_0
        out[32 if d < 0 else bucket(d), SKEW_W + c] = 1
    return out


def units_a(w):
    n = w.shape[1]
    return w.reshape(16, P, n // 256, 256).transpose(2, 1, 0, 3).reshape(n // 256, P, UNIT)


def units_b(w):
    n = w.shape[1]
    return w.reshape(2, 32, P, n // P, P).transpose(3, 0, 2, 1, 4).reshape(2 * (n // P), P, UNIT)


def cols(v):
    return np.ascontiguousarray(v.reshape(-1, P).T)


def layout(i):
    f = {k: np.asarray(v) for k, v in i.items()}
    w_in = f["w_in"][0]
    w_u = f["peer_u"][0].T
    w_v = f["peer_v"][0]
    z = f["w_in_2"][0]
    z = np.concatenate([z[:, 2048:4352], z[:, 1536:2048], z[:, 0:1536]], axis=1)
    abc = np.concatenate([f["w_a_out_2"][0], f["w_b_out_2"][0], f["w_c_out_2"][0]], axis=0)
    cmp_u = lambda w: w.reshape(2, 16, P, 256).transpose(0, 2, 1, 3).reshape(2, P, UNIT)
    glu = f["ssm_w_glu"][0].reshape(8, P, 2, 512).transpose(2, 1, 0, 3).reshape(2, P, UNIT)
    wst = np.concatenate([
        units_a(f["w_ada"][0]), units_a(w_in[:, 0:3584]), glu, cmp_u(f["cmp_w1_k"][0]), cmp_u(f["cmp_w1_v"][0]),
        units_a(f["w_out"][0]), units_a(f["peer_w_q"][0]),
        units_a(w_u[:, 0:8192]), units_b(w_v[0:8192]), units_a(w_u[:, 8192:]), units_b(w_v[8192:]),
        units_a(z), units_a(f["w_gate_2"][0]), units_a(abc), units_a(f["w_o_2"][0]),
        units_a(f["w_up_2"][0]), units_b(f["w_down_2"][0])], axis=0)
    rcnt = np.zeros((4, 16), np.float32)
    for g in range(4):
        rcnt[g] = 1 / np.minimum(np.arange(16) + 1, 2 << g).astype(np.float32)
    table = {
        "c": cols(f["c"][0]), "b_ada": cols(f["b_ada"][0]), "norm1_g": cols(f["norm1_g"][0]),
        "norm2_g": cols(f["norm2_g"][0]), "final_g": cols(f["final_g"]), "g_mix": cols(f["g_mix_2"][0]),
        "g_mlp": cols(f["g_mlp_2"][0]), "g_final": cols(f["g_final_2"]),
        "beta": np.concatenate([cols(f["beta_ssm"][0]), cols(f["beta_attn"][0])], axis=1),
        "lam_re": cols(f["ssm_lam_re"][0]), "lam_im": cols(f["ssm_lam_im"][0]),
        "log_dt": cols(np.repeat(f["ssm_log_dt"][0], 64)), "d_skip": cols(f["ssm_d"][0]),
        "b_glu": cols(f["ssm_b_glu"][0]), "b_gate": cols(f["b_gate_2"][0]), "b_glu2": cols(f["b_glu_2"][0]),
        "w_dw_a": f["w_dw_a_2"][0].reshape(31, 6, P).transpose(2, 1, 0).reshape(P, 186),
        "b_dw_a": cols(f["b_dw_a_2"][0]), "ln_g": cols(f["ln_g_a_2"][0]), "ln_b": cols(f["ln_b_a_2"][0]),
        "pool_scale": cols(f["pool_scale_2"][0]),
        "w_dw_c": f["w_dw_c_2"][0].reshape(3, 6, P).transpose(2, 1, 0).reshape(P, 18),
        "pool_rcnt": np.tile(rcnt.reshape(1, 64), (P, 1)),
    }
    cst = np.concatenate([table[n] for n, _ in CONST], axis=1)
    gcols = w_in[:, 3584:3608].reshape(D_MODEL, 3, HEADS)[:, [1, 2, 0], :].transpose(0, 2, 1).reshape(D_MODEL, 24)
    half = lambda w: w.reshape(2, P, P).transpose(1, 0, 2).reshape(P, 256)
    dyn1 = np.concatenate([gcols.reshape(KT, P, 24).transpose(1, 0, 2).reshape(P, 384),
                           half(f["cmp_w2_k"][0]), half(f["cmp_w2_v"][0]),
                           f["cmp_pe_k"][0].T, f["cmp_pe_v"][0].T], axis=1)
    dyn2 = np.concatenate([f["peer_k1"][0].T, f["peer_k2"][0].T], axis=1)
    dyn3 = f["w_pool_grp_2"][0].transpose(1, 0, 2).reshape(P, 512)
    rel = np.concatenate([f["rel_bias"], np.full((1, HEADS), NEG, np.float32)], axis=0)
    onehot = np.concatenate([bucket_onehot(), rel], axis=1)
    bm = np.zeros((2, 8, 4, 2, 16, 2, 64), np.float32)
    cm = np.zeros((2, 32, 2, 64, 2, 16), np.float32)
    for r, n in enumerate(("re", "im")):
        b = f["ssm_b_" + n][0].reshape(8, 4, 2, 64, 16).transpose(0, 1, 2, 4, 3)
        c = f["ssm_c_" + n][0].reshape(32, 2, 16, 64).transpose(0, 1, 3, 2)
        for g in range(2):
            bm[r, :, :, g, :, g, :] = b[:, :, g]
            cm[r, :, g, :, g, :] = c[:, g]
    bmat = bm.reshape(2, 8, P, P).transpose(2, 1, 0, 3)
    cmat = cm.reshape(2, 32, P, 32).transpose(2, 0, 1, 3)
    xT = f["x"][0].T.reshape(KT, P, T).transpose(1, 0, 2)
    arrays = {"xT": xT, "wst": wst, "cst": cst, "dyn1": dyn1, "dyn2": dyn2, "dyn3": dyn3, "onehot": onehot,
              "bmat": bmat, "cmat": cmat}
    return {k + "_dram": np.ascontiguousarray(v) for k, v in arrays.items()}


def kernel(**inputs):
    import concourse.bacc as bacc
    from concourse.bass_utils import run_bass_kernel_spmd

    arrays = layout(inputs)
    nc = bacc.Bacc("TRN2", target_bir_lowering=False, num_devices=1)
    aps = [nc.dram_tensor(k, a.shape, mybir.dt.from_np(a.dtype), kind="ExternalInput").ap() for k, a in arrays.items()]
    skew = nc.dram_tensor("bias_rows", (HEADS, P, SKEW_W), F32, kind="Internal").ap()
    out = nc.dram_tensor("out_dram", (P, KT, T), F32, kind="ExternalOutput").ap()
    program(nc, *aps, skew, out)
    r = run_bass_kernel_spmd(nc, [arrays], core_ids=[0])
    y = np.asarray(r.results[0]["out_dram"])
    return np.ascontiguousarray(y.transpose(1, 0, 2).reshape(D_MODEL, T).T)[None]
```
